# Optimizing a Trainium2 kernel written in Bass

```python
import jax, jax.numpy as jnp
from jax import lax
import numpy as np

D_MODEL = 2048
BATCH = 1
SEQ = 512
DEPTH = 2

GRID_W = 64
HEAD_DIM = 128
A_HEADS = 8
A_KV_HEADS = 2
B_HEADS = 4
B_Q_LORA = 512
B_KV_LORA = 256
B_NOPE = 128
B_ROPE = 64
B_V = 128
C_HEADS = 4
WIN_ROWS = 8
WIN_COLS = 16
D_MIX = A_HEADS * HEAD_DIM + B_HEADS * B_V + C_HEADS * HEAD_DIM
Q_BLOCK = 128
ROPE_THETA = 10000.0
NORM_EPS = 1e-6
IN_SPLITS = (
    A_HEADS * HEAD_DIM,
    A_KV_HEADS * HEAD_DIM,
    A_KV_HEADS * HEAD_DIM,
    A_HEADS * HEAD_DIM,
    B_Q_LORA,
    B_KV_LORA,
    B_ROPE,
    B_HEADS * B_V,
    C_HEADS * HEAD_DIM,
    C_HEADS * HEAD_DIM,
    C_HEADS * HEAD_DIM,
    C_HEADS * HEAD_DIM,
)
D_IN = sum(IN_SPLITS)


def _rms_norm(x, g):
    xf = x.astype(jnp.float32)
    y = xf * lax.rsqrt(jnp.mean(xf * xf, axis=-1, keepdims=True) + NORM_EPS)
    return (y * g.astype(jnp.float32)).astype(x.dtype)

def _rope_half(x, pos):
    n = x.shape[-1]
    inv_freq = 1.0 / (ROPE_THETA ** (jnp.arange(0, n, 2, dtype=jnp.float32) / n))
    ang = pos.astype(jnp.float32)[:, None] * inv_freq[None, :]
    cos = jnp.cos(ang)[:, None, :]
    sin = jnp.sin(ang)[:, None, :]
    xf = x.astype(jnp.float32)
    x1, x2 = xf[..., : n // 2], xf[..., n // 2:]
    out = jnp.concatenate([x1 * cos - x2 * sin, x2 * cos + x1 * sin], axis=-1)
    return out.astype(x.dtype)

def _rope_axial(x, row, col):
    h = x.shape[-1] // 2
    return jnp.concatenate([_rope_half(x[..., :h], row), _rope_half(x[..., h:], col)], axis=-1)

def _dense_block_attention(q, k, v):
    B, S, H, dq = q.shape
    Hk = k.shape[2]
    G = H // Hk
    dv = v.shape[-1]
    nb = S // Q_BLOCK
    scale = dq ** -0.5
    qb = q.reshape(B, nb, Q_BLOCK, Hk, G, dq).transpose(1, 0, 2, 3, 4, 5)

    def one(qblk):
        s = jnp.einsum('bqkgd,bskd->bkgqs', qblk, k).astype(jnp.float32) * scale
        p = jax.nn.softmax(s, axis=-1).astype(v.dtype)
        return jnp.einsum('bkgqs,bskd->bqkgd', p, v)

    o = lax.map(one, qb)
    return o.transpose(1, 0, 2, 3, 4, 5).reshape(B, S, H, dv)

def _neighbourhood_attention(q, k, v, rpb):
    B, S, H, d = q.shape
    rows = S // GRID_W
    kr = min(WIN_ROWS, rows)
    nk = kr * WIN_COLS
    t = jnp.arange(S)
    r = t // GRID_W
    c = t % GRID_W
    r0 = jnp.clip(r - kr // 2, 0, rows - kr)
    c0 = jnp.clip(c - WIN_COLS // 2, 0, GRID_W - WIN_COLS)
    key_r = r0[:, None, None] + jnp.arange(kr)[None, :, None]
    key_c = c0[:, None, None] + jnp.arange(WIN_COLS)[None, None, :]
    idx = (key_r * GRID_W + key_c).reshape(S, nk)
    dr = key_r - r[:, None, None] + (WIN_ROWS - 1)
    dc = key_c - c[:, None, None] + (WIN_COLS - 1)
    bias = rpb[:, dr, dc].reshape(H, S, nk)
    nb = S // Q_BLOCK
    scale = d ** -0.5
    qb = q.reshape(B, nb, Q_BLOCK, H, d).transpose(1, 0, 2, 3, 4)
    idxb = idx.reshape(nb, Q_BLOCK, nk)
    biasb = bias.reshape(H, nb, Q_BLOCK, nk).transpose(1, 0, 2, 3)

    def one(args):
        qblk, iblk, bblk = args
        kg = jnp.take(k, iblk, axis=1)
        vg = jnp.take(v, iblk, axis=1)
        s = jnp.einsum('bqhd,bqnhd->bhqn', qblk, kg).astype(jnp.float32) * scale
        s = s + bblk[None].astype(jnp.float32)
        p = jax.nn.softmax(s, axis=-1).astype(v.dtype)
        return jnp.einsum('bhqn,bqnhd->bqhd', p, vg)

    o = lax.map(one, (qb, idxb, biasb))
    return o.transpose(1, 0, 2, 3, 4).reshape(B, S, H, d)

def _layer(x, g_pre, g_post, w_in, a_qn, a_kn, b_qn, b_kvn, w_uq, w_ukv, rpb, w_out, row, col):
    B, S, _ = x.shape
    h = _rms_norm(x, g_pre)
    proj = jnp.einsum('bsd,de->bse', h, w_in)
    split_points = [int(p) for p in np.cumsum(IN_SPLITS)[:-1]]
    (a_q, a_k, a_v, a_g, b_cq, b_ckv, b_kr, b_g,
     c_q, c_k, c_v, c_g) = jnp.split(proj, split_points, axis=-1)

    qa = _rms_norm(a_q.reshape(B, S, A_HEADS, HEAD_DIM), a_qn)
    ka = _rms_norm(a_k.reshape(B, S, A_KV_HEADS, HEAD_DIM), a_kn)
    va = a_v.reshape(B, S, A_KV_HEADS, HEAD_DIM)
    qa = _rope_axial(qa, row, col)
    ka = _rope_axial(ka, row, col)
    o_a = _dense_block_attention(qa, ka, va).reshape(B, S, A_HEADS * HEAD_DIM) * jax.nn.silu(a_g)

    cq = _rms_norm(b_cq, b_qn)
    qb = jnp.einsum('bsr,re->bse', cq, w_uq).reshape(B, S, B_HEADS, B_NOPE + B_ROPE)
    q_nope, q_pe = qb[..., :B_NOPE], qb[..., B_NOPE:]
    q_pe = _rope_axial(q_pe, row, col)
    ckv = _rms_norm(b_ckv, b_kvn)
    kv = jnp.einsum('bsr,re->bse', ckv, w_ukv).reshape(B, S, B_HEADS, B_NOPE + B_V)
    k_nope, vb = kv[..., :B_NOPE], kv[..., B_NOPE:]
    k_pe = _rope_axial(b_kr.reshape(B, S, 1, B_ROPE), row, col)
    k_pe = jnp.broadcast_to(k_pe, (B, S, B_HEADS, B_ROPE))
    q_full = jnp.concatenate([q_nope, q_pe], axis=-1)
    k_full = jnp.concatenate([k_nope, k_pe], axis=-1)
    o_b = _dense_block_attention(q_full, k_full, vb).reshape(B, S, B_HEADS * B_V) * jax.nn.silu(b_g)

    qc = c_q.reshape(B, S, C_HEADS, HEAD_DIM)
    kc = c_k.reshape(B, S, C_HEADS, HEAD_DIM)
    vc = c_v.reshape(B, S, C_HEADS, HEAD_DIM)
    o_c = _neighbourhood_attention(qc, kc, vc, rpb).reshape(B, S, C_HEADS * HEAD_DIM) * jax.nn.silu(c_g)

    y = jnp.einsum('bse,ed->bsd', jnp.concatenate([o_a, o_b, o_c], axis=-1), w_out)
    return x + _rms_norm(y, g_post)

def first_inputs(seed: int = 0) -> dict:
    key = jax.random.key(seed)
    ks = jax.random.split(key, 13)
    f32 = jnp.float32

    def gain(k, n):
        return 1.0 + 0.05 * jax.random.normal(k, (DEPTH, n), f32)

    x = jax.random.normal(ks[0], (BATCH, SEQ, D_MODEL), f32)
    norm_pre = gain(ks[1], D_MODEL)
    norm_post = gain(ks[2], D_MODEL)
    w_in = jax.random.normal(ks[3], (DEPTH, D_MODEL, D_IN), f32) * D_MODEL ** -0.5
    a_q_norm = gain(ks[4], HEAD_DIM)
    a_k_norm = gain(ks[5], HEAD_DIM)
    b_q_norm = gain(ks[6], B_Q_LORA)
    b_kv_norm = gain(ks[7], B_KV_LORA)
    b_w_uq = jax.random.normal(ks[8], (DEPTH, B_Q_LORA, B_HEADS * (B_NOPE + B_ROPE)), f32) * B_Q_LORA ** -0.5
    b_w_ukv = jax.random.normal(ks[9], (DEPTH, B_KV_LORA, B_HEADS * (B_NOPE + B_V)), f32) * B_KV_LORA ** -0.5
    c_rpb = 0.1 * jax.random.normal(ks[10], (DEPTH, C_HEADS, 2 * WIN_ROWS - 1, 2 * WIN_COLS - 1), f32)
    w_out = jax.random.normal(ks[11], (DEPTH, D_MIX, D_MODEL), f32) * D_MIX ** -0.5
    return {"x": x, "norm_pre": norm_pre, "norm_post": norm_post, "w_in": w_in,
            "a_q_norm": a_q_norm, "a_k_norm": a_k_norm, "b_q_norm": b_q_norm,
            "b_kv_norm": b_kv_norm, "b_w_uq": b_w_uq, "b_w_ukv": b_w_ukv,
            "c_rpb": c_rpb, "w_out": w_out}

def first_block(x, norm_pre, norm_post, w_in, a_q_norm, a_k_norm, b_q_norm, b_kv_norm,
              b_w_uq, b_w_ukv, c_rpb, w_out):
    S = x.shape[1]
    t = jnp.arange(S)
    row = t // GRID_W
    col = t % GRID_W
    h = x
    for l in range(DEPTH):
        h = _layer(h, norm_pre[l], norm_post[l], w_in[l], a_q_norm[l], a_k_norm[l],
                   b_q_norm[l], b_kv_norm[l], b_w_uq[l], b_w_ukv[l], c_rpb[l], w_out[l],
                   row, col)
    return h


D_MIX_2 = D_MODEL
EPS = 1e-6
SWA_HEAD_DIM = 64
SWA_HEADS = D_MIX_2 // 2 // SWA_HEAD_DIM
SWA_KV_HEADS = 4
SWA_GROUP = SWA_HEADS // SWA_KV_HEADS
SWA_WIDTH = SWA_HEADS * SWA_HEAD_DIM
SWA_KV_WIDTH = SWA_KV_HEADS * SWA_HEAD_DIM
WINDOW = 128
ROT_DIM = SWA_HEAD_DIM // 4
ROPE_THETA_2 = 500000.0
SG_WIDTH = D_MIX_2 // 4
SG_GROUPS = 8
SG_GROUP_DIM = SG_WIDTH // SG_GROUPS
SG_CHUNK = 128
GLA_HEADS = 4
GLA_WIDTH = D_MIX_2 // 4
GLA_DV = GLA_WIDTH // GLA_HEADS
GLA_DK = GLA_DV // 2
GLA_KEY_WIDTH = GLA_HEADS * GLA_DK
GLA_GATE_RANK = 16
GLA_GATE_TAU = 16.0
GLA_CHUNK = 64
IN_SIZES = (SWA_WIDTH, SWA_KV_WIDTH, SWA_KV_WIDTH,
            SG_WIDTH, SG_WIDTH,
            GLA_KEY_WIDTH, GLA_KEY_WIDTH, GLA_WIDTH,
            GLA_GATE_RANK,
            D_MIX_2)
IN_PROJ_WIDTH = SWA_WIDTH + 2 * SWA_KV_WIDTH + 2 * SG_WIDTH + 2 * GLA_KEY_WIDTH + GLA_WIDTH + GLA_GATE_RANK + D_MIX_2


def rms_norm(x, g):
    x32 = x.astype(jnp.float32)
    y = x32 * lax.rsqrt(jnp.mean(x32 * x32, axis=-1, keepdims=True) + EPS)
    return (y * g.astype(jnp.float32)).astype(x.dtype)

def partial_rope(t, positions):
    half = ROT_DIM // 2
    inv_freq = ROPE_THETA_2 ** (-(jnp.arange(half, dtype=jnp.float32) * (2.0 / ROT_DIM)))
    ang = positions.astype(jnp.float32)[..., None] * inv_freq
    cos = jnp.cos(ang)[:, :, None, :]
    sin = jnp.sin(ang)[:, :, None, :]
    tr = t[..., :ROT_DIM].astype(jnp.float32)
    t1, t2 = tr[..., :half], tr[..., half:]
    rot = jnp.concatenate([t1 * cos - t2 * sin, t2 * cos + t1 * sin], axis=-1)
    return jnp.concatenate([rot.astype(t.dtype), t[..., ROT_DIM:]], axis=-1)

def sliding_window_attention(q, k, v, sinks):
    bsz, seq = q.shape[0], q.shape[1]
    nb = seq // WINDOW
    qb = q.reshape(bsz, nb, WINDOW, SWA_KV_HEADS, SWA_GROUP, SWA_HEAD_DIM).astype(jnp.float32)

    def band(t):
        tb = t.reshape(bsz, nb, WINDOW, SWA_KV_HEADS, SWA_HEAD_DIM)
        prev = jnp.pad(tb[:, :-1], ((0, 0), (1, 0), (0, 0), (0, 0), (0, 0)))
        return jnp.concatenate([prev, tb], axis=2).astype(jnp.float32)

    kb, vb = band(k), band(v)
    scores = jnp.einsum('bnqgrd,bnkgd->bngrqk', qb, kb) * (SWA_HEAD_DIM ** -0.5)
    qi = jnp.arange(WINDOW)[:, None]
    kj = jnp.arange(2 * WINDOW)[None, :]
    dist = qi + WINDOW - kj
    blk = jnp.arange(nb)[:, None, None]
    valid = (dist >= 0) & (dist < WINDOW) & (blk * WINDOW + kj[None] - WINDOW >= 0)
    scores = jnp.where(valid[None, :, None, None], scores, -jnp.inf)
    sink = sinks.astype(jnp.float32).reshape(1, 1, SWA_KV_HEADS, SWA_GROUP, 1, 1)
    m = jnp.maximum(scores.max(axis=-1, keepdims=True), sink)
    p = jnp.exp(scores - m)
    probs = p / (p.sum(axis=-1, keepdims=True) + jnp.exp(sink - m))
    out = jnp.einsum('bngrqk,bnkgd->bnqgrd', probs, vb)
    return out.reshape(bsz, seq, SWA_WIDTH).astype(q.dtype)

def chunked_spatial_gating(u, v, w_s, b_s, ln_g, ln_b):
    bsz, seq = v.shape[0], v.shape[1]
    nc = seq // SG_CHUNK
    v32 = v.astype(jnp.float32)
    mu = jnp.mean(v32, axis=-1, keepdims=True)
    var = jnp.mean(jnp.square(v32 - mu), axis=-1, keepdims=True)
    vn = (v32 - mu) * lax.rsqrt(var + EPS) * ln_g.astype(jnp.float32) + ln_b.astype(jnp.float32)
    vn = vn.reshape(bsz, nc, SG_CHUNK, SG_GROUPS, SG_GROUP_DIM)
    causal = jnp.tril(jnp.ones((SG_CHUNK, SG_CHUNK), dtype=bool))
    w = jnp.where(causal[None], w_s.astype(jnp.float32), 0.0)
    mixed = jnp.einsum('gts,bnsgc->bntgc', w, vn) + b_s.astype(jnp.float32).T[None, None, :, :, None]
    return (u.astype(jnp.float32) * mixed.reshape(bsz, seq, SG_WIDTH)).astype(u.dtype)

def gated_linear_attention(q, k, v, log_alpha):
    bsz, seq = q.shape[0], q.shape[1]
    nc = seq // GLA_CHUNK

    def to_chunks(t):
        return t.astype(jnp.float32).reshape(bsz, nc, GLA_CHUNK, GLA_HEADS, t.shape[-1]).transpose(1, 0, 3, 2, 4)

    causal = jnp.tril(jnp.ones((GLA_CHUNK, GLA_CHUNK), dtype=bool))

    def step(state, xs):
        qc, kc, vc, lac = xs
        b = jnp.cumsum(lac, axis=2)
        diff = b[:, :, :, None, :] - b[:, :, None, :, :]
        decay = jnp.exp(jnp.where(causal[:, :, None], diff, -jnp.inf))
        scores = jnp.einsum('bhtd,bhsd,bhtsd->bhts', qc, kc, decay)
        o = jnp.einsum('bhts,bhsv->bhtv', scores, vc) + jnp.einsum('bhtd,bhdv->bhtv', qc * jnp.exp(b), state)
        b_last = b[:, :, -1:, :]
        state = state * jnp.exp(b_last)[:, :, 0, :, None] + jnp.einsum('bhsd,bhsv->bhdv', kc * jnp.exp(b_last - b), vc)
        return state, o

    state0 = jnp.zeros((bsz, GLA_HEADS, GLA_DK, GLA_DV), dtype=jnp.float32)
    qs = to_chunks(q) * (GLA_DK ** -0.5)
    _, o = lax.scan(step, state0, (qs, to_chunks(k), to_chunks(v), to_chunks(log_alpha)))
    return o.transpose(1, 0, 3, 2, 4).reshape(bsz, seq, GLA_HEADS, GLA_DV)

def hybrid_layer(x, c, positions, w_mod, b_mod, g_pre, g_post, w_in, w_out, swa_sinks,
                 sg_w, sg_b, sg_ln_g, sg_ln_b, gla_w_gate_up, gla_b_gate, gla_norm_g):
    bsz, seq = x.shape[0], x.shape[1]
    mod = jax.nn.silu(c) @ w_mod + b_mod
    shift, scale, gate = jnp.split(mod, 3, axis=-1)
    h = rms_norm(x, g_pre) * (1.0 + scale[:, None, :]) + shift[:, None, :]
    proj = h @ w_in
    offsets = np.cumsum(IN_SIZES)[:-1].tolist()
    a_q, a_k, a_v, s_u, s_v, c_q, c_k, c_v, c_g, z = jnp.split(proj, offsets, axis=-1)
    a_q = partial_rope(a_q.reshape(bsz, seq, SWA_HEADS, SWA_HEAD_DIM), positions)
    a_k = partial_rope(a_k.reshape(bsz, seq, SWA_KV_HEADS, SWA_HEAD_DIM), positions)
    a_v = a_v.reshape(bsz, seq, SWA_KV_HEADS, SWA_HEAD_DIM)
    y_a = sliding_window_attention(a_q, a_k, a_v, swa_sinks)
    y_b = chunked_spatial_gating(jax.nn.gelu(s_u), jax.nn.gelu(s_v), sg_w, sg_b, sg_ln_g, sg_ln_b)
    gate_logits = (c_g @ gla_w_gate_up + gla_b_gate).astype(jnp.float32)
    log_alpha = jax.nn.log_sigmoid(gate_logits) / GLA_GATE_TAU
    o_c = gated_linear_attention(c_q.reshape(bsz, seq, GLA_HEADS, GLA_DK),
                                 c_k.reshape(bsz, seq, GLA_HEADS, GLA_DK),
                                 c_v.reshape(bsz, seq, GLA_HEADS, GLA_DV),
                                 log_alpha.reshape(bsz, seq, GLA_HEADS, GLA_DK))
    y_c = rms_norm(o_c, gla_norm_g).reshape(bsz, seq, GLA_WIDTH).astype(x.dtype)
    y = jnp.concatenate([y_a, y_b, y_c], axis=-1) * jax.nn.silu(z)
    out = y @ w_out
    return x + gate[:, None, :] * rms_norm(out, g_post)

def second_inputs(seed: int = 0) -> dict:
    key = jax.random.key(seed)
    ks = jax.random.split(key, 17)
    nrm = jax.random.normal
    f32 = jnp.float32
    x = nrm(ks[0], (BATCH, SEQ, D_MODEL), f32)
    c = nrm(ks[1], (BATCH, D_MODEL), f32)
    positions = jax.random.randint(ks[2], (BATCH, 1), 0, 4096, dtype=jnp.int32) + jnp.arange(SEQ, dtype=jnp.int32)[None, :]
    w_mod = nrm(ks[3], (DEPTH, D_MODEL, 3 * D_MODEL), f32) * (0.5 * D_MODEL ** -0.5)
    b_mod = 0.01 * nrm(ks[4], (DEPTH, 3 * D_MODEL), f32)
    g_pre = 1.0 + 0.05 * nrm(ks[5], (DEPTH, D_MODEL), f32)
    g_post = 1.0 + 0.05 * nrm(ks[6], (DEPTH, D_MODEL), f32)
    w_in = nrm(ks[7], (DEPTH, D_MODEL, IN_PROJ_WIDTH), f32) * (D_MODEL ** -0.5)
    w_out = nrm(ks[8], (DEPTH, D_MIX_2, D_MODEL), f32) * (D_MIX_2 ** -0.5)
    swa_sinks = 0.5 * nrm(ks[9], (DEPTH, SWA_HEADS), f32)
    sg_w = nrm(ks[10], (DEPTH, SG_GROUPS, SG_CHUNK, SG_CHUNK), f32) * (SG_CHUNK ** -0.5)
    sg_b = 1.0 + 0.1 * nrm(ks[11], (DEPTH, SG_GROUPS, SG_CHUNK), f32)
    sg_ln_g = 1.0 + 0.05 * nrm(ks[12], (DEPTH, SG_WIDTH), f32)
    sg_ln_b = 0.02 * nrm(ks[13], (DEPTH, SG_WIDTH), f32)
    gla_w_gate_up = nrm(ks[14], (DEPTH, GLA_GATE_RANK, GLA_KEY_WIDTH), f32) * (GLA_GATE_RANK ** -0.5)
    gla_b_gate = 0.1 * nrm(ks[15], (DEPTH, GLA_KEY_WIDTH), f32)
    gla_norm_g = 1.0 + 0.05 * nrm(ks[16], (DEPTH, GLA_DV), f32)
    return {'x': x, 'c': c, 'positions': positions, 'w_mod': w_mod, 'b_mod': b_mod,
            'g_pre': g_pre, 'g_post': g_post, 'w_in': w_in, 'w_out': w_out, 'swa_sinks': swa_sinks,
            'sg_w': sg_w, 'sg_b': sg_b, 'sg_ln_g': sg_ln_g, 'sg_ln_b': sg_ln_b,
            'gla_w_gate_up': gla_w_gate_up, 'gla_b_gate': gla_b_gate, 'gla_norm_g': gla_norm_g}

def second_block(x, c, positions, w_mod, b_mod, g_pre, g_post, w_in, w_out, swa_sinks,
              sg_w, sg_b, sg_ln_g, sg_ln_b, gla_w_gate_up, gla_b_gate, gla_norm_g):
    for l in range(DEPTH):
        x = hybrid_layer(x, c, positions, w_mod[l], b_mod[l], g_pre[l], g_post[l], w_in[l], w_out[l],
                         swa_sinks[l], sg_w[l], sg_b[l], sg_ln_g[l], sg_ln_b[l],
                         gla_w_gate_up[l], gla_b_gate[l], gla_norm_g[l])
    return x


def setup_inputs(seed=0):
    out = dict(first_inputs(seed))
    for name, value in second_inputs(seed + 1).items():
        if name != "x":
            out[name + "_2"] = value
    return out


def reference(
    x, norm_pre, norm_post, w_in, a_q_norm, a_k_norm, b_q_norm, b_kv_norm, b_w_uq, b_w_ukv,
    c_rpb, w_out, c_2, positions_2, w_mod_2, b_mod_2, g_pre_2, g_post_2, w_in_2, w_out_2,
    swa_sinks_2, sg_w_2, sg_b_2, sg_ln_g_2, sg_ln_b_2, gla_w_gate_up_2, gla_b_gate_2,
    gla_norm_g_2,
):
    x = first_block(
        x, norm_pre, norm_post, w_in, a_q_norm, a_k_norm, b_q_norm, b_kv_norm, b_w_uq, b_w_ukv,
        c_rpb, w_out,
    )
    return second_block(
        x, c_2, positions_2, w_mod_2, b_mod_2, g_pre_2, g_post_2, w_in_2, w_out_2, swa_sinks_2,
        sg_w_2, sg_b_2, sg_ln_g_2, sg_ln_b_2, gla_w_gate_up_2, gla_b_gate_2, gla_norm_g_2,
    )


_drawn_inputs = setup_inputs


def setup_inputs(seed=0):
    import zlib

    import numpy as np

    out = dict(_drawn_inputs(seed))
    spreads = {}
    factors = {'b_mod_2': 4.894,
     'g_post_2': 4.7,
     'swa_sinks_2': 37.338,
     'sg_b_2': 4.845,
     'sg_ln_g_2': 8.0,
     'sg_ln_b_2': 47.18,
     'gla_b_gate_2': 6.691,
     'gla_norm_g_2': 5.774}
    for name, (base, spread) in spreads.items():
        noise = np.random.default_rng([zlib.crc32(name.encode()), seed]).standard_normal(out[name].shape)
        drawn = base * np.exp(spread * noise) if base else spread * noise
        out[name] = __import__('jax').numpy.asarray(drawn.astype(out[name].dtype))
    for name, factor in factors.items():
        out[name] = (out[name] * factor).astype(out[name].dtype)
    return out
```

```python
from contextlib import ExitStack

import numpy as np

import concourse.bass as bass
from concourse import mybir

F32 = mybir.dt.float32
F32R = mybir.dt.float32r
I32 = mybir.dt.int32
ALU = mybir.AluOpType
ACT = mybir.ActivationFunctionType
AX = mybir.AxisListType

P = 128
SEQ = 512
TT = SEQ // P
DM = 2048
KC = DM // P
PW = 512
ND = KC // 2
RS, RH = 2, 4
NIN, NOUT = 12, DM // PW
NP = NIN + NOUT
EPS = 1e-6
HD = 128
A_H, A_KV, B_H, C_H = 8, 2, 4, 4
B_Q, B_KV, B_NOPE, B_ROPE, B_V = 512, 256, 128, 64, 128
GRID_W = 64
DIN1 = 5952
A_Q0, B_CQ0, B_CKV0, B_G0, C_Q0 = 0, 2560, 3072, 3392, 3904
B_CKV_W = B_KV + B_ROPE
LEAD = 2
DVE_LINKS1, DVE_LINKS2 = 256, 383
SC_A, SC_B, SC_C = HD ** -0.5, (B_NOPE + B_ROPE) ** -0.5, HD ** -0.5
Y_B, Y_C = 1024, 1536
UNITS = 64
RPB_R, RPB_C = 15, 31
RPB_P = 2 * GRID_W - 1
GM = 14
MASKED = -1e30
S_H, S_KV, S_D, ROT = 16, 4, 64, 16
S_SC = S_D ** -0.5
SG_G, SG_C = 8, 64
G_H, G_DK, G_DV, G_RANK, CHUNK = 4, 64, 128, 16, 64
LEVELS = 6
CUM, TAIL = LEVELS, LEVELS + 1
SU0, CG0, Z0 = 1536, 3584, 3600
GELU_A, GELU_B = 0.044715, 0.7978845608028654


class Count:

    def __init__(self, sem, per, credit=0):
        self.sem, self.per, self.credit = sem, per, credit
        self.made = 0

    def at(self, blk, l, n):
        return l * self.per[blk] + (self.credit + n + (2 * self.per[0] if blk else 0))

    def next(self):
        self.made += 1
        return self.sem

    def now(self, blk, l):
        return self.at(blk, l, self.made)


def tables():
    t = np.arange(SEQ)
    row, col = t // GRID_W, t % GRID_W

    def axial(width):
        n = width // 2
        inv = (np.float32(1.0) / (np.float32(10000.0) ** (np.arange(0, n, 2, dtype=np.float32) / np.float32(n)))).astype(np.float32)
        cs, sn = [], []
        for pos in (row, col):
            ang = (pos.astype(np.float32)[:, None] * inv[None, :]).astype(np.float32)
            c, s = np.cos(ang).astype(np.float32), np.sin(ang).astype(np.float32)
            cs += [c, c]
            sn += [-s, s]
        out = np.stack([np.concatenate(cs, 1), np.concatenate(sn, 1)])
        return np.ascontiguousarray(out.reshape(2, TT, P, width).transpose(2, 0, 1, 3))

    c = np.arange(GRID_W)
    c0 = np.clip(c - 8, 0, GRID_W - 16)
    kc = np.arange(GRID_W)
    near = (kc[None] >= c0[:, None]) & (kc[None] < c0[:, None] + 16)
    mask = np.where(near, 0.0, MASKED).astype(np.float32)
    return axial(HD), axial(B_ROPE), np.concatenate([mask, mask], 0)


def tables_2():
    i = np.arange(P)
    j = np.arange(2 * P)
    dist = i[:, None] + P - j[None]
    band = np.where((dist >= 0) & (dist < P), 0.0, MASKED).astype(np.float32)
    inv = (np.float32(500000.0) ** (-(np.arange(ROT // 2, dtype=np.float32) * np.float32(2.0 / ROT)))).astype(np.float32)
    u, t = i[:, None], i[None, :]
    same = u // CHUNK == t // CHUNK
    sums = np.zeros((P, LEVELS + 2, P), np.float32)
    masks = np.zeros((P, LEVELS + 2, P), np.float32)
    for n in range(LEVELS):
        half = CHUNK >> (n + 1)
        m = t // (2 * half) * (2 * half) + half - 1
        sums[:, n, :] = ((u > m) & (u <= t)) | ((u > t) & (u <= m))
        masks[:, n, :] = (u // (2 * half) == t // (2 * half)) & (u // half % 2 == 0) & (t // half % 2 == 1)
    sums[:, CUM, :] = same & (u <= t)
    sums[:, TAIL, :] = same & (u > t)
    masks[:, LEVELS, :] = u == t
    masks[:, LEVELS + 1, :] = u <= t
    sums /= 16.0
    return band, inv, sums, masks


def build(nc, io, only_first=False):
    with ExitStack() as ctx:
        base = -(-nc.sbuf_base // 64) * 64
        arena_bytes = 212800 // 64 * 64 - 64
        assert base + arena_bytes <= nc.sbuf_usable_end
        place = [base]
        sb_at = {}

        def sb(name, shape, dt=F32, at=None):
            size = int(np.prod(shape[1:])) * 4
            offset = place[0] if at is None else at
            t = nc.alloc_sbuf_tensor_at(name, shape, dt, offset=offset, align_bytes=4)
            if at is None:
                sb_at[name] = offset
                place[0] += size
                assert place[0] <= base + arena_bytes, (name, place[0] - base)
            return t

        ht_at = place[0]
        act_hi = sb("act_hi", [P, KC, SEQ], F32R)
        act_lo = sb("act_lo", [P, KC, SEQ], F32R)
        late = sb("late", [P, 2 * KC * SEQ], at=ht_at)
        Y = sb("Y", [P, TT, DM])
        stage = sb("stage", [P, RS, 2, PW])
        whi = sb("whi", [P, RH, 2, PW], F32R)
        wlo = sb("wlo", [P, RH, 2, PW], F32R)
        zone_at = place[0]
        zone = sb("zone", [P, 14336])
        wmod = sb("wmod", [P, 2, PW])
        mprod = sb("mprod", [P, PW])
        macc = sb("macc", [P, PW])
        mrow = sb("mrow", [1, PW])
        ident = sb("ident", [P, P])
        gmask = sb("gmask", [P, GRID_W])
        rows = sb("rows", [P, P])
        cols = sb("cols", [P, 96])
        csil = sb("csil", [P, KC])
        ctmp = sb("ctmp", [P, KC])
        ones = sb("ones", [P, 2])
        ss = sb("ss", [P, 64])
        rs = sb("rs", [P, 64])
        nv = sb("nv", [P, 3, 64])
        rsq = sb("rsq", [P, TT, A_H])
        nmx = sb("nmx", [P, 4, 2])
        sm = sb("sm", [P, 4])
        ri = sb("ri", [P, 4, 2])

        wmod_at = sb_at["wmod"]
        band = sb("band", [P, 2 * P], at=wmod_at)
        sinks = sb("sinks", [P, S_H], at=wmod_at + 1024)
        rot = sb("rot", [P, 2, TT, ROT // 2], at=wmod_at + 1088)
        rtmp = sb("rtmp", [P, 6, TT, ROT // 2], at=wmod_at + 1344)
        pos_i = sb("pos_i", [P, TT], I32, at=wmod_at + 2112)
        pos_f = sb("pos_f", [P, TT], at=wmod_at + 2128)
        freq = sb("freq", [P, ROT // 2], at=wmod_at + 2144)
        bias_c = sb("bias_c", [P, SG_G], at=wmod_at + 2176)
        bnst = sb("bnst", [P, TT, 6], at=wmod_at + 2208)
        mv = sb("mv", [P, TT, 2], at=wmod_at + 2304)
        decay = sb("decay", [P, 2, 8], at=wmod_at + 2336)
        es = sb("es", [P, 4], at=wmod_at + 2400)
        den = sb("den", [P, 4], at=wmod_at + 2416)

        PP, ZQ, ZT, ZK, ZV = 0, 4096, 8192, 10240, 12288

        def view(first, *shape, of=zone):
            size = int(np.prod(shape))
            names = "abcd"[:len(shape)]
            v = of[:, first:first + size]
            if len(shape) == 1:
                return v
            return v.rearrange(f"p ({' '.join(names)}) -> p {' '.join(names)}",
                               **{n: s for n, s in zip(names, shape)})

        xs = view(0, TT, DM)
        probs = view(PP, 4, SEQ)
        probsT = view(PP + 2048, 4, SEQ)
        tanh_tmp = view(ZT, 2, PW)

        bank = [ctx.enter_context(nc.psum_tensor(f"bank{i}", [P, 512], F32)) for i in range(8)]
        LIN, JOB, OUTB, SCORE, TURN = bank[0:4], bank[0:2], bank[2:4], bank[4:6], bank[6:8]
        PAST = [bank[0:2], bank[6:8]]
        XP = bank[4:8]
        MSUM = bank[7]

        rpb_dram = nc.dram_tensor("rpb_pad", (2 * C_H * RPB_R, RPB_P), F32, kind="Internal").ap()
        g_dram = nc.dram_tensor("rpb_tiles", (2, P, C_H, GM, GRID_W), F32, kind="Internal").ap()
        mod_dram = nc.dram_tensor("mod_rows", (2, 3 * DM), F32, kind="Internal").ap()
        x_dram = io["out"].rearrange("o (t p) d -> p (o t) d", p=P)
        x_in = io["x"].rearrange("o (t p) d -> p (o t) d", p=P)

        def sem(name):
            return ctx.enter_context(nc.semaphore(name))

        def count(name, per1, per2=None, credit=0):
            return Count(sem(name), (per1, per1 if per2 is None else per2), credit)

        boot_dma = sem("boot_dma")
        boot_rpb = sem("boot_rpb")
        boot_x = sem("boot_x")
        boot_pool = sem("boot_pool")
        boot_pe = sem("boot_pe")
        boot_dve = sem("boot_dve")
        boot_act = sem("boot_act")
        boot_g = sem("boot_g")
        w_landed = [count(f"w_landed{s}", 16 * NP * ND // RS) for s in range(RS)]
        hi_done = count("hi_done", NP * ND)
        lo_done = count("lo_done", NP * ND, credit=RS)
        w_used = count("w_used", NP * (ND - 1), credit=RH - 1)
        lin_done = count("lin_done", NP * TT, credit=1)
        lin_free = [count(f"lin_free{t}", NP, credit=1) for t in range(TT)]
        xp_done = count("xp_done", 2 * KC)
        xp_hi = count("xp_hi", 2 * KC)
        xp_free = count("xp_free", 2 * KC, credit=4)
        J1, J2 = 46, 39
        job_done = count("job_done", J1, J2)
        job_ev = count("job_ev", J1, J2, credit=2)
        score_done = count("score_done", UNITS)
        max_done = count("max_done", UNITS)
        exp_done = count("exp_done", UNITS, credit=2)
        turn_done = count("turn_done", UNITS, credit=4)
        pt_done = count("pt_done", UNITS, credit=2)
        pv_done = count("pv_done", UNITS, credit=4)
        fin_done = count("fin_done", UNITS, credit=2)
        sq_done = count("sq_done", TT + TT * NOUT, TT + TT * NOUT)
        tanh_done = count("tanh_done", 16, 16)
        prep = count("prep", 11, 15, credit=TT)
        XS_READY, A_READY, BTM_READY, QPE_READY = 0, 4, 5, 6
        XNEW = 7
        small_in = count("small_in", 16 * 3, 16 * 6)
        a_in = count("a_in", 16 * 3, 0)
        b_in = count("b_in", 16 * 3, 0)
        g_in = count("g_in", 16, 0)
        S_READY, SG_READY, LA_READY, QC_READY, Y_READY, GB_READY = 4, 5, 6, 7, 9, 10
        XNEW2 = 11
        boot2_dma = sem("boot2_dma")
        boot2_act = sem("boot2_act")
        boot2_dve = sem("boot2_dve")
        sink_in = count("sink_in", 0, 16)
        sg_in = count("sg_in", 0, 16 * 6)
        gla_in = count("gla_in", 0, 16 * 2)
        gelu_act = count("gelu_act", 0, 4)
        gelu_dve = count("gelu_dve", 0, 4)
        soft_dve = count("soft_dve", 0, 1)
        soft_act = count("soft_act", 0, 2)
        ajob_done = count("ajob_done", 0, 17)
        ajob_ev = count("ajob_ev", 0, 17, credit=2)
        ge_done = count("ge_done", 0, 2 + 2 * LEVELS)
        gt_done = count("gt_done", 0, 28)
        gte_done = count("gte_done", 0, 28)
        gs_done = count("gs_done", 0, 28)
        gm_done = count("gm_done", 0, 28)
        ga_done = count("ga_done", 0, 24)
        go_done = count("go_done", 0, TT)
        go_free = count("go_free", 0, TT)
        go_copied = count("go_copied", 0, TT)
        end_in = count("end_in", 16 * 2, 16 * 4)
        x_saved = count("x_saved", 16 * TT, credit=1)
        mod_landed = [count(f"mod_landed{s}", 16 * NIN * KC // 2, 0) for s in range(2)]
        mod_used = count("mod_used", NIN * KC, 0, credit=2)
        mod_added = count("mod_added", NIN * KC, 0)
        mod_sum = count("mod_sum", NIN, 0, credit=1)
        mod_ev = count("mod_ev", NIN, 0, credit=1)
        mod_row = count("mod_row", 16 * NIN, 0, credit=1)
        dve_link = count("dve_link", DVE_LINKS1, DVE_LINKS2)

        aside = {}

        def apart(eng):
            if eng not in aside:
                aside[eng] = sem(f"aside{len(aside)}")
            eng.sem_inc(aside[eng], 1)

        block = ctx.enter_context(nc.Block())

        qT_c, kT_c, v_c = view(ZT, C_H, SEQ), view(ZK, C_H, SEQ), view(ZV, TT, PW)
        g_c = view(ZQ, C_H, GM, GRID_W)
        q_a, kv_a = view(ZQ, TT, A_H * HD), view(ZV, TT, 2 * A_KV * HD)
        qT_a, kT_a = view(ZT, 4, SEQ), view(ZK, A_KV, SEQ)
        cq_b, ckv_b = view(ZQ, TT, B_Q), view(ZV, TT, B_CKV_W)
        wuq, wukv = view(PP, 4, 768), view(ZK, 2, 1024)
        cos_b = view(PP + 3072, TT, B_ROPE)
        sin_b = view(PP + 3072 + TT * B_ROPE, TT, B_ROPE)
        cqT, ckvT = view(0, 4, SEQ, of=late), view(2048, 2, SEQ, of=late)
        kpT = view(3072, SEQ, of=late)
        qnT, qpT = view(3584, B_H, SEQ, of=late), view(5632, B_H, SEQ, of=late)
        knT, v_b = view(7680, B_H, SEQ, of=late), view(9728, TT, SEQ, of=late)
        qpe = view(11776, TT, B_H * B_ROPE, of=late)
        late_tmp = view(12800, 2, 1024, of=late)

        def ring_free(p, j):
            if j == RH - 1:
                return lin_done, p * TT
            return w_used, p * (ND - 1) + (j - RH + 1 if j >= RH else j - RH + 2)

        def tok(t):
            return slice(t * P, (t + 1) * P)

        def scores_c(h, t):
            return [(qT_c[:, h, tok(t)], kT_c[:, h, :])]

        def scores_a(h, t):
            return [(qT_a[:, h % 4, tok(t)], kT_a[:, h // 4, :])]

        def scores_b(h, t):
            return [(qnT[:, h, tok(t)], knT[:, h, :]), (qpT[0:B_ROPE, h, tok(t)], kpT[0:B_ROPE, :])]

        BR_C = dict(name="C", first=0, heads=C_H, scores=scores_c, v=lambda h, kt: v_c[:, kt, h * HD:(h + 1) * HD],
                    y=Y_C, j0=1)
        BR_A = dict(name="A", first=16, heads=A_H, scores=scores_a,
                    v=lambda h, kt: kv_a[:, kt, (A_KV + h // 4) * HD:(A_KV + h // 4 + 1) * HD], y=0, j0=9)
        BR_B = dict(name="B", first=48, heads=B_H, scores=scores_b, v=lambda h, kt: v_b[:, kt, h * HD:(h + 1) * HD],
                    y=Y_B, j0=19)

        def turn_job(srcs, width, dst, scale=1.0):
            return ("turn", srcs, width, dst, scale)

        def mm_job(groups, n, dst, scale=1.0):
            return ("mm", groups, n, dst, scale)

        JOBS_C = [turn_job([view(PP + 2048, TT, PW)[:, t, h * HD:(h + 1) * HD] for t in range(TT)], P, kT_c[:, h, :])
                  for h in range(C_H)] + \
                 [turn_job([view(PP, TT, PW)[:, t, h * HD:(h + 1) * HD] for t in range(TT)], P, qT_c[:, h, :], SC_C)
                  for h in range(C_H)]
        JOBS_AK = [turn_job([kv_a[:, t, h * HD:(h + 1) * HD] for t in range(TT)], P, kT_a[:, h, :]) for h in range(A_KV)]
        JOBS_AQ = [turn_job([q_a[:, t, h * HD:(h + 1) * HD] for t in range(TT)], P, qT_a[:, h % 4, :]) for h in range(A_H)]
        B_QC, B_KC = KC, KC + 4
        wuq_h = wuq.rearrange("p k (h e) -> p k h e", h=B_H)
        wukv_h = wukv.rearrange("p k (h e) -> p k h e", h=B_H)
        JOBS_B1 = [turn_job([cq_b[:, t, tok(r)] for t in range(TT)], P, cqT[:, r, :], cols[:, B_QC + r:B_QC + r + 1])
                   for r in range(4)] + \
                  [turn_job([ckv_b[:, t, tok(r)] for t in range(TT)], P, ckvT[:, r, :], cols[:, B_KC + r:B_KC + r + 1])
                   for r in range(2)] + \
                  [turn_job([ckv_b[:, t, B_KV:B_CKV_W] for t in range(TT)], B_ROPE, kpT[0:B_ROPE, :])]
        JOBS_B2 = [mm_job([(cqT[:, r, tok(t)], wuq_h[:, r, :, B_NOPE:]) for r in range(4)], B_H * B_ROPE,
                          qpe[:, t, :], SC_B) for t in range(TT)] + \
                  [mm_job([(wuq_h[:, r, h, 0:B_NOPE], cqT[:, r, :]) for r in range(4)], SEQ, qnT[:, h, :], SC_B)
                   for h in range(B_H)] + \
                  [mm_job([(wukv_h[:, r, h, 0:B_NOPE], ckvT[:, r, :]) for r in range(2)], SEQ, knT[:, h, :])
                   for h in range(B_H)] + \
                  [mm_job([(ckvT[:, r, tok(t)], wukv_h[:, r, :, B_NOPE:]) for r in range(2)], SEQ, v_b[:, t, :])
                   for t in range(TT)]
        JOBS_B3 = [turn_job([qpe[:, t, h * B_ROPE:(h + 1) * B_ROPE] for t in range(TT)], B_ROPE, qpT[0:B_ROPE, h, :])
                   for h in range(B_H)]
        assert 1 + len(JOBS_C + JOBS_AK + JOBS_AQ + JOBS_B1 + JOBS_B2 + JOBS_B3) == J1

        q_s, kv_s = view(ZQ, TT, S_H * S_D), view(ZV, TT, 2 * S_KV * S_D)
        qT_s, kT_s = view(ZT, 4, SEQ), view(ZK, S_KV, SEQ)

        def keys_of(n):
            return [n] if n == 0 else [n - 1, n]

        def scores_s(h, n):
            ks = keys_of(n)
            return [(qT_s[0:S_D, h % 4, tok(n)], kT_s[0:S_D, h // 4, ks[0] * P:(ks[-1] + 1) * P])]

        BR_S = dict(name="S", first=0, heads=S_H, scores=scores_s, y=0, j0=1, blk=1,
                    v=lambda h, kt: kv_s[:, kt, (S_KV + h // 4) * S_D:(S_KV + h // 4 + 1) * S_D])

        def tiles_of(br, i):
            return keys_of(i % 4) if br["name"] == "S" else list(range(TT))

        def dv_of(br):
            return S_D if br["name"] == "S" else HD

        JOBS_SK = [turn_job([kv_s[:, t, g * S_D:(g + 1) * S_D] for t in range(TT)], S_D, kT_s[0:S_D, g, :])
                   for g in range(S_KV)]
        JOBS_SQ = [turn_job([q_s[:, t, h * S_D:(h + 1) * S_D] for t in range(TT)], S_D, qT_s[0:S_D, h % 4, :], S_SC)
                   for h in range(S_H)]
        u_g, v_g = view(ZQ, TT, PW), view(ZQ + 2048, TT, PW)
        sg_wt, sg_wT = view(PP, SG_G, P), view(PP + 1024, SG_G, P)
        ln_g, ln_b = view(PP + 2048, PW), view(PP + 2560, PW)
        gelu_tmp = view(ZT, TT * PW)
        qk_g, vv_g = view(ZV, TT, 2, G_H * G_DK), view(ZK, TT, G_H * G_DV)
        cg = view(PP + 3072, TT, G_RANK)
        gate_w, gate_b, gla_g = view(PP + 3136, 256), view(PP + 3392, 256), view(PP + 3648, G_DV)
        gsum, gmasks = view(ZT, LEVELS + 2, P), view(ZT + 1024, LEVELS + 2, P)
        cgT = view(0, SEQ, of=late)
        lg, la = view(512, TT * 256, of=late), view(1536, TT, 256, of=late)
        soft = view(2560, TT * 256, of=late)
        eg = view(3584, 2, 2, 256, of=late)
        qke = late[:, 4608:6656].rearrange(
            "p (r t w n) -> p r t w n", r=2, t=2, w=2)
        qkT = view(6656, 2, 4, P, of=late)
        sacc = view(7680, TT, 2, 2 * P, of=late)
        stmp = view(9728, 2, 2, 2 * P, of=late)
        kt_g, qc_g = view(10752, TT, 256, of=late), view(11776, TT, 256, of=late)
        qcT = view(12800, TT, 2, P, of=late)
        state = view(13824, 8, 2, P, of=late)
        og = view(ZQ, TT, G_H, G_DV)
        osq = view(ZQ + 2048, G_H, G_DV)
        turn_tmp = view(ZT, 2, SEQ)

        JOB_CG = turn_job([cg[:, t, :] for t in range(TT)], G_RANK, cgT[0:G_RANK, :])
        JOBS_QC = [turn_job([qc_g[:, 2 * pr + i, tok(hp)] for i in range(2) for hp in range(2)], P,
                            qcT[:, 2 * pr:2 * pr + 2, :, :].rearrange("p t h n -> p (t h n)")) for pr in range(2)]

        @block.sync
        def _(sp):
            def double(blk, l, p, j, w, col, width=PW):
                sp.wait_ge(lo_done.sem, lo_done.at(blk, l, p * ND + j + 1 - RS))
                apart(sp)
                src = w[bass.ds(l, 1), 2 * j * P:(2 * j + 2) * P, bass.ds(col, width)]
                sp.dma_start(stage[:, j % RS, :, 0:width], src.rearrange("o (a p) n -> p (o a) n", p=P))\
                  .then_inc(w_landed[j % RS].sem, 16)

            def mod_double(l, p, j):
                for k in (2 * j, 2 * j + 1):
                    sp.wait_ge(mod_used.sem, mod_used.at(0, l, p * KC + k + 1 - 2))
                    apart(sp)
                    src = io["w_mod_2"][bass.ds(l, 1), k * P:(k + 1) * P, bass.ds(p * PW, PW)]
                    sp.dma_start(wmod[:, k % 2, :], src.rearrange("o p n -> (o p) n"))\
                      .then_inc(mod_landed[k % 2].sem, 16)

            def in_panel(l, p, col, width=PW):
                for j in range(ND):
                    double(0, l, p, j, io["w_in"], col, width)
                    mod_double(l, p, j)

            def out_panel(blk, l, p, w):
                for j in range(ND):
                    double(blk, l, p, j, w, (p - NIN) * PW)

            sp.sem_inc(x_saved.sem, x_saved.credit)
            for t in range(TT):
                sp.dma_start(Y[:, t, :], x_in[:, t, :]).then_inc(boot_x, 16)
            sp.dma_start(rows[0:KC, :], io["c_2"].rearrange("o (k p) -> (o k) p", p=P)).then_inc(boot_dma, 16)
            sp.dma_start(gmask[:, :], io["near_mask"]).then_inc(boot_dma, 16)
            sp.wait_ge(boot_pool, 6)
            pad = view(0, RPB_P)
            sp.dma_start(pad[0:2 * C_H * RPB_R, 48:48 + RPB_C],
                         io["c_rpb"].rearrange("l h r c -> (l h r) c")).then_inc(boot_rpb, 16)
            sp.wait_ge(boot_rpb, 16)
            sp.dma_start(rpb_dram, pad[0:2 * C_H * RPB_R, :]).then_inc(boot_rpb, 16)
            sp.wait_ge(boot_x, 16 * TT)
            for t in range(TT):
                sp.dma_start(x_dram[:, t, :], Y[:, t, :]).then_inc(boot_x, 16)
            sp.wait_ge(boot_rpb, 32)
            for l in range(2):
                for h in range(C_H):
                    for rr in range(2):
                        src = bass.AP(tensor=rpb_dram.tensor,
                                      offset=((l * C_H + h) * RPB_R + 1 - rr) * RPB_P + GRID_W - 1,
                                      ap=[[RPB_P, GM], [-1, GRID_W], [1, GRID_W]])
                        sp.dma_start(g_dram[l, rr * GRID_W:(rr + 1) * GRID_W, h].rearrange("c m k -> m c k"), src).then_inc(boot_g, 16)
            sp.wait_ge(boot_g, 16 * 16)
            sp.wait_ge(boot_x, 32 * TT)
            sp.wait_ge(boot_pe, 1)

            with sp.Fori(0, 2) as l:
                sp.dma_start(rows[0:KC, :], io["norm_pre"][bass.ds(l, 1), :].rearrange("o (k p) -> (o k) p", p=P))\
                  .then_inc(small_in.sem, 16)
                sp.dma_start(rows[KC:KC + 4, :], io["b_q_norm"][bass.ds(l, 1), :].rearrange("o (k p) -> (o k) p", p=P))\
                  .then_inc(small_in.sem, 16)
                sp.dma_start(rows[KC + 4:KC + 6, :], io["b_kv_norm"][bass.ds(l, 1), :].rearrange("o (k p) -> (o k) p", p=P))\
                  .then_inc(small_in.sem, 16)
                in_panel(l, 0, C_Q0)
                sp.wait_ge(xp_done.sem, xp_done.at(0, l, KC))
                apart(sp)
                sp.dma_start(view(ZQ, C_H * GM * GRID_W),
                             g_dram[bass.ds(l, 1)].rearrange("o p h m k -> (o p) (h m k)")).then_inc(g_in.sem, 16)
                with sp.Fori(1, 4) as p:
                    in_panel(l, p, C_Q0 + p * PW)
                in_panel(l, 4, 0)
                sp.wait_ge(fin_done.sem, fin_done.at(0, l, 16))
                apart(sp)
                sp.dma_start(view(PP + 3072, 2 * TT * HD), io["rope_a"].rearrange("p a t d -> p (a t d)"))\
                  .then_inc(a_in.sem, 16)
                for n, name in enumerate(("a_q_norm", "a_k_norm")):
                    src = io[name][bass.ds(l, 1), :]
                    sp.dma_start(view(PP + 2560 + n * HD, HD), src.broadcast_to([P, HD])).then_inc(a_in.sem, 16)
                with sp.Fori(5, 9) as p:
                    in_panel(l, p, (p - 4) * PW)
                in_panel(l, 9, B_CQ0)
                sp.wait_ge(fin_done.sem, fin_done.at(0, l, 48))
                apart(sp)
                sp.dma_start(view(PP, 4, 768), io["b_w_uq"][bass.ds(l, 1)].rearrange("o (k p) n -> p (o k) n", p=P))\
                  .then_inc(b_in.sem, 16)
                sp.dma_start(view(ZK, 2, 1024), io["b_w_ukv"][bass.ds(l, 1)].rearrange("o (k p) n -> p (o k) n", p=P))\
                  .then_inc(b_in.sem, 16)
                sp.dma_start(view(PP + 3072, 2 * TT * B_ROPE), io["rope_b"].rearrange("p a t d -> p (a t d)"))\
                  .then_inc(b_in.sem, 16)
                in_panel(l, 10, B_CKV0, B_CKV_W)
                in_panel(l, 11, B_G0)
                out_panel(0, l, NIN, io["w_out"])
                sp.wait_ge(fin_done.sem, fin_done.at(0, l, UNITS))
                apart(sp)
                sp.wait_ge(x_saved.sem, x_saved.at(0, l, 0))
                apart(sp)
                sp.dma_start(xs, x_dram).then_inc(end_in.sem, 16)
                src = io["norm_post"][bass.ds(l, 1), :]
                sp.dma_start(view(ZT, DM), src.broadcast_to([P, DM])).then_inc(end_in.sem, 16)
                with sp.Fori(NIN + 1, NP) as p:
                    out_panel(0, l, p, io["w_out"])
                for t in range(TT):
                    sp.wait_ge(prep.sem, prep.at(0, l, XNEW + t + 1))
                    apart(sp)
                    sp.dma_start(x_dram[:, t, :], Y[:, t, :]).then_inc(x_saved.sem, 16)

            sp.wait_ge(mod_row.sem, mod_row.at(0, 2, 0))
            apart(sp)
            sp.wait_ge(mod_added.sem, mod_added.at(0, 2, 0))
            apart(sp)
            sp.dma_start(band[:, :], io["band"]).then_inc(boot2_dma, 16)
            sp.dma_start(pos_i[:, :].rearrange("p (t o) -> p t o", o=1),
                         io["positions_2"].rearrange("o (t p) -> p t o", p=P),
                         allow_slow_non_contiguous=True).then_inc(boot2_dma, 16)
            sp.dma_start(freq[:, :], io["freq"].rearrange("(o f) -> o f", o=1).broadcast_to([P, ROT // 2]))\
              .then_inc(boot2_dma, 16)

            def rows_in(first, src):
                n = src.shape[-1] // P
                sp.dma_start(rows[first:first + n, :], src.rearrange("o (k p) -> (o k) p", p=P)).then_inc(small_in.sem, 16)

            def spread(dst, src, landed):
                sp.dma_start(dst, src.broadcast_to([P, src.shape[-1]])).then_inc(landed.sem, 16)

            with sp.Fori(0, 2) as l:
                one = bass.ds(l, 1)
                sp.wait_ge(job_ev.sem, job_ev.at(1, l, 0))
                apart(sp)
                rows_in(0, io["g_pre_2"][one, :])
                rows_in(16, mod_dram[one, 0:DM])
                rows_in(32, mod_dram[one, DM:2 * DM])
                rows_in(48, io["b_mod_2"][one, 0:DM])
                rows_in(64, io["b_mod_2"][one, DM:2 * DM])
                sp.dma_start(rows[80:80 + SG_G, :], io["sg_b_2"][one].rearrange("o g t -> (o g) t")).then_inc(small_in.sem, 16)
                sp.wait_ge(fin_done.sem, fin_done.at(1, l, 0))
                apart(sp)
                spread(sinks[:, :], io["swa_sinks_2"][one, :], sink_in)
                with sp.Fori(0, 3) as p:
                    for j in range(ND):
                        double(1, l, p, j, io["w_in_2"], p * PW)
                with sp.Fori(3, 7) as p:
                    for j in range(ND):
                        double(1, l, p, j, io["w_in_2"], (p - 3) * PW + Z0)
                for j in range(ND):
                    double(1, l, 7, j, io["w_in_2"], SU0)
                sp.wait_ge(fin_done.sem, fin_done.at(1, l, UNITS))
                apart(sp)
                sp.dma_start(sg_wt, io["sg_w_2"][one].rearrange("o g t s -> t (o g) s")).then_inc(sg_in.sem, 16)
                spread(ln_g, io["sg_ln_g_2"][one, :], sg_in)
                spread(ln_b, io["sg_ln_b_2"][one, :], sg_in)
                sp.dma_start(gate_w[0:G_RANK, :], io["gla_w_gate_up_2"][one].rearrange("o r n -> (o r) n")).then_inc(sg_in.sem, 16)
                spread(gate_b, io["gla_b_gate_2"][one, :], sg_in)
                spread(gla_g, io["gla_norm_g_2"][one, :], sg_in)
                with sp.Fori(8, 11) as p:
                    for j in range(ND):
                        double(1, l, p, j, io["w_in_2"], (p - 7) * PW + SU0)
                for j in range(ND):
                    double(1, l, 11, j, io["w_in_2"], CG0, G_RANK)
                sp.wait_ge(prep.sem, prep.at(1, l, SG_READY + 1))
                apart(sp)
                sp.dma_start(gsum, io["gla_sums"]).then_inc(gla_in.sem, 16)
                sp.dma_start(gmasks, io["gla_masks"]).then_inc(gla_in.sem, 16)
                out_panel(1, l, NIN, io["w_out_2"])
                sp.wait_ge(prep.sem, prep.at(1, l, Y_READY + 1))
                apart(sp)
                sp.wait_ge(x_saved.sem, x_saved.at(1, l, 0))
                apart(sp)
                sp.dma_start(xs, x_dram).then_inc(end_in.sem, 16)
                spread(view(ZT, DM), mod_dram[one, 2 * DM:3 * DM], end_in)
                spread(view(ZV, DM), io["b_mod_2"][one, 2 * DM:3 * DM], end_in)
                out_panel(1, l, NIN + 1, io["w_out_2"])
                sp.wait_ge(prep.sem, prep.at(1, l, GB_READY + 1))
                apart(sp)
                spread(view(ZV, DM), io["g_post_2"][one, :], end_in)
                with sp.Fori(NIN + 2, NP) as p:
                    out_panel(1, l, p, io["w_out_2"])
                for t in range(TT):
                    sp.wait_ge(prep.sem, prep.at(1, l, XNEW2 + t + 1))
                    apart(sp)
                    sp.dma_start(x_dram[:, t, :], Y[:, t, :]).then_inc(x_saved.sem, 16)
            sp.wait_ge(x_saved.sem, x_saved.at(1, 2, 0))
            apart(sp)

        @block.tensor
        def _(pe):
            def panel(blk, l, p, width=PW):
                for j in range(ND):
                    pe.wait_ge(lo_done.sem, lo_done.at(blk, l, p * ND + j + 1))
                    if j == 0:
                        for t in range(TT):
                            pe.wait_ge(lin_free[t].sem, lin_free[t].at(blk, l, p))
                    for a in range(2):
                        k = 2 * j + a
                        hi_w, lo_w = whi[:, j % RH, a, 0:width], wlo[:, j % RH, a, 0:width]
                        for t in range(TT):
                            out = LIN[t][:, 0:width]
                            hi_x, lo_x = act_hi[:, k, tok(t)], act_lo[:, k, tok(t)]
                            pe.matmul(out, hi_x, lo_w, start=(k == 0), stop=False)
                            pe.matmul(out, hi_x, hi_w, start=False, stop=False)
                            mm = pe.matmul(out, lo_x, hi_w, start=False, stop=(k == KC - 1))
                            if k == KC - 1:
                                mm.then_inc(lin_done.sem, 1)
                    if j < ND - 1:
                        mm.then_inc(w_used.sem, 1)

            def turns(blk, l, n0, src):
                for k in range(KC):
                    pe.wait_ge(xp_free.sem, xp_free.at(blk, l, n0 + k + 1 - 4))
                    for t in range(TT):
                        tr = pe.transpose(XP[k % 4][:, tok(t)], src[:, t, tok(k)], ident[:, :])
                    tr.then_inc(xp_done.sem, 1)

            def job(blk, l, n, jb):
                kind, parts, width, dst, scale = jb
                pe.wait_ge(job_ev.sem, job_ev.at(blk, l, n + 1 - 2))
                apart(pe)
                if kind == "turn":
                    for t, src in enumerate(parts):
                        mm = pe.transpose(JOB[n % 2][0:width, t * src.shape[0]:(t + 1) * src.shape[0]], src,
                                          ident[0:src.shape[0], 0:src.shape[0]])
                else:
                    for r, (lhs, rhs) in enumerate(parts):
                        mm = pe.matmul(JOB[n % 2][:, 0:width], lhs, rhs, start=(r == 0), stop=(r == len(parts) - 1))
                mm.then_inc(job_done.sem, 1)

            def score(blk, l, br, i):
                u = br["first"] + i
                pe.wait_ge(exp_done.sem, exp_done.at(blk, l, u + 1 - 2))
                parts = br["scores"](i // 4, i % 4)
                for r, (lhs, rhs) in enumerate(parts):
                    mm = pe.matmul(SCORE[u % 2][:, 0:P * len(tiles_of(br, i))], lhs, rhs, start=(r == 0),
                                   stop=(r == len(parts) - 1))
                mm.then_inc(score_done.sem, 1)

            def turn(blk, l, br, i):
                u = br["first"] + i
                pe.wait_ge(exp_done.sem, exp_done.at(blk, l, u + 1))
                pe.wait_ge(pt_done.sem, pt_done.at(blk, l, u + 1 - 2))
                for kt in range(len(tiles_of(br, i))):
                    mm = pe.transpose(TURN[u % 2][:, tok(kt)], probs[:, u % 4, tok(kt)], ident[:, :])
                mm.then_inc(turn_done.sem, 1)

            def pv(blk, l, br, i):
                u = br["first"] + i
                pe.wait_ge(pt_done.sem, pt_done.at(blk, l, u + 1))
                pe.wait_ge(fin_done.sem, fin_done.at(blk, l, u + 1 - 2))
                tiles = tiles_of(br, i)
                for n, kt in enumerate(tiles):
                    mm = pe.matmul(OUTB[u % 2][:, 0:dv_of(br)], probsT[:, u % 4, tok(n)], br["v"](i // 4, kt),
                                   start=(n == 0), stop=(n == len(tiles) - 1))
                mm.then_inc(pv_done.sem, 1)

            def attention(blk, l, br, early=None):
                n = 4 * br["heads"]
                for i in range(n + 3):
                    if early and i % 4 == 0 and i < n:
                        early(i // 4)
                    if i < n:
                        score(blk, l, br, i)
                    if 2 <= i < n + 2:
                        turn(blk, l, br, i - 2)
                    if i >= 3:
                        pv(blk, l, br, i - 3)
                pe.wait_ge(fin_done.sem, fin_done.at(blk, l, br["first"] + n))

            def mod_row_sum(l, p):
                pe.wait_ge(mod_added.sem, mod_added.at(0, l, (p + 1) * KC))
                pe.wait_ge(mod_ev.sem, mod_ev.at(0, l, p))
                pe.matmul(MSUM[0:1, :], ones[:, 0:1], macc[:, :], start=True, stop=True).then_inc(mod_sum.sem, 1)

            def in_panel(l, p, width=PW):
                panel(0, l, p, width)
                mod_row_sum(l, p)

            def banks_free(l, panels, blk=0):
                for t in range(TT):
                    pe.wait_ge(lin_free[t].sem, lin_free[t].at(blk, l, panels))

            pe.sem_inc(w_used.sem, w_used.credit)
            pe.sem_inc(mod_sum.sem, mod_sum.credit)
            pe.sem_inc(lin_done.sem, lin_done.credit)
            pe.sem_inc(turn_done.sem, turn_done.credit)
            pe.sem_inc(pv_done.sem, pv_done.credit)
            pe.wait_ge(boot_pool, 7)
            pe.wait_ge(boot_dma, 32)
            pe.transpose(JOB[0][:, 0:KC], rows[0:KC, :], ident[0:KC, 0:KC]).then_inc(boot_pe, 1)
            pe.wait_ge(boot_dve, 1)
            with pe.Fori(0, 2) as l:
                pe.wait_ge(small_in.sem, small_in.at(0, l, 48))
                pe.wait_ge(lin_free[0].sem, lin_free[0].at(0, l, 0))
                job(0, l, 0, turn_job([rows[0:KC + 6, :]], P, None))
                for t in range(TT):
                    pe.wait_ge(prep.sem, prep.at(0, l, XS_READY + t + 1))
                turns(0, l, 0, xs)
                pe.wait_ge(xp_free.sem, xp_free.at(0, l, KC))
                pe.wait_ge(job_ev.sem, job_ev.at(0, l, 1))
                apart(pe)
                with pe.Fori(0, 4) as p:
                    in_panel(l, p)
                banks_free(l, 4)
                pe.wait_ge(mod_ev.sem, mod_ev.at(0, l, 4))
                for n, jb in enumerate(JOBS_C):
                    job(0, l, BR_C["j0"] + n, jb)
                pe.wait_ge(job_ev.sem, job_ev.at(0, l, BR_C["j0"] + 8))
                attention(0, l, BR_C)
                apart(pe)
                with pe.Fori(4, 9) as p:
                    in_panel(l, p)
                banks_free(l, 9)
                pe.wait_ge(mod_ev.sem, mod_ev.at(0, l, 9))
                pe.wait_ge(prep.sem, prep.at(0, l, A_READY + 1))
                j0 = BR_A["j0"]
                for n, jb in enumerate(JOBS_AK + JOBS_AQ[0:1]):
                    job(0, l, j0 + n, jb)

                def next_queries(h):
                    if h + 1 < A_H:
                        job(0, l, j0 + 3 + h, JOBS_AQ[h + 1])
                    pe.wait_ge(job_ev.sem, job_ev.at(0, l, j0 + 3 + h))
                attention(0, l, BR_A, next_queries)
                in_panel(l, 9)
                in_panel(l, 10, B_CKV_W)
                in_panel(l, 11)
                banks_free(l, NIN)
                pe.wait_ge(mod_ev.sem, mod_ev.at(0, l, NIN))
                pe.wait_ge(prep.sem, prep.at(0, l, BTM_READY + 1))
                n = BR_B["j0"]
                for jb in JOBS_B1:
                    job(0, l, n, jb)
                    n += 1
                pe.wait_ge(b_in.sem, b_in.at(0, l, 48))
                pe.wait_ge(job_ev.sem, job_ev.at(0, l, n))
                for jb in JOBS_B2:
                    job(0, l, n, jb)
                    n += 1
                pe.wait_ge(prep.sem, prep.at(0, l, QPE_READY + 1))
                for jb in JOBS_B3:
                    job(0, l, n, jb)
                    n += 1
                pe.wait_ge(job_ev.sem, job_ev.at(0, l, n))
                attention(0, l, BR_B)
                turns(0, l, KC, Y)
                pe.wait_ge(xp_free.sem, xp_free.at(0, l, 2 * KC))
                apart(pe)
                with pe.Fori(NIN, NP) as p:
                    panel(0, l, p)

            def ajob(l, n, parts):
                pe.wait_ge(ajob_ev.sem, ajob_ev.at(1, l, n + 1 - 2))
                for lhs, rhs, c, w in parts:
                    mm = pe.matmul(OUTB[n % 2][:, c:c + w], lhs, rhs, start=True, stop=True)
                mm.then_inc(ajob_done.sem, 1)

            def decay_sums(l, n, level, pr):
                ajob(l, n, [(gsum[:, level, :], la[:, 2 * pr + i, :], i * 256, 256) for i in range(2)])

            def level_turns(l, g, level, t):
                if g >= 2:
                    pe.wait_ge(gte_done.sem, gte_done.at(1, l, g + 1 - 2))
                s = g // 2
                if level < LEVELS:
                    pe.wait_ge(ge_done.sem, ge_done.at(1, l, 2 + (s // (LEVELS + 1)) * LEVELS + level + 1))
                for w in range(2):
                    for hp in range(2):
                        src = qk_g[:, t, w, tok(hp)] if level == LEVELS else qke[:, s % 2, t % 2, w, tok(hp)]
                        mm = pe.transpose(TURN[g % 2][:, tok(2 * w + hp)], src, ident[:, :])
                mm.then_inc(gt_done.sem, 1)

            def level_scores(l, g):
                pe.wait_ge(gte_done.sem, gte_done.at(1, l, g + 1))
                if g >= 1:
                    pe.wait_ge(gm_done.sem, gm_done.at(1, l, g))
                for hp in range(2):
                    for e in range(2):
                        half = slice(e * G_DK, (e + 1) * G_DK)
                        mm = pe.matmul(SCORE[e][:, tok(hp)], qkT[half, g % 2, 2 + hp, :], qkT[half, g % 2, hp, :],
                                       start=True, stop=True)
                mm.then_inc(gs_done.sem, 1)

            def gla(l):
                n = 27
                job(1, l, n, JOB_CG)
                pe.wait_ge(job_ev.sem, job_ev.at(1, l, n + 1))
                pe.wait_ge(sg_in.sem, sg_in.at(1, l, 96))
                for pr in range(2):
                    pe.wait_ge(job_ev.sem, job_ev.at(1, l, n + 1 + pr + 1 - 2))
                    for i in range(2):
                        mm = pe.matmul(JOB[(n + 1 + pr) % 2][:, i * 256:(i + 1) * 256], cgT[0:G_RANK, tok(2 * pr + i)],
                                       gate_w[0:G_RANK, :], start=True, stop=True)
                    mm.then_inc(job_done.sem, 1)
                pe.wait_ge(gla_in.sem, gla_in.at(1, l, 32))
                pe.wait_ge(prep.sem, prep.at(1, l, LA_READY + 1))
                for n_, (level, pr) in enumerate(((CUM, 0), (CUM, 1), (TAIL, 0), (TAIL, 1))):
                    decay_sums(l, n_, level, pr)
                ajob(l, 4, [(la[:, t, tok(hp)], gsum[:, CUM, CHUNK - 1:P:CHUNK], hp * 8 + 2 * t, 2)
                            for hp in range(2) for t in range(TT)])
                for pr in range(2):
                    pe.wait_ge(prep.sem, prep.at(1, l, QC_READY + pr + 1))
                    job(1, l, 30 + pr, JOBS_QC[pr])
                pe.wait_ge(ge_done.sem, ge_done.at(1, l, 2))
                for c in range(7):
                    t, half = c // 2, slice(c % 2 * CHUNK, (c % 2 + 1) * CHUNK)
                    pe.wait_ge(job_ev.sem, job_ev.at(1, l, 32 + c + 1 - 2))
                    apart(pe)
                    for hp in range(2):
                        for e in range(2):
                            h = 2 * hp + e
                            mm = pe.matmul(JOB[c % 2][e * G_DK:(e + 1) * G_DK, tok(hp)],
                                           kt_g[half, t, h * G_DK:(h + 1) * G_DK], vv_g[half, t, tok(h)],
                                           start=True, stop=True)
                    mm.then_inc(job_done.sem, 1)
                order = [(pr, level, i) for pr in range(2) for level in range(LEVELS + 1) for i in range(2)]
                decay_sums(l, 5, 0, 0)
                decay_sums(l, 6, 1, 0)
                for g in range(len(order) + 1):
                    if g < len(order):
                        pr, level, i = order[g]
                        level_turns(l, g, level, 2 * pr + i)
                        if i == 1:
                            k = pr * LEVELS + level + 2
                            if level < LEVELS and k < 2 * LEVELS:
                                decay_sums(l, 5 + k, k % LEVELS, k // LEVELS)
                    if g >= 1:
                        level_scores(l, g - 1)
                pe.wait_ge(ga_done.sem, ga_done.at(1, l, 24))
                pe.wait_ge(job_ev.sem, job_ev.at(1, l, 39))
                for t in range(TT):
                    if t >= 2:
                        pe.wait_ge(go_free.sem, go_free.at(1, l, t + 1 - 2))
                    apart(pe)
                    for h in range(G_H):
                        hp, e = h // 2, h % 2
                        for half in range(2):
                            c = 2 * t + half
                            pe.matmul(PAST[t % 2][e][half * CHUNK:(half + 1) * CHUNK, tok(hp)],
                                      qcT[e * G_DK:(e + 1) * G_DK, t, hp, half * CHUNK:(half + 1) * CHUNK],
                                      state[e * G_DK:(e + 1) * G_DK, c, hp, :], start=True, stop=True)
                        mm = pe.matmul(OUTB[t % 2][:, tok(h)], sacc[:, t, e, tok(hp)], vv_g[:, t, tok(h)],
                                       start=True, stop=True)
                    mm.then_inc(go_done.sem, 1)

            with pe.Fori(0, 2) as l:
                pe.wait_ge(small_in.sem, small_in.at(1, l, 96))
                pe.wait_ge(lin_free[0].sem, lin_free[0].at(1, l, 0))
                job(1, l, 0, turn_job([rows[0:88, :]], P, None))
                for t in range(TT):
                    pe.wait_ge(prep.sem, prep.at(1, l, XS_READY + t + 1))
                turns(1, l, 0, xs)
                pe.wait_ge(xp_free.sem, xp_free.at(1, l, KC))
                pe.wait_ge(job_ev.sem, job_ev.at(1, l, 1))
                apart(pe)
                with pe.Fori(0, 7) as p:
                    panel(1, l, p)
                banks_free(l, 7, 1)
                pe.wait_ge(prep.sem, prep.at(1, l, S_READY + 1))
                j0 = BR_S["j0"]
                for n, jb in enumerate(JOBS_SK + JOBS_SQ[0:1]):
                    job(1, l, j0 + n, jb)

                def next_queries2(h):
                    if h + 1 < S_H:
                        job(1, l, j0 + 5 + h, JOBS_SQ[h + 1])
                    pe.wait_ge(job_ev.sem, job_ev.at(1, l, j0 + 5 + h))
                attention(1, l, BR_S, next_queries2)
                apart(pe)
                with pe.Fori(7, 11) as p:
                    panel(1, l, p)
                panel(1, l, 11, G_RANK)
                banks_free(l, NIN, 1)
                pe.wait_ge(gla_in.sem, gla_in.at(1, l, 32))
                pe.wait_ge(prep.sem, prep.at(1, l, SG_READY + 1))
                for n in range(2):
                    job(1, l, 21 + n, turn_job([sg_wt[:, 4 * n + i, :] for i in range(4)], P, None))
                for n in range(4):
                    pe.wait_ge(job_ev.sem, job_ev.at(1, l, max(23, 23 + n + 1 - 2)))
                    for i in range(2):
                        g = 2 * n + i
                        mm = pe.matmul(JOB[(23 + n) % 2][:, i * 256:(i + 1) * 256], sg_wT[:, g, :],
                                       v_g[:, :, g * SG_C:(g + 1) * SG_C], start=True, stop=True)
                    mm.then_inc(job_done.sem, 1)
                gla(l)
                pe.wait_ge(prep.sem, prep.at(1, l, Y_READY + 1))
                turns(1, l, KC, Y)
                pe.wait_ge(xp_free.sem, xp_free.at(1, l, 2 * KC))
                apart(pe)
                with pe.Fori(NIN, NP) as p:
                    panel(1, l, p)

        @block.scalar
        def _(act):
            def split_hi(blk, l, p, j, width=PW):
                act.wait_ge(w_landed[j % RS].sem, w_landed[j % RS].at(blk, l, 16 * (p * (ND // RS) + j // RS + 1)))
                used, n = ring_free(p, j)
                act.wait_ge(used.sem, used.at(blk, l, n))
                act.activation(whi[:, j % RH, :, 0:width], stage[:, j % RS, :, 0:width], ACT.Copy)\
                   .then_inc(hi_done.sem, 1)

            def panel(blk, l, p, take, width=PW, after=True, next_width=PW, between=None):
                for j in range(LEAD, ND):
                    split_hi(blk, l, p, j, width)
                    if between:
                        between(j)
                if after:
                    for j in range(LEAD):
                        split_hi(blk, l, p + 1, j, next_width)
                if take:
                    take(l, p)

            def take_copy(dst, width=PW, blk=0):
                def go(l, p):
                    for t in (0, 2):
                        act.wait_ge(lin_done.sem, lin_done.at(blk, l, p * TT + t + 1))
                        act.activation(dst(t, p), LIN[t][:, 0:width], ACT.Copy).then_inc(lin_free[t].sem, 1)
                return go

            def take_tanh(blk=0):
                def go(l, p):
                    for t in range(TT):
                        act.wait_ge(lin_done.sem, lin_done.at(blk, l, p * TT + t + 1))
                        if t >= 2:
                            act.wait_ge(lin_free[t - 2].sem, lin_free[t - 2].at(blk, l, p + 1))
                        act.activation(tanh_tmp[:, t % 2, :], LIN[t][:, :], ACT.Tanh, scale=0.5)\
                           .then_inc(tanh_done.sem, 1)
                return go

            def mod_row_out(l, p):
                act.wait_ge(mod_sum.sem, mod_sum.at(0, l, p + 1))
                act.wait_ge(mod_row.sem, mod_row.at(0, l, 16 * p))
                act.activation(mrow[:, :], MSUM[0:1, :], ACT.Copy).then_inc(mod_ev.sem, 1)
                act.wait_ge(mod_ev.sem, mod_ev.at(0, l, p + 1))
                act.dma_start(mod_dram[bass.ds(l, 1), bass.ds(p * PW, PW)], mrow[:, :]).then_inc(mod_row.sem, 16)

            def in_panel(l, p, take, **kw):
                panel(0, l, p, take, **kw)
                mod_row_out(l, p)

            def square_sums(blk, l):
                for t in range(TT):
                    act.wait_ge(prep.sem, prep.at(blk, l, t + 1 - TT))
                    act.activation(xs[:, t, :], Y[:, t, :], ACT.Square, accum_out=ss[:, t:t + 1])\
                       .then_inc(sq_done.sem, 1)

            def turned_hi(blk, l, n0, scale, bias=None):
                for k in range(KC):
                    act.wait_ge(xp_done.sem, xp_done.at(blk, l, n0 + k + 1))
                    s = scale if isinstance(scale, float) else scale[:, k:k + 1]
                    act.activation(act_hi[:, k, :], XP[k % 4][:, :], ACT.Copy, scale=s).then_inc(xp_hi.sem, 1)

            def exp(blk, l, br, i):
                u = br["first"] + i
                act.wait_ge(max_done.sem, max_done.at(blk, l, u + 1))
                act.wait_ge(turn_done.sem, turn_done.at(blk, l, u + 1 - 4))
                kw = dict(bias=nmx[:, u % 4, 1:2])
                if br["name"] == "A":
                    kw["scale"] = rsq[:, i % 4, i // 4:i // 4 + 1]
                w = P * len(tiles_of(br, i))
                if br["name"] == "S":
                    act.activation(es[:, u % 4:u % 4 + 1], sinks[:, i // 4:i // 4 + 1], ACT.Exp, bias=nmx[:, u % 4, 1:2])
                act.activation(probs[:, u % 4, 0:w], SCORE[u % 2][:, 0:w], ACT.Exp, accum_out=sm[:, u % 4:u % 4 + 1], **kw)\
                   .then_inc(exp_done.sem, 1)

            def take_turn(blk, l, br, i):
                u = br["first"] + i
                act.wait_ge(turn_done.sem, turn_done.at(blk, l, u + 1))
                act.wait_ge(pv_done.sem, pv_done.at(blk, l, u + 1 - 4))
                w = P * len(tiles_of(br, i))
                act.activation(probsT[:, u % 4, 0:w], TURN[u % 2][:, 0:w], ACT.Copy).then_inc(pt_done.sem, 1)

            def attention(blk, l, br):
                n = 4 * br["heads"]
                for i in range(n + 2):
                    if i < n:
                        exp(blk, l, br, i)
                    if i >= 2:
                        take_turn(blk, l, br, i - 2)

            def out_panel(blk, l, p, after):
                panel(blk, l, p, None, after=after)
                act.wait_ge(sq_done.sem, sq_done.at(blk, l, TT + (p - NIN) * TT))
                for t in range(TT):
                    act.wait_ge(lin_done.sem, lin_done.at(blk, l, p * TT + t + 1))
                    act.activation(view(ZK + t * PW, PW), LIN[t][:, :], ACT.Square,
                                   accum_out=ss[:, bass.ds(TT + t * NOUT + p - NIN, 1)]).then_inc(sq_done.sem, 1)

            act.sem_inc(exp_done.sem, exp_done.credit)
            act.sem_inc(mod_ev.sem, mod_ev.credit)
            act.sem_inc(ajob_ev.sem, ajob_ev.credit)
            act.sem_inc(mod_row.sem, mod_row.credit)
            act.sem_inc(pt_done.sem, pt_done.credit)
            act.wait_ge(boot_pe, 1)
            act.activation(ctmp[:, :], JOB[0][:, 0:KC], ACT.Tanh, scale=0.5).then_inc(boot_act, 1)
            act.wait_ge(boot_x, 16 * 2 * TT)
            act.wait_ge(boot_rpb, 32)
            with act.Fori(0, 2) as l:
                for j in range(LEAD):
                    split_hi(0, l, 0, j)
                square_sums(0, l)
                act.wait_ge(job_ev.sem, job_ev.at(0, l, 1))
                turned_hi(0, l, 0, cols)
                with act.Fori(0, 2) as p:
                    in_panel(l, p, take_copy(lambda t, p: zone[:, bass.ds(p * 2048 + t * PW, PW)]))
                in_panel(l, 2, take_copy(lambda t, p: v_c[:, t, :]))
                in_panel(l, 3, take_tanh())
                attention(0, l, BR_C)
                with act.Fori(4, 6) as p:
                    in_panel(l, p, take_copy(lambda t, p: zone[:, bass.ds(ZQ + t * 1024 + (p - 4) * PW, PW)]))
                in_panel(l, 6, take_copy(lambda t, p: kv_a[:, t, :]))
                with act.Fori(7, 9) as p:
                    in_panel(l, p, take_tanh())
                attention(0, l, BR_A)
                in_panel(l, 9, take_copy(lambda t, p: cq_b[:, t, :]), next_width=B_CKV_W)
                in_panel(l, 10, take_copy(lambda t, p: ckv_b[:, t, :], B_CKV_W), width=B_CKV_W)
                in_panel(l, 11, take_tanh())
                attention(0, l, BR_B)
                turned_hi(0, l, KC, 0.5)
                with act.Fori(NIN, NP - 1) as p:
                    out_panel(0, l, p, True)
                out_panel(0, l, NP - 1, False)
            act.wait_ge(mod_row.sem, mod_row.at(0, 2, 0))

            act.wait_ge(boot2_dve, 10)
            act.activation(rot[:, 1, :, :], rtmp[:, 2, :, :], ACT.Sin).then_inc(boot2_act, 1)
            act.activation(rot[:, 0, :, :], rtmp[:, 3, :, :], ACT.Sin).then_inc(boot2_act, 1)

            def gelu_between(l):
                def go(j):
                    if j not in (2, 3, 4, 5):
                        return
                    x = u_g if j < 4 else v_g
                    if j == 2:
                        for t in range(TT):
                            act.wait_ge(lin_free[t].sem, lin_free[t].at(1, l, 9))
                    act.wait_ge(gelu_dve.sem, gelu_dve.at(1, l, j - 2))
                    if j % 2 == 0:
                        act.activation(gelu_tmp, x.rearrange("p t n -> p (t n)"), ACT.Square).then_inc(gelu_act.sem, 1)
                    else:
                        act.activation(gelu_tmp, gelu_tmp, ACT.Tanh, scale=GELU_B).then_inc(gelu_act.sem, 1)
                return go

            def take_decays(l, n, dst):
                act.wait_ge(ajob_done.sem, ajob_done.at(1, l, n + 1))
                act.activation(dst, OUTB[n % 2][:, 0:512], ACT.Exp).then_inc(ajob_ev.sem, 1)

            def gla(l):
                act.wait_ge(soft_dve.sem, soft_dve.at(1, l, 1))
                act.activation(soft, soft, ACT.Exp).then_inc(soft_act.sem, 1)
                act.wait_ge(soft_act.sem, soft_act.at(1, l, 1))
                act.activation(soft, soft, ACT.Ln, bias=1.0).then_inc(soft_act.sem, 1)
                for n in range(4):
                    if n >= 2:
                        act.wait_ge(prep.sem, prep.at(1, l, QC_READY + n + 1 - 2))
                    take_decays(l, n, eg[:, n % 2, :, :].rearrange("p t n -> p (t n)"))
                act.wait_ge(ajob_done.sem, ajob_done.at(1, l, 5))
                act.activation(decay[:, :, :].rearrange("p h c -> p (h c)"), OUTB[0][:, 0:16], ACT.Exp).then_inc(ajob_ev.sem, 1)

                def level_decays(k):
                    act.wait_ge(ge_done.sem, ge_done.at(1, l, 2 + k + 1 - 2))
                    take_decays(l, 5 + k, eg[:, k % 2, :, :].rearrange("p t n -> p (t n)"))
                level_decays(0)
                level_decays(1)
                for g in range(4 * (LEVELS + 1)):
                    act.wait_ge(gt_done.sem, gt_done.at(1, l, g + 1))
                    if g >= 2:
                        act.wait_ge(gs_done.sem, gs_done.at(1, l, g + 1 - 2))
                    act.activation(qkT[:, g % 2, :, :].rearrange("p w n -> p (w n)"), TURN[g % 2][:, :], ACT.Copy)\
                       .then_inc(gte_done.sem, 1)
                    pr, level, i = g // (2 * LEVELS + 2), g // 2 % (LEVELS + 1), g % 2
                    k = pr * LEVELS + level + 2
                    if i == 1 and level < LEVELS and k < 2 * LEVELS:
                        level_decays(k)

            with act.Fori(0, 2) as l:
                for j in range(LEAD):
                    split_hi(1, l, 0, j)
                square_sums(1, l)
                act.wait_ge(prep.sem, prep.at(1, l, XS_READY + 1))
                for k in range(KC):
                    act.wait_ge(xp_done.sem, xp_done.at(1, l, k + 1))
                    act.wait_ge(xp_free.sem, xp_free.at(1, l, k + 1 - 2))
                    act.activation(turn_tmp[:, k % 2, :], XP[k % 4][:, :], ACT.Identity, scale=cols[:, k:k + 1],
                                   bias=cols[:, KC + k:KC + k + 1]).then_inc(xp_hi.sem, 1)
                with act.Fori(0, 2) as p:
                    panel(1, l, p, take_copy(lambda t, p: zone[:, bass.ds(ZQ + t * 1024 + p * PW, PW)], blk=1))
                panel(1, l, 2, take_copy(lambda t, p: kv_s[:, t, :], blk=1))
                with act.Fori(3, 7) as p:
                    panel(1, l, p, take_tanh(1))
                act.wait_ge(sink_in.sem, sink_in.at(1, l, 16))
                attention(1, l, BR_S)
                with act.Fori(7, 9) as p:
                    panel(1, l, p, take_copy(lambda t, p: zone[:, bass.ds(ZQ + (p - 7) * 2048 + t * PW, PW)], blk=1))
                panel(1, l, 9, take_copy(lambda t, p: view(ZV, TT, PW)[:, t, :], blk=1), between=gelu_between(l))
                panel(1, l, 10, take_copy(lambda t, p: vv_g[:, t, :], blk=1), next_width=G_RANK)
                panel(1, l, 11, take_copy(lambda t, p: cg[:, t, :], G_RANK, blk=1), width=G_RANK)
                gla(l)
                turned_hi(1, l, KC, 0.5)
                with act.Fori(NIN, NP - 1) as p:
                    out_panel(1, l, p, True)
                out_panel(1, l, NP - 1, False)

        @block.vector
        def _(dve):

            def split_lo(blk, l, p, j, width=PW):
                c = p * ND + j
                dve.wait_ge(hi_done.sem, hi_done.at(blk, l, c + 1))
                used, n = ring_free(p, j)
                dve.wait_ge(used.sem, used.at(blk, l, n))
                dve.tensor_tensor(wlo[:, j % RH, :, 0:width], stage[:, j % RS, :, 0:width],
                                  whi[:, j % RH, :, 0:width].bitcast(F32), ALU.subtract).then_inc(lo_done.sem, 1)

            def panel(blk, l, p, take, width=PW, after=True, next_width=PW, between=None):
                for j in range(LEAD, ND):
                    split_lo(blk, l, p, j, width)
                    if between:
                        between(j)
                if after:
                    for j in range(LEAD):
                        split_lo(blk, l, p + 1, j, next_width)
                if take:
                    take(l, p)

            def take_copy(dst, width=PW, blk=0):
                def go(l, p):
                    for t in (1, 3):
                        dve.wait_ge(lin_done.sem, lin_done.at(blk, l, p * TT + t + 1))
                        dve.tensor_copy(dst(t, p), LIN[t][:, 0:width]).then_inc(lin_free[t].sem, 1)
                return go

            def take_gate(ycol, n, blk=0):
                def go(l, p):
                    for t in range(TT):
                        dve.wait_ge(tanh_done.sem, tanh_done.at(blk, l, n(p) * TT + t + 1))
                        dve.scalar_tensor_tensor(out=Y[:, t, bass.ds(ycol(p), PW)], in0=tanh_tmp[:, t % 2, :], scalar=1.0,
                                                 in1=LIN[t][:, :], op0=ALU.add, op1=ALU.mult)\
                           .then_inc(lin_free[t].sem, 1)
                return go

            def rsqrt(blk, l, n, width):
                v, y, a = (nv[:, i, 0:n] for i in range(3))
                dve.wait_ge(dve_link.sem, dve_link.now(blk, l))
                dve.tensor_scalar(v, ss[:, 0:n], 1.0 / width, EPS, ALU.mult, ALU.add).then_inc(dve_link.next(), 1)
                dve.wait_ge(dve_link.sem, dve_link.now(blk, l))
                dve.tensor_scalar(a.bitcast(I32), v.bitcast(I32), 1, None, ALU.logical_shift_right).then_inc(dve_link.next(), 1)
                dve.wait_ge(dve_link.sem, dve_link.now(blk, l))
                dve.tensor_scalar(y.bitcast(I32), a.bitcast(I32), -1, 0x5F3759DF, ALU.mult, ALU.add).then_inc(dve_link.next(), 1)
                for i in range(3):
                    dve.wait_ge(dve_link.sem, dve_link.now(blk, l))
                    dve.tensor_tensor(a, y, y, ALU.mult).then_inc(dve_link.next(), 1)
                    dve.wait_ge(dve_link.sem, dve_link.now(blk, l))
                    dve.scalar_tensor_tensor(out=a, in0=a, scalar=-0.5, in1=v, op0=ALU.mult, op1=ALU.mult).then_inc(dve_link.next(), 1)
                    dve.wait_ge(dve_link.sem, dve_link.now(blk, l))
                    out = rs[:, 0:n] if i == 2 else y
                    dve.scalar_tensor_tensor(out=out, in0=a, scalar=1.5, in1=y, op0=ALU.add, op1=ALU.mult).then_inc(dve_link.next(), 1)
                dve.wait_ge(dve_link.sem, dve_link.now(blk, l))

            def normalise(blk, l):
                for t in range(TT):
                    dve.wait_ge(sq_done.sem, sq_done.at(blk, l, t + 1))
                rsqrt(blk, l, TT, DM)
                for t in range(TT):
                    dve.tensor_scalar(xs[:, t, :], Y[:, t, :], rs[:, t:t + 1], None, ALU.mult).then_inc(prep.sem, 1)

            def turned_lo(blk, l, n0, scale):
                for k in range(KC):
                    dve.wait_ge(xp_hi.sem, xp_hi.at(blk, l, n0 + k + 1))
                    s = scale if isinstance(scale, float) else scale[:, k:k + 1]
                    dve.scalar_tensor_tensor(out=act_lo[:, k, :], in0=XP[k % 4][:, :], scalar=s,
                                             in1=act_hi[:, k, :].bitcast(F32), op0=ALU.mult, op1=ALU.subtract)\
                       .then_inc(xp_free.sem, 1)

            def take_job(blk, l, n, jb):
                kind, parts, width, dst, scale = jb
                dve.wait_ge(job_done.sem, job_done.at(blk, l, n + 1))
                if kind == "turn":
                    src = JOB[n % 2][0:width, 0:sum(s.shape[0] for s in parts)]
                else:
                    src = JOB[n % 2][:, 0:width]
                if isinstance(scale, float) and scale == 1.0:
                    dve.tensor_copy(dst, src).then_inc(job_ev.sem, 1)
                else:
                    dve.tensor_scalar(dst, src, scale, None, ALU.mult).then_inc(job_ev.sem, 1)

            def row_max(blk, l, br, i):
                u = br["first"] + i
                h, t = i // 4, i % 4
                dve.wait_ge(score_done.sem, score_done.at(blk, l, u + 1))
                s, m, nm = SCORE[u % 2][:, :], nmx[:, u % 4, 0:1], nmx[:, u % 4, 1:2]
                if br["name"] == "C":
                    bias = g_c[:, h, 6 - 2 * t:14 - 2 * t, :].rearrange("p m k -> p (m k)")
                    apart(dve)
                    dve.tensor_tensor_reduce(s, s, bias, 1.0, -3.0e38, ALU.add, ALU.max, m).then_inc(dve_link.next(), 1)
                    dve.wait_ge(dve_link.sem, dve_link.now(blk, l))
                    dve.tensor_scalar(nm, m, -1.0, None, ALU.mult).then_inc(max_done.sem, 1)
                elif br["name"] == "A":
                    dve.tensor_reduce(m, s, AX.X, ALU.max, negate=True).then_inc(dve_link.next(), 1)
                    dve.wait_ge(dve_link.sem, dve_link.now(blk, l))
                    dve.tensor_tensor(nm, m, rsq[:, t, h:h + 1], ALU.mult).then_inc(max_done.sem, 1)
                elif br["name"] == "S":
                    w = P * len(tiles_of(br, i))
                    apart(dve)
                    dve.tensor_tensor_reduce(s[:, 0:w], s[:, 0:w], band[:, 2 * P - w:2 * P], 1.0, sinks[:, h:h + 1],
                                             ALU.add, ALU.max, m).then_inc(dve_link.next(), 1)
                    dve.wait_ge(dve_link.sem, dve_link.now(blk, l))
                    dve.tensor_scalar(nm, m, -1.0, None, ALU.mult).then_inc(max_done.sem, 1)
                else:
                    dve.tensor_reduce(nm, s, AX.X, ALU.max, negate=True).then_inc(max_done.sem, 1)

            def finish(blk, l, br, i):
                u = br["first"] + i
                h, t = i // 4, i % 4
                dve.wait_ge(pv_done.sem, pv_done.at(blk, l, u + 1))
                total, dv = sm[:, u % 4:u % 4 + 1], dv_of(br)
                if br["name"] == "S":
                    total = den[:, u % 4:u % 4 + 1]
                    dve.tensor_tensor(total, sm[:, u % 4:u % 4 + 1], es[:, u % 4:u % 4 + 1], ALU.add).then_inc(dve_link.next(), 1)
                    dve.wait_ge(dve_link.sem, dve_link.now(blk, l))
                dve.reciprocal(ri[:, u % 4, 0:1], total).then_inc(dve_link.next(), 1)
                dve.wait_ge(dve_link.sem, dve_link.now(blk, l))
                y = Y[:, t, br["y"] + h * dv:br["y"] + (h + 1) * dv]
                dve.scalar_tensor_tensor(out=y, in0=OUTB[u % 2][:, 0:dv], scalar=ri[:, u % 4, 0:1], in1=y,
                                         op0=ALU.mult, op1=ALU.mult).then_inc(fin_done.sem, 1)

            def attention(blk, l, br, early=None):
                n = 4 * br["heads"]
                for i in range(n + 3):
                    if early and i % 4 == 0 and i < n:
                        early(i // 4)
                    if i < n:
                        row_max(blk, l, br, i)
                    if i >= 3:
                        finish(blk, l, br, i - 3)

            def out_panel(blk, l, p, after, between=None):
                panel(blk, l, p, None, after=after, between=between)
                for t in range(TT):
                    dve.wait_ge(sq_done.sem, sq_done.at(blk, l, TT + (p - NIN) * TT + t + 1))
                    dve.tensor_copy(Y[:, t, bass.ds((p - NIN) * PW, PW)], LIN[t][:, :]).then_inc(lin_free[t].sem, 1)

            def residual(blk, l):
                dve.tensor_reduce(ss[:, 0:TT], ss[:, TT:TT + TT * NOUT].rearrange("p (t q) -> p t q", t=TT), AX.X, ALU.add).then_inc(dve_link.next(), 1)
                rsqrt(blk, l, TT, DM)
                dve.wait_ge(end_in.sem, end_in.at(blk, l, 64 if blk else 32))
                if blk:
                    dve.tensor_tensor(view(ZT, DM), view(ZT, DM), view(ZV, DM), ALU.mult).then_inc(dve_link.next(), 1)
                    dve.wait_ge(dve_link.sem, dve_link.now(blk, l))
                for t in range(TT):
                    dve.scalar_tensor_tensor(out=Y[:, t, :], in0=Y[:, t, :], scalar=rs[:, t:t + 1], in1=view(ZT, DM),
                                             op0=ALU.mult, op1=ALU.mult).then_inc(dve_link.next(), 1)
                    dve.wait_ge(dve_link.sem, dve_link.now(blk, l))
                    dve.tensor_tensor(Y[:, t, :], Y[:, t, :], xs[:, t, :], ALU.add).then_inc(prep.sem, 1)

            def rope(blk, l, x, t1, t2, cos, sin, half):
                dve.tensor_tensor(t1, x, cos, ALU.mult).then_inc(dve_link.next(), 1)
                for s in range(2):
                    dve.tensor_tensor(t2.rearrange("p h (a s f) -> p h a s f", a=2, s=2)[:, :, :, s, :],
                                      x.rearrange("p h (a s f) -> p h a s f", a=2, s=2)[:, :, :, 1 - s, :],
                                      sin.rearrange("p h (a s f) -> p h a s f", a=2, s=2)[:, :, :, s, :], ALU.mult).then_inc(dve_link.next(), 1)
                dve.wait_ge(dve_link.sem, dve_link.now(blk, l))
                return dve.tensor_tensor(x, t1, t2, ALU.add)

            def over(ap, n):
                return ap.unsqueeze(1).broadcast_to([P, n, ap.shape[-1]])

            gains_a = view(PP + 2560, 2, HD)
            rope_a = view(PP + 3072, 2, TT, HD)

            def a_sums(l, t):
                nh = A_H + A_KV
                sq = view(PP, nh, HD)
                if t == 0:
                    for i in range(TT):
                        dve.wait_ge(lin_free[i].sem, lin_free[i].at(0, l, 7))
                q, k = q_a[:, t, :], kv_a[:, t, 0:A_KV * HD]
                dve.wait_ge(dve_link.sem, dve_link.now(0, l))
                dve.tensor_tensor(view(PP, A_H * HD), q, q, ALU.mult).then_inc(dve_link.next(), 1)
                dve.tensor_tensor(view(PP + A_H * HD, A_KV * HD), k, k, ALU.mult).then_inc(dve_link.next(), 1)
                dve.wait_ge(dve_link.sem, dve_link.now(0, l))
                dve.tensor_reduce(ss[:, t * nh:(t + 1) * nh], sq, AX.X, ALU.add).then_inc(dve_link.next(), 1)

            def a_rope(l, t):
                nh = A_H + A_KV
                q = q_a[:, t, :].rearrange("p (h d) -> p h d", d=HD)
                k = kv_a[:, t, 0:A_KV * HD].rearrange("p (h d) -> p h d", d=HD)
                rk = rs[:, t * nh + A_H:(t + 1) * nh].unsqueeze(2).broadcast_to([P, A_KV, HD])
                if t == 0:
                    dve.wait_ge(a_in.sem, a_in.at(0, l, 48))
                dve.tensor_tensor(k, k, rk, ALU.mult).then_inc(dve_link.next(), 1)
                dve.tensor_tensor(q, q, over(gains_a[:, 0, :], A_H), ALU.mult).then_inc(dve_link.next(), 1)
                dve.wait_ge(dve_link.sem, dve_link.now(0, l))
                dve.tensor_tensor(k, k, over(gains_a[:, 1, :], A_KV), ALU.mult).then_inc(dve_link.next(), 1)
                dve.wait_ge(dve_link.sem, dve_link.now(0, l))
                for x, n, o in ((q, A_H, 0), (k, A_KV, A_H * HD)):
                    done = rope(0, l, x, view(PP + o, n, HD), view(PP + 1280 + o, n, HD),
                                over(rope_a[:, 0, t, :], n), over(rope_a[:, 1, t, :], n), 32)
                    if t == TT - 1 and n == A_KV:
                        done.then_inc(prep.sem, 1)
                    else:
                        done.then_inc(dve_link.next(), 1)
                        dve.wait_ge(dve_link.sem, dve_link.now(0, l))

            def a_between1(l):
                def go(j):
                    if j < 6:
                        a_sums(l, j - 2)
                    elif j == 6:
                        rsqrt(0, l, TT * (A_H + A_KV), HD)
                        dve.tensor_scalar(rsq[:, :, :], rs[:, 0:40].rearrange("p (t h) -> p t h", t=TT)[:, :, 0:A_H],
                                          SC_A, None, ALU.mult).then_inc(dve_link.next(), 1)
                    else:
                        a_rope(l, 0)
                return go

            def a_between2(l):
                def go(j):
                    if j < 5:
                        a_rope(l, j - 1)
                return go

            def b_between(l):
                junk = view(ZT + 1024, PW)

                def go(j):
                    if j == 2:
                        for t in range(TT):
                            dve.wait_ge(lin_free[t].sem, lin_free[t].at(0, l, 11))
                        for t in range(TT):
                            for x, o in ((cq_b[:, t, :], 0), (ckv_b[:, t, 0:B_KV], TT)):
                                dve.tensor_tensor_reduce(junk[:, 0:x.shape[-1]], x, x, float(B_Q // x.shape[-1]), 0.0,
                                                         ALU.mult, ALU.add, ss[:, o + t:o + t + 1]).then_inc(dve_link.next(), 1)
                                dve.wait_ge(dve_link.sem, dve_link.now(0, l))
                    elif j == 3:
                        rsqrt(0, l, 2 * TT, B_Q)
                    elif j == 4:
                        for t in range(TT):
                            dve.tensor_scalar(cq_b[:, t, :], cq_b[:, t, :], rs[:, t:t + 1], None, ALU.mult).then_inc(dve_link.next(), 1)
                            dve.tensor_scalar(ckv_b[:, t, 0:B_KV], ckv_b[:, t, 0:B_KV], rs[:, TT + t:TT + t + 1], None,
                                              ALU.mult).then_inc(dve_link.next(), 1)
                    elif j == 5:
                        dve.wait_ge(b_in.sem, b_in.at(0, l, 48))
                        dve.wait_ge(dve_link.sem, dve_link.now(0, l))
                        rope(0, l, ckv_b[:, :, B_KV:B_CKV_W], view(PP + 3584, TT, B_ROPE), view(PP + 3840, TT, B_ROPE),
                             cos_b, sin_b, 16).then_inc(prep.sem, 1)
                return go

            dve.sem_inc(lo_done.sem, lo_done.credit)
            for c in lin_free:
                dve.sem_inc(c.sem, c.credit)
            for c in (xp_free, job_ev, fin_done, prep):
                dve.sem_inc(c.sem, c.credit)
            dve.wait_ge(boot_act, 1)
            dve.scalar_tensor_tensor(out=csil[:, :], in0=ctmp[:, :], scalar=1.0, in1=JOB[0][:, 0:KC],
                                     op0=ALU.add, op1=ALU.mult).then_inc(boot_dve, 1)
            dve.wait_ge(boot_dve, 1)
            dve.tensor_scalar(csil[:, :], csil[:, :], 0.5, None, ALU.mult).then_inc(boot_dve, 1)
            dve.wait_ge(boot_g, 256)
            with dve.Fori(0, 2) as l:
                dve_link.made = 0
                for j in range(LEAD):
                    split_lo(0, l, 0, j)
                dve.wait_ge(job_done.sem, job_done.at(0, l, 1))
                dve.tensor_copy(cols[:, 0:KC + 6], JOB[0][:, 0:KC + 6]).then_inc(job_ev.sem, 1)
                normalise(0, l)
                dve.wait_ge(job_ev.sem, job_ev.at(0, l, 1))
                turned_lo(0, l, 0, cols)

                def mask_bias(j):
                    if j == 4:
                        dve.wait_ge(g_in.sem, g_in.at(0, l, 16))
                        g = view(ZQ, C_H * GM, GRID_W)
                        dve.tensor_tensor(g, g, over(gmask[:, :], C_H * GM), ALU.add).then_inc(dve_link.next(), 1)

                with dve.Fori(0, 2) as p:
                    panel(0, l, p, take_copy(lambda t, p: zone[:, bass.ds(p * 2048 + t * PW, PW)]))
                panel(0, l, 2, take_copy(lambda t, p: v_c[:, t, :]), between=mask_bias)
                dve.wait_ge(x_saved.sem, x_saved.at(0, l, 0))
                panel(0, l, 3, take_gate(lambda p: Y_C, lambda p: 0))
                for n, jb in enumerate(JOBS_C):
                    take_job(0, l, BR_C["j0"] + n, jb)
                dve.wait_ge(dve_link.sem, dve_link.now(0, l))
                attention(0, l, BR_C)
                with dve.Fori(4, 6) as p:
                    panel(0, l, p, take_copy(lambda t, p: zone[:, bass.ds(ZQ + t * 1024 + (p - 4) * PW, PW)]))
                panel(0, l, 6, take_copy(lambda t, p: kv_a[:, t, :]))
                panel(0, l, 7, take_gate(lambda p: 0, lambda p: 1), between=a_between1(l))
                panel(0, l, 8, take_gate(lambda p: PW, lambda p: 2), between=a_between2(l))
                j0 = BR_A["j0"]
                for n, jb in enumerate(JOBS_AK + JOBS_AQ[0:1]):
                    take_job(0, l, j0 + n, jb)

                def next_queries(h):
                    if h + 1 < A_H:
                        take_job(0, l, j0 + 3 + h, JOBS_AQ[h + 1])
                attention(0, l, BR_A, next_queries)
                panel(0, l, 9, take_copy(lambda t, p: cq_b[:, t, :]), next_width=B_CKV_W)
                panel(0, l, 10, take_copy(lambda t, p: ckv_b[:, t, :], B_CKV_W), width=B_CKV_W)
                panel(0, l, 11, take_gate(lambda p: Y_B, lambda p: 3), between=b_between(l))
                n = BR_B["j0"]
                for jb in JOBS_B1 + JOBS_B2:
                    take_job(0, l, n, jb)
                    n += 1
                dve.wait_ge(job_ev.sem, job_ev.at(0, l, BR_B["j0"] + 11))
                for t in range(TT):
                    x = qpe[:, t, :].rearrange("p (h d) -> p h d", h=B_H)
                    done = rope(0, l, x, late_tmp[:, 0, t * 256:(t + 1) * 256].rearrange("p (h d) -> p h d", h=B_H),
                                late_tmp[:, 1, t * 256:(t + 1) * 256].rearrange("p (h d) -> p h d", h=B_H),
                                over(cos_b[:, t, :], B_H), over(sin_b[:, t, :], B_H), 16)
                    if t == TT - 1:
                        done.then_inc(prep.sem, 1)
                    else:
                        done.then_inc(dve_link.next(), 1)
                dve.wait_ge(dve_link.sem, dve_link.now(0, l))
                for jb in JOBS_B3:
                    take_job(0, l, n, jb)
                    n += 1
                attention(0, l, BR_B)
                turned_lo(0, l, KC, 0.5)
                with dve.Fori(NIN, NP - 1) as p:
                    out_panel(0, l, p, True)
                out_panel(0, l, NP - 1, False)
                residual(0, l)
                assert dve_link.made == DVE_LINKS1, dve_link.made

            dve.wait_ge(boot2_dma, 48)
            booted = [0]

            def boot(ins):
                ins.then_inc(boot2_dve, 1)
                booted[0] += 1
                dve.wait_ge(boot2_dve, booted[0])
            r = [rtmp[:, i, :, :] for i in range(6)]
            boot(dve.tensor_copy(pos_f[:, :], pos_i[:, :]))
            boot(dve.tensor_tensor(r[0], pos_f[:, :].unsqueeze(2).broadcast_to([P, TT, ROT // 2]),
                                   freq[:, :].unsqueeze(1).broadcast_to([P, TT, ROT // 2]), ALU.mult))
            boot(dve.tensor_scalar(r[1], r[0], 1 / (2 * np.pi), 1.5 * 2 ** 23, ALU.mult, ALU.add))
            boot(dve.tensor_scalar(r[1], r[1], 1.5 * 2 ** 23, None, ALU.subtract))
            turn1, turn2 = 6.28125, 0.0019350051879882812
            boot(dve.scalar_tensor_tensor(out=r[4], in0=r[1], scalar=-turn1, in1=r[0], op0=ALU.mult, op1=ALU.add))
            boot(dve.scalar_tensor_tensor(out=r[5], in0=r[1], scalar=-turn2, in1=r[4], op0=ALU.mult, op1=ALU.add))
            boot(dve.scalar_tensor_tensor(out=r[4], in0=r[1], scalar=-(2 * np.pi - turn1 - turn2), in1=r[5],
                                          op0=ALU.mult, op1=ALU.add))
            boot(dve.tensor_scalar(r[2], r[4], 3.1415925, -3.1415925, ALU.min, ALU.max))
            boot(dve.scalar_tensor_tensor(out=r[0], in0=r[2], scalar=-1.0, in1=r[2], op0=ALU.mult, op1=ALU.max))
            boot(dve.tensor_scalar(r[3], r[0], -1.0, np.pi / 2, ALU.mult, ALU.add))
            assert booted[0] == 10

            def swa_rope(l):
                for t in range(TT):
                    dve.wait_ge(lin_free[t].sem, lin_free[t].at(1, l, 3))
                dve.wait_ge(boot2_act, 2)
                hh = ROT // 2
                cos = rot[:, 0, :, :].unsqueeze(2)
                sin = rot[:, 1, :, :].unsqueeze(2)
                for x, n, o in ((q_s, S_H, 0), (kv_s[:, :, 0:S_KV * S_D], S_KV, 2048)):
                    xh = x.rearrange("p t (h d) -> p t h d", d=S_D)
                    x1, x2 = xh[:, :, :, 0:hh], xh[:, :, :, hh:ROT]
                    c, s_ = (a.broadcast_to([P, TT, n, hh]) for a in (cos, sin))
                    t1, t2, t3, t4 = (view(PP + o + i * TT * n * hh, TT, n, hh) for i in range(4))
                    dve.tensor_tensor(t1, x1, c, ALU.mult).then_inc(dve_link.next(), 1)
                    dve.tensor_tensor(t2, x2, s_, ALU.mult).then_inc(dve_link.next(), 1)
                    dve.tensor_tensor(t3, x2, c, ALU.mult).then_inc(dve_link.next(), 1)
                    dve.tensor_tensor(t4, x1, s_, ALU.mult).then_inc(dve_link.next(), 1)
                    dve.wait_ge(dve_link.sem, dve_link.now(1, l))
                    dve.tensor_tensor(x1, t1, t2, ALU.subtract).then_inc(dve_link.next(), 1)
                    if n == S_H:
                        dve.tensor_tensor(x2, t3, t4, ALU.add).then_inc(dve_link.next(), 1)
                dve.wait_ge(dve_link.sem, dve_link.now(1, l))
                dve.tensor_tensor(x2, t3, t4, ALU.add).then_inc(prep.sem, 1)

            def gelu_between(l):
                def go(j):
                    if j not in (2, 3, 4, 5):
                        return
                    x = (u_g if j < 4 else v_g).rearrange("p t n -> p (t n)")
                    if j == 2:
                        for t in range(TT):
                            dve.wait_ge(lin_free[t].sem, lin_free[t].at(1, l, 9))
                    dve.wait_ge(gelu_act.sem, gelu_act.at(1, l, j - 1))
                    if j % 2 == 0:
                        dve.tensor_scalar(gelu_tmp, gelu_tmp, GELU_A, 1.0, ALU.mult, ALU.add).then_inc(dve_link.next(), 1)
                        dve.wait_ge(dve_link.sem, dve_link.now(1, l))
                        dve.tensor_tensor(gelu_tmp, gelu_tmp, x, ALU.mult).then_inc(gelu_dve.sem, 1)
                    else:
                        dve.scalar_tensor_tensor(out=x, in0=gelu_tmp, scalar=1.0, in1=x, op0=ALU.add, op1=ALU.mult)\
                           .then_inc(gelu_dve.sem, 1)
                return go

            def norm_between(l):
                def go(j):
                    if j == 2:
                        dve.wait_ge(gelu_dve.sem, gelu_dve.at(1, l, 4))
                        for t in range(TT):
                            dve.bn_stats(bnst[:, t, :], v_g[:, t, :]).then_inc(dve_link.next(), 1)
                        dve.wait_ge(dve_link.sem, dve_link.now(1, l))
                        apart(dve)
                        for t in range(TT):
                            dve.bn_aggr(mv[:, t, :], bnst[:, t, :]).then_inc(dve_link.next(), 1)
                        dve.wait_ge(dve_link.sem, dve_link.now(1, l))
                        dve.tensor_copy(ss[:, 0:TT], mv[:, :, 1]).then_inc(dve_link.next(), 1)
                        rsqrt(1, l, TT, 4.0)
                        dve.tensor_scalar(rs[:, 0:TT], rs[:, 0:TT], 0.5, None, ALU.mult).then_inc(dve_link.next(), 1)
                        dve.wait_ge(sg_in.sem, sg_in.at(1, l, 96))
                        dve.wait_ge(dve_link.sem, dve_link.now(1, l))
                    elif j in (3, 4):
                        for t in (2 * j - 6, 2 * j - 5):
                            dve.tensor_scalar(v_g[:, t, :], v_g[:, t, :], mv[:, t, 0:1], rs[:, t:t + 1],
                                              ALU.subtract, ALU.mult).then_inc(dve_link.next(), 1)
                            dve.wait_ge(dve_link.sem, dve_link.now(1, l))
                            dve.tensor_tensor(v_g[:, t, :], v_g[:, t, :], ln_g, ALU.mult).then_inc(dve_link.next(), 1)
                            dve.wait_ge(dve_link.sem, dve_link.now(1, l))
                            done = dve.tensor_tensor(v_g[:, t, :], v_g[:, t, :], ln_b, ALU.add)
                            if t == TT - 1:
                                done.then_inc(prep.sem, 1)
                            else:
                                done.then_inc(dve_link.next(), 1)
                return go

            def spatial(l):
                for n in range(2):
                    dve.wait_ge(job_done.sem, job_done.at(1, l, 21 + n + 1))
                    dve.scalar_tensor_tensor(out=sg_wT[:, 4 * n:4 * n + 4, :],
                                             in0=JOB[(21 + n) % 2][:, :].rearrange("p (g t) -> p g t", g=4), scalar=0.5,
                                             in1=gmasks[:, LEVELS + 1, :].unsqueeze(1).broadcast_to([P, 4, P]),
                                             op0=ALU.mult, op1=ALU.mult).then_inc(job_ev.sem, 1)
                for n in range(4):
                    dve.wait_ge(job_done.sem, job_done.at(1, l, 23 + n + 1))
                    for i in range(2):
                        g = 2 * n + i
                        tmp = view(PP + (n % 2) * PW + i * 256, TT, SG_C)
                        src = JOB[(23 + n) % 2][:, i * 256:(i + 1) * 256].rearrange("p (t c) -> p t c", t=TT)
                        ins = dve.scalar_tensor_tensor(out=tmp, in0=src, scalar=bias_c[:, g:g + 1],
                                                       in1=u_g[:, :, g * SG_C:(g + 1) * SG_C], op0=ALU.add, op1=ALU.mult)
                        if i == 1:
                            ins.then_inc(job_ev.sem, 1)
                        else:
                            ins.then_inc(dve_link.next(), 1)
                    dve.wait_ge(job_ev.sem, job_ev.at(1, l, 23 + n + 1))
                    dve.wait_ge(dve_link.sem, dve_link.now(1, l))
                    for i in range(2):
                        g = 2 * n + i
                        y = Y[:, :, Y_B + g * SG_C:Y_B + (g + 1) * SG_C]
                        dve.tensor_tensor(y, y, view(PP + (n % 2) * PW + i * 256, TT, SG_C), ALU.mult).then_inc(dve_link.next(), 1)

            def gla(l):
                take_job(1, l, 27, JOB_CG)
                for pr in range(2):
                    dve.wait_ge(job_done.sem, job_done.at(1, l, 28 + pr + 1))
                    dve.tensor_tensor(lg[:, pr * 512:(pr + 1) * 512].rearrange("p (t n) -> p t n", t=2),
                                      JOB[pr % 2][:, :].rearrange("p (t n) -> p t n", t=2),
                                      over(gate_b, 2), ALU.add).then_inc(job_ev.sem, 1)
                dve.wait_ge(job_ev.sem, job_ev.at(1, l, 30))
                dve.scalar_tensor_tensor(out=soft, in0=lg, scalar=-1.0, in1=lg, op0=ALU.mult, op1=ALU.min)\
                   .then_inc(soft_dve.sem, 1)
                dve.tensor_scalar(qk_g[:, :, 0, :], qk_g[:, :, 0, :], G_DK ** -0.5, None, ALU.mult).then_inc(dve_link.next(), 1)
                dve.wait_ge(soft_act.sem, soft_act.at(1, l, 2))
                dve.scalar_tensor_tensor(out=la.rearrange("p t n -> p (t n)"), in0=lg, scalar=0.0, in1=soft,
                                         op0=ALU.min, op1=ALU.subtract).then_inc(prep.sem, 1)
                dve.wait_ge(dve_link.sem, dve_link.now(1, l))
                for n in range(2):
                    dve.wait_ge(ajob_ev.sem, ajob_ev.at(1, l, n + 1))
                    dve.tensor_tensor(qc_g[:, 2 * n:2 * n + 2, :], qk_g[:, 2 * n:2 * n + 2, 0, :], eg[:, n % 2, :, :],
                                      ALU.mult).then_inc(prep.sem, 1)
                for n in range(2):
                    dve.wait_ge(ajob_ev.sem, ajob_ev.at(1, l, 2 + n + 1))
                    dve.tensor_tensor(kt_g[:, 2 * n:2 * n + 2, :], qk_g[:, 2 * n:2 * n + 2, 1, :], eg[:, n % 2, :, :],
                                      ALU.mult).then_inc(ge_done.sem, 1)
                for pr in range(2):
                    take_job(1, l, 30 + pr, JOBS_QC[pr])
                dve.wait_ge(ajob_ev.sem, ajob_ev.at(1, l, 5))
                dve.memset(state[:, 0, :, :], 0.0).then_inc(dve_link.next(), 1)
                for c in range(7):
                    dve.wait_ge(job_done.sem, job_done.at(1, l, 32 + c + 1))
                    if c == 0:
                        dve.tensor_copy(state[:, 1, :, :], JOB[0][:, 0:256].rearrange("p (h v) -> p h v", h=2))\
                           .then_inc(job_ev.sem, 1)
                        continue
                    dve.wait_ge(job_ev.sem, job_ev.at(1, l, 32 + c))
                    dve.wait_ge(dve_link.sem, dve_link.now(1, l))
                    for hp in range(2):
                        ins = dve.scalar_tensor_tensor(out=state[:, c + 1, hp, :], in0=state[:, c, hp, :],
                                                       scalar=decay[:, hp, c:c + 1], in1=JOB[c % 2][:, tok(hp)],
                                                       op0=ALU.mult, op1=ALU.add)
                        if hp == 0:
                            ins.then_inc(dve_link.next(), 1)
                        else:
                            ins.then_inc(job_ev.sem, 1)

                def decayed(k):
                    pr, level = k // LEVELS, k % LEVELS
                    s = pr * (LEVELS + 1) + level
                    dve.wait_ge(ajob_ev.sem, ajob_ev.at(1, l, 5 + k + 1))
                    if s >= 2:
                        dve.wait_ge(gt_done.sem, gt_done.at(1, l, 2 * (s - 1)))
                    for i in range(2):
                        ins = dve.tensor_tensor(qke[:, s % 2, i, :, :], qk_g[:, 2 * pr + i, :, :],
                                                over(eg[:, k % 2, i, :], 2), ALU.mult)
                        if i == 0:
                            ins.then_inc(dve_link.next(), 1)
                        else:
                            ins.then_inc(ge_done.sem, 1)
                decayed(0)
                for g in range(4 * (LEVELS + 1)):
                    pr, level, i = g // (2 * LEVELS + 2), g // 2 % (LEVELS + 1), g % 2
                    t = 2 * pr + i
                    if i == 0 and level < LEVELS and pr * LEVELS + level + 1 < 2 * LEVELS:
                        decayed(pr * LEVELS + level + 1)
                    dve.wait_ge(gs_done.sem, gs_done.at(1, l, g + 1))
                    if level >= 1 and not (pr == 0 and level == 1):
                        dve.wait_ge(ga_done.sem, ga_done.at(1, l, pr * 12 + (level - 1) * 2 + i + 1 - 2))
                    for e in range(2):
                        dst = sacc[:, t, e, :] if level == 0 else stmp[:, g % 2, e, :]
                        ins = dve.tensor_tensor(dst.rearrange("p (h n) -> p h n", h=2),
                                                SCORE[e][:, 0:256].rearrange("p (h n) -> p h n", h=2),
                                                over(gmasks[:, level, :], 2), ALU.mult)
                        if e == 0:
                            ins.then_inc(dve_link.next(), 1)
                        else:
                            ins.then_inc(gm_done.sem, 1)
                for t in range(TT):
                    dve.wait_ge(go_done.sem, go_done.at(1, l, t + 1))
                    dve.tensor_copy(og[:, t, :, :], OUTB[t % 2][:, :].rearrange("p (h v) -> p h v", h=G_H))\
                       .then_inc(go_copied.sem, 1)
                    dve.wait_ge(go_copied.sem, go_copied.at(1, l, t + 1))
                    for e in range(2):
                        half = og[:, t, :, :].rearrange("p (h e) v -> p h e v", e=2)[:, :, e, :]
                        ins = dve.tensor_tensor(half, half, PAST[t % 2][e][:, 0:256].rearrange("p (h v) -> p h v", h=2), ALU.add)
                        if e == 0:
                            ins.then_inc(dve_link.next(), 1)
                        else:
                            ins.then_inc(go_free.sem, 1)
                    dve.wait_ge(go_free.sem, go_free.at(1, l, t + 1))
                    dve.wait_ge(dve_link.sem, dve_link.now(1, l))
                    dve.tensor_tensor(osq, og[:, t, :, :], og[:, t, :, :], ALU.mult).then_inc(dve_link.next(), 1)
                    dve.wait_ge(dve_link.sem, dve_link.now(1, l))
                    dve.tensor_reduce(ss[:, t * G_H:(t + 1) * G_H], osq, AX.X, ALU.add).then_inc(dve_link.next(), 1)
                rsqrt(1, l, TT * G_H, G_DV)
                for t in range(TT):
                    r_ = rs[:, t * G_H:(t + 1) * G_H].unsqueeze(2).broadcast_to([P, G_H, G_DV])
                    dve.tensor_tensor(og[:, t, :, :], og[:, t, :, :], r_, ALU.mult).then_inc(dve_link.next(), 1)
                dve.wait_ge(dve_link.sem, dve_link.now(1, l))
                for t in range(TT):
                    dve.tensor_tensor(og[:, t, :, :], og[:, t, :, :], over(gla_g, G_H), ALU.mult).then_inc(dve_link.next(), 1)
                dve.wait_ge(dve_link.sem, dve_link.now(1, l))
                for t in range(TT):
                    y = Y[:, t, Y_C:DM].rearrange("p (h v) -> p h v", h=G_H)
                    if t == TT - 1:
                        dve.wait_ge(dve_link.sem, dve_link.now(1, l))
                        dve.tensor_tensor(y, y, og[:, t, :, :], ALU.mult).then_inc(prep.sem, 1)
                    else:
                        dve.tensor_tensor(y, y, og[:, t, :, :], ALU.mult).then_inc(dve_link.next(), 1)

            with dve.Fori(0, 2) as l:
                dve_link.made = 0
                for j in range(LEAD):
                    split_lo(1, l, 0, j)
                dve.wait_ge(job_done.sem, job_done.at(1, l, 1))
                dve.tensor_copy(cols[:, 0:88], JOB[0][:, 0:88]).then_inc(job_ev.sem, 1)
                dve.wait_ge(job_ev.sem, job_ev.at(1, l, 1))
                dve.tensor_tensor(cols[:, 32:48], cols[:, 32:48], cols[:, 64:80], ALU.add).then_inc(dve_link.next(), 1)
                dve.tensor_tensor(cols[:, 16:32], cols[:, 16:32], cols[:, 48:64], ALU.add).then_inc(dve_link.next(), 1)
                dve.tensor_scalar(bias_c[:, :], cols[:, 80:88], 0.5, None, ALU.mult).then_inc(dve_link.next(), 1)
                dve.wait_ge(dve_link.sem, dve_link.now(1, l))
                dve.scalar_tensor_tensor(out=cols[:, 0:16], in0=cols[:, 32:48], scalar=1.0, in1=cols[:, 0:16],
                                         op0=ALU.add, op1=ALU.mult).then_inc(dve_link.next(), 1)
                normalise(1, l)
                for k in range(KC):
                    dve.wait_ge(xp_hi.sem, xp_hi.at(1, l, k + 1))
                    dve.tensor_copy(act_hi[:, k, :], turn_tmp[:, k % 2, :]).then_inc(dve_link.next(), 1)
                    dve.wait_ge(dve_link.sem, dve_link.now(1, l))
                    dve.tensor_tensor(act_lo[:, k, :], turn_tmp[:, k % 2, :], act_hi[:, k, :].bitcast(F32), ALU.subtract)\
                       .then_inc(xp_free.sem, 1)
                with dve.Fori(0, 2) as p:
                    panel(1, l, p, take_copy(lambda t, p: zone[:, bass.ds(ZQ + t * 1024 + p * PW, PW)], blk=1))
                panel(1, l, 2, take_copy(lambda t, p: kv_s[:, t, :], blk=1))
                dve.wait_ge(x_saved.sem, x_saved.at(1, l, 0))
                panel(1, l, 3, take_gate(lambda p: 0, lambda p: 0, 1), between=lambda j: swa_rope(l) if j == 4 else None)
                with dve.Fori(4, 7) as p:
                    panel(1, l, p, take_gate(lambda p: (p - 3) * PW, lambda p: p - 3, 1))
                j0 = BR_S["j0"]
                dve.wait_ge(sink_in.sem, sink_in.at(1, l, 16))
                for n, jb in enumerate(JOBS_SK + JOBS_SQ[0:1]):
                    take_job(1, l, j0 + n, jb)

                def next_queries2(h):
                    if h + 1 < S_H:
                        take_job(1, l, j0 + 5 + h, JOBS_SQ[h + 1])
                attention(1, l, BR_S, next_queries2)
                with dve.Fori(7, 9) as p:
                    panel(1, l, p, take_copy(lambda t, p: zone[:, bass.ds(ZQ + (p - 7) * 2048 + t * PW, PW)], blk=1))
                panel(1, l, 9, take_copy(lambda t, p: view(ZV, TT, PW)[:, t, :], blk=1), between=gelu_between(l))
                panel(1, l, 10, take_copy(lambda t, p: vv_g[:, t, :], blk=1), next_width=G_RANK, between=norm_between(l))
                panel(1, l, 11, take_copy(lambda t, p: cg[:, t, :], G_RANK, blk=1), width=G_RANK)
                for t in range(TT):
                    dve.wait_ge(lin_free[t].sem, lin_free[t].at(1, l, NIN))
                dve.wait_ge(gla_in.sem, gla_in.at(1, l, 32))
                spatial(l)
                gla(l)
                turned_lo(1, l, KC, 0.5)
                out_panel(1, l, NIN, True)

                def gate_bias(j):
                    if j == 6:
                        dve.wait_ge(end_in.sem, end_in.at(1, l, 48))
                        dve.tensor_tensor(view(ZT, DM), view(ZT, DM), view(ZV, DM), ALU.add).then_inc(prep.sem, 1)
                out_panel(1, l, NIN + 1, True, gate_bias)
                out_panel(1, l, NIN + 2, True)
                out_panel(1, l, NP - 1, False)
                residual(1, l)
                assert dve_link.made == DVE_LINKS2, dve_link.made

        @block.gpsimd
        def _(pool):
            pool.sem_inc(mod_used.sem, mod_used.credit)
            pool.memset(ident[:, :], 0.0).then_inc(boot_pool, 1)
            pool.memset(ones[:, :], 1.0).then_inc(boot_pool, 1)
            pool.memset(view(0, RPB_P + 1), 0.0).then_inc(boot_pool, 4)
            pool.wait_ge(boot_pool, 6)
            pool.affine_select(out=ident[:, :], in_=ident[:, :], compare_op=ALU.not_equal, fill=1.0,
                               base=0, pattern=[[-1, P]], channel_multiplier=1).then_inc(boot_pool, 1)
            pool.wait_ge(boot_dve, 2)

            def mod_panel(l, p):
                for k in range(KC):
                    m = p * KC + k
                    pool.wait_ge(mod_landed[k % 2].sem, mod_landed[k % 2].at(0, l, 16 * (p * (KC // 2) + k // 2 + 1)))
                    if k == 0:
                        pool.wait_ge(mod_sum.sem, mod_sum.at(0, l, p))
                    apart(pool)
                    pool.tensor_scalar(mprod[:, :], wmod[:, k % 2, :], csil[:, k:k + 1], 0.0, ALU.mult, ALU.add)\
                        .then_inc(mod_used.sem, 1)
                    pool.wait_ge(mod_used.sem, mod_used.at(0, l, m + 1))
                    apart(pool)
                    if k == 0:
                        pool.tensor_copy(macc[:, :], mprod[:, :]).then_inc(mod_added.sem, 1)
                    else:
                        pool.tensor_tensor(macc[:, :], macc[:, :], mprod[:, :], ALU.add).then_inc(mod_added.sem, 1)
                    pool.wait_ge(mod_added.sem, mod_added.at(0, l, m + 1))

            with pool.Fori(0, 2) as l:
                with pool.Fori(0, NIN) as p:
                    mod_panel(l, p)
            with pool.Fori(0, 2) as l:
                for g in range(4 * (LEVELS + 1)):
                    pr, level, i = g // (2 * LEVELS + 2), g // 2 % (LEVELS + 1), g % 2
                    if level == 0:
                        continue
                    n = pr * 12 + (level - 1) * 2 + i
                    pool.wait_ge(gm_done.sem, gm_done.at(1, l, g + 1))
                    if n >= 2:
                        pool.wait_ge(ga_done.sem, ga_done.at(1, l, n - 1))
                    acc = sacc[:, 2 * pr + i, :, :]
                    pool.tensor_tensor(acc, acc, stmp[:, g % 2, :, :], ALU.add).then_inc(ga_done.sem, 1)


INPUTS = ["x", "norm_pre", "norm_post", "w_in", "a_q_norm", "a_k_norm", "b_q_norm", "b_kv_norm", "b_w_uq", "b_w_ukv",
          "c_rpb", "w_out", "c_2", "positions_2", "w_mod_2", "b_mod_2", "g_pre_2", "g_post_2", "w_in_2", "w_out_2",
          "swa_sinks_2", "sg_w_2", "sg_b_2", "sg_ln_g_2", "sg_ln_b_2", "gla_w_gate_up_2", "gla_b_gate_2",
          "gla_norm_g_2"]


def kernel(**inputs):
    import concourse.bacc as bacc
    from concourse.bass_utils import run_bass_kernel_spmd

    nc = bacc.Bacc("TRN2", target_bir_lowering=False, num_devices=1)
    rope_a, rope_b, near = tables()
    arrays = {name: np.ascontiguousarray(inputs[name]) for name in INPUTS}
    band, freq, sums, masks = tables_2()
    arrays |= {"rope_a": rope_a, "rope_b": rope_b, "near_mask": near, "band": band, "freq": freq,
               "gla_sums": sums, "gla_masks": masks}
    io = {name: nc.dram_tensor(f"in_{name}", a.shape, mybir.dt.from_np(a.dtype), kind="ExternalInput").ap()
          for name, a in arrays.items()}
    io["out"] = nc.dram_tensor("out_0", (1, SEQ, DM), F32, kind="ExternalOutput").ap()
    build(nc, io)
    r = run_bass_kernel_spmd(nc, [{f"in_{name}": a for name, a in arrays.items()}], core_ids=[0])
    return r.results[0]["out_0"]
```

```python
from contextlib import ExitStack

import numpy as np

import concourse.bass as bass
from concourse import mybir

F32 = mybir.dt.float32
F32R = mybir.dt.float32r
I32 = mybir.dt.int32
ALU = mybir.AluOpType
ACT = mybir.ActivationFunctionType
AX = mybir.AxisListType

P = 128
SEQ = 512
TT = SEQ // P
DM = 2048
KC = DM // P
PW = 512
ND = KC // 2
RS, RH = 2, 4
NOUT = DM // PW
NIN, NIN2 = 12, 11
NINS = NIN, NIN2
NP, NP2 = NIN + NOUT, NIN2 + NOUT
EPS = 1e-6
HD = 128
A_H, A_KV, B_H, C_H = 8, 2, 4, 4
B_Q, B_KV, B_NOPE, B_ROPE, B_V = 512, 256, 128, 64, 128
GRID_W = 64
DIN1 = 5952
A_Q0, B_CQ0, B_CKV0, B_G0, C_Q0 = 0, 2560, 3072, 3392, 3904
B_CKV_W = B_KV + B_ROPE
LEAD = 2
DVE_LINKS1, DVE_LINKS2 = 236, 334
SC_A, SC_B, SC_C = HD ** -0.5, (B_NOPE + B_ROPE) ** -0.5, HD ** -0.5
Y_B, Y_C = 1024, 1536
UNITS = 64
RPB_R, RPB_C = 15, 31
RPB_P = 2 * GRID_W - 1
GM = 14
MASKED = -1e30
S_H, S_KV, S_D, ROT = 16, 4, 64, 16
S_SC = S_D ** -0.5
SG_G, SG_C = 8, 64
G_H, G_DK, G_DV, G_RANK, CHUNK = 4, 64, 128, 16, 64
LEVELS = 6
CUM, TAIL = LEVELS, LEVELS + 1
SU0, CG0, Z0 = 1536, 3584, 3600
GELU_A, GELU_B = 0.044715, 0.7978845608028654


class Count:

    def __init__(self, sem, per, credit=0):
        self.sem, self.per, self.credit = sem, per, credit
        self.made = 0

    def at(self, blk, l, n):
        return l * self.per[blk] + (self.credit + n + (2 * self.per[0] if blk else 0))

    def next(self):
        self.made += 1
        return self.sem

    def now(self, blk, l):
        return self.at(blk, l, self.made)


def tables():
    t = np.arange(SEQ)
    row, col = t // GRID_W, t % GRID_W

    def axial(width):
        n = width // 2
        inv = (np.float32(1.0) / (np.float32(10000.0) ** (np.arange(0, n, 2, dtype=np.float32) / np.float32(n)))).astype(np.float32)
        cs, sn = [], []
        for pos in (row, col):
            ang = (pos.astype(np.float32)[:, None] * inv[None, :]).astype(np.float32)
            c, s = np.cos(ang).astype(np.float32), np.sin(ang).astype(np.float32)
            cs += [c, c]
            sn += [-s, s]
        out = np.stack([np.concatenate(cs, 1), np.concatenate(sn, 1)])
        return np.ascontiguousarray(out.reshape(2, TT, P, width).transpose(2, 0, 1, 3))

    c = np.arange(GRID_W)
    c0 = np.clip(c - 8, 0, GRID_W - 16)
    kc = np.arange(GRID_W)
    near = (kc[None] >= c0[:, None]) & (kc[None] < c0[:, None] + 16)
    mask = np.where(near, 0.0, MASKED).astype(np.float32)
    return axial(HD), axial(B_ROPE), np.concatenate([mask, mask], 0)


def tables_2():
    i = np.arange(P)
    j = np.arange(2 * P)
    dist = i[:, None] + P - j[None]
    band = np.where((dist >= 0) & (dist < P), 0.0, -MASKED)
    band = band.astype(np.float32)
    inv = (np.float32(500000.0) ** (-(np.arange(ROT // 2, dtype=np.float32) * np.float32(2.0 / ROT)))).astype(np.float32)
    u, t = i[:, None], i[None, :]
    same = u // CHUNK == t // CHUNK
    sums = np.zeros((P, LEVELS + 2, P), np.float32)
    masks = np.zeros((P, LEVELS + 2, P), np.float32)
    for n in range(LEVELS):
        half = CHUNK >> (n + 1)
        m = t // (2 * half) * (2 * half) + half - 1
        sums[:, n, :] = ((u > m) & (u <= t)) | ((u > t) & (u <= m))
        masks[:, n, :] = (u // (2 * half) == t // (2 * half)) & (u // half % 2 == 0) & (t // half % 2 == 1)
    sums[:, CUM, :] = same & (u <= t)
    sums[:, TAIL, :] = same & (u > t)
    masks[:, LEVELS, :] = u == t
    masks[:, LEVELS + 1, :] = u <= t
    sums /= 16.0
    return band, inv, sums, masks


def build(nc, io, only_first=False):
    with ExitStack() as ctx:
        base = -(-nc.sbuf_base // 64) * 64
        arena_bytes = 212800 // 64 * 64 - 64
        assert base + arena_bytes <= nc.sbuf_usable_end
        place = [base]
        sb_at = {}

        def sb(name, shape, dt=F32, at=None):
            size = int(np.prod(shape[1:])) * 4
            offset = place[0] if at is None else at
            t = nc.alloc_sbuf_tensor_at(name, shape, dt, offset=offset, align_bytes=4)
            if at is None:
                sb_at[name] = offset
                place[0] += size
                assert place[0] <= base + arena_bytes, (name, place[0] - base)
            return t

        ht_at = place[0]
        act_hi = sb("act_hi", [P, KC, SEQ], F32R)
        act_lo = sb("act_lo", [P, KC, SEQ], F32R)
        late = sb("late", [P, 2 * KC * SEQ], at=ht_at)
        Y = sb("Y", [P, TT, DM])
        stage = sb("stage", [P, RS, 2, PW])
        whi = sb("whi", [P, RH, 2, PW], F32R)
        wlo = sb("wlo", [P, RH, 2, PW], F32R)
        zone_at = place[0]
        zone = sb("zone", [P, 14336])
        wmod = sb("wmod", [P, 2, PW])
        mprod = sb("mprod", [P, PW])
        macc = sb("macc", [P, PW])
        mrow = sb("mrow", [1, PW])
        ident = sb("ident", [P, P])
        gmask = sb("gmask", [P, GRID_W])
        rows = sb("rows", [P, P])
        cols = sb("cols", [P, 96])
        csil = sb("csil", [P, KC])
        ctmp = sb("ctmp", [P, KC])
        ones = sb("ones", [P, 2])
        ss = sb("ss", [P, 64])
        rs = sb("rs", [P, 64])
        nv = sb("nv", [P, 3, 64])
        rsq = sb("rsq", [P, TT, A_H])
        nmx = sb("nmx", [P, 4, 2])
        sm = sb("sm", [P, 4])
        ri = sb("ri", [P, 4, 2])

        wmod_at = sb_at["wmod"]
        band = sb("band", [P, 2 * P], at=wmod_at)
        sinks = sb("sinks", [P, S_H], at=wmod_at + 1024)
        rot = sb("rot", [P, 2, TT, ROT // 2], at=wmod_at + 1088)
        rtmp = sb("rtmp", [P, 6, TT, ROT // 2], at=wmod_at + 1344)
        pos_i = sb("pos_i", [P, TT], I32, at=wmod_at + 2112)
        pos_f = sb("pos_f", [P, TT], at=wmod_at + 2128)
        freq = sb("freq", [P, ROT // 2], at=wmod_at + 2144)
        bias_c = sb("bias_c", [P, SG_G], at=wmod_at + 2176)
        bnst = sb("bnst", [P, TT, 6], at=wmod_at + 2208)
        mv = sb("mv", [P, TT, 2], at=wmod_at + 2304)
        decay = sb("decay", [P, 2, 8], at=wmod_at + 2336)
        es = sb("es", [P, 4], at=wmod_at + 2400)
        cgw = sb("cgw", [P, KC, G_RANK], at=wmod_at + 2432)
        cgw_hi = sb("cgw_hi", [P, KC, G_RANK], F32R, at=sb_at["mprod"])
        cgw_lo = sb("cgw_lo", [P, KC, G_RANK], F32R, at=sb_at["mprod"] + 4 * KC * G_RANK)
        den = sb("den", [P, 4], at=wmod_at + 2416)

        PP, ZQ, ZT, ZK, ZV = 0, 4096, 8192, 10240, 12288

        def view(first, *shape, of=zone):
            size = int(np.prod(shape))
            names = "abcd"[:len(shape)]
            v = of[:, first:first + size]
            if len(shape) == 1:
                return v
            return v.rearrange(f"p ({' '.join(names)}) -> p {' '.join(names)}",
                               **{n: s for n, s in zip(names, shape)})

        xs = view(0, TT, DM)
        probs = view(PP, 4, SEQ)
        probsT = view(PP + 2048, 4, SEQ)
        tanh_tmp = view(ZT, 2, PW)
        rpb_pad = view(ZV, RPB_P)

        bank = [ctx.enter_context(nc.psum_tensor(f"bank{i}", [P, 512], F32)) for i in range(8)]
        LIN, JOB, OUTB, SCORE, TURN = bank[0:4], bank[0:2], bank[2:4], bank[4:6], bank[6:8]
        PAST = [bank[0:2], bank[6:8]]
        LEVEL = [bank[4:6], bank[0:2]]
        XP = bank[4:8]
        MSUM = bank[7]

        rpb_dram = nc.dram_tensor("rpb_pad", (2 * C_H * RPB_R, RPB_P), F32, kind="Internal").ap()
        g_dram = nc.dram_tensor("rpb_tiles", (2, P, C_H, GM, GRID_W), F32, kind="Internal").ap()
        mod_dram = nc.dram_tensor("mod_rows", (2, 3 * DM), F32, kind="Internal").ap()
        x_dram = io["out"].rearrange("o (t p) d -> p (o t) d", p=P)
        x_in = io["x"].rearrange("o (t p) d -> p (o t) d", p=P)

        def sem(name):
            return ctx.enter_context(nc.semaphore(name))

        def count(name, per1, per2=None, credit=0):
            return Count(sem(name), (per1, per1 if per2 is None else per2), credit)

        boot_dma = sem("boot_dma")
        boot_rpb = sem("boot_rpb")
        boot_x = [sem(f"boot_x{t}") for t in range(TT)]
        boot_pool = sem("boot_pool")
        boot_pe = sem("boot_pe")
        boot_dve = sem("boot_dve")
        boot_act = sem("boot_act")
        g_built = count("g_built", 16 * 2 * C_H)
        w_landed = [count(f"w_landed{s}", 16 * NP * ND // RS, 16 * NP2 * ND // RS) for s in range(RS)]
        hi_done = count("hi_done", NP * ND, NP2 * ND)
        lo_done = count("lo_done", NP * ND, NP2 * ND, credit=RS)
        w_used = count("w_used", NP * (ND - 1), NP2 * (ND - 1), credit=RH - 1)
        lin_done = count("lin_done", NP * TT, NP2 * TT, credit=1)
        lin_free = [count(f"lin_free{t}", NP, NP2, credit=1) for t in range(TT)]
        xp_done = count("xp_done", 2 * KC)
        xp_hi = count("xp_hi", 2 * KC)
        xp_free = count("xp_free", 2 * KC, credit=4)
        J1, J2 = 46, 39
        job_done = count("job_done", J1, J2)
        job_ev = count("job_ev", J1, J2, credit=2)
        score_done = count("score_done", UNITS)
        max_done = count("max_done", UNITS)
        exp_done = count("exp_done", UNITS, credit=2)
        turn_done = count("turn_done", UNITS, credit=4)
        pt_done = count("pt_done", UNITS, credit=2)
        pv_done = count("pv_done", UNITS, credit=4)
        fin_done = count("fin_done", UNITS, credit=2)
        sq_done = count("sq_done", TT + TT * NOUT, TT + TT * NOUT)
        tanh_done = count("tanh_done", 16, 16)
        prep = count("prep", 15, 18, credit=TT)
        XS_READY, A_READY, BTM_READY, QPE_READY = 0, 8, 9, 10
        XNEW = 11
        small_in = count("small_in", 16 * 3, 16 * 6)
        a_in = count("a_in", 16 * 3, 0)
        b_in = count("b_in", 16 * 3, 0)
        g_in = count("g_in", 16 * 2, 0)
        S_READY, SG_READY, LA_READY, QC_READY, Y_READY = 8, 9, 10, 11, 13
        XNEW2 = 14
        boot2_dma = sem("boot2_dma")
        angles_done = count("angles_done", 0, 1)
        rot_done = count("rot_done", 0, 2)
        sink_in = count("sink_in", 0, 16)
        sg_in = count("sg_in", 0, 16 * 6)
        gla_in = count("gla_in", 0, 16 * 2)
        gelu_act = count("gelu_act", 0, 4)
        gelu_dve = count("gelu_dve", 0, 4)
        cg_in = count("cg_in", 0, 16)
        cg_hi = count("cg_hi", 0, 1)
        cg_lo = count("cg_lo", 0, 1)
        soft_dve = count("soft_dve", 0, 1)
        soft_act = count("soft_act", 0, 2)
        ajob_done = count("ajob_done", 0, 17)
        ajob_ev = count("ajob_ev", 0, 17, credit=2)
        ge_done = count("ge_done", 0, 2 + 2 * LEVELS)
        gt_done = count("gt_done", 0, 28)
        gte_done = count("gte_done", 0, 28)
        gs_done = count("gs_done", 0, 28)
        gm_done = count("gm_done", 0, 28)
        ga_done = count("ga_done", 0, 24)
        go_done = count("go_done", 0, TT)
        go_free = count("go_free", 0, TT)
        go_copied = count("go_copied", 0, TT)
        end_in = count("end_in", 16, 16)
        gain_in = count("gain_in", 16, 16 * 3)
        x_saved = count("x_saved", 16 * TT)
        mod_landed = [count(f"mod_landed{s}", 16 * NIN * KC // 2, 0) for s in range(2)]
        mod_used = count("mod_used", NIN * KC, 0, credit=2)
        mod_added = count("mod_added", NIN * KC, 0)
        mod_sum = count("mod_sum", NIN, 0, credit=1)
        mod_ev = count("mod_ev", NIN, 0, credit=1)
        mod_row = count("mod_row", 16 * NIN, 0, credit=1)
        dve_link = count("dve_link", DVE_LINKS1, DVE_LINKS2)

        aside = {}

        def apart(eng):
            if eng not in aside:
                aside[eng] = sem(f"aside{len(aside)}")
            eng.sem_inc(aside[eng], 1)

        block = ctx.enter_context(nc.Block())

        qT_c, kT_c, v_c = view(ZT, C_H, SEQ), view(ZK, C_H, SEQ), view(ZV, TT, PW)
        g_c = view(ZQ, C_H, GM, GRID_W)
        q_a, kv_a = view(ZQ, TT, A_H * HD), view(ZV, TT, 2 * A_KV * HD)
        qT_a, kT_a = view(ZT, 4, SEQ), view(ZK, A_KV, SEQ)
        cq_b, ckv_b = view(ZQ, TT, B_Q), view(ZV, TT, B_CKV_W)
        wuq, wukv = view(PP, 4, 768), view(ZK, 2, 1024)
        cos_b = view(PP + 3072, TT, B_ROPE)
        sin_b = view(PP + 3072 + TT * B_ROPE, TT, B_ROPE)
        cqT, ckvT = view(0, 4, SEQ, of=late), view(2048, 2, SEQ, of=late)
        kpT = view(3072, SEQ, of=late)
        qnT, qpT = view(3584, B_H, SEQ, of=late), view(5632, B_H, SEQ, of=late)
        knT, v_b = view(7680, B_H, SEQ, of=late), view(9728, TT, SEQ, of=late)
        qpe = view(11776, TT, B_H * B_ROPE, of=late)
        late_tmp = view(12800, 2, 1024, of=late)

        def ring_free(p, j):
            if j == RH - 1:
                return lin_done, p * TT
            return w_used, p * (ND - 1) + (j - RH + 1 if j >= RH else j - RH + 2)

        def tok(t):
            return slice(t * P, (t + 1) * P)

        def scores_c(h, t):
            return [(qT_c[:, h, tok(t)], kT_c[:, h, :])]

        def scores_a(h, t):
            return [(qT_a[:, h % 4, tok(t)], kT_a[:, h // 4, :])]

        def scores_b(h, t):
            return [(qnT[:, h, tok(t)], knT[:, h, :]), (qpT[0:B_ROPE, h, tok(t)], kpT[0:B_ROPE, :])]

        BR_C = dict(name="C", first=0, heads=C_H, scores=scores_c, v=lambda h, kt: v_c[:, kt, h * HD:(h + 1) * HD],
                    y=Y_C, j0=1)
        BR_A = dict(name="A", first=16, heads=A_H, scores=scores_a,
                    v=lambda h, kt: kv_a[:, kt, (A_KV + h // 4) * HD:(A_KV + h // 4 + 1) * HD], y=0, j0=9)
        BR_B = dict(name="B", first=48, heads=B_H, scores=scores_b, v=lambda h, kt: v_b[:, kt, h * HD:(h + 1) * HD],
                    y=Y_B, j0=19)

        def turn_job(srcs, width, dst, scale=1.0):
            return ("turn", srcs, width, dst, scale)

        def mm_job(groups, n, dst, scale=1.0):
            return ("mm", groups, n, dst, scale)

        JOBS_C = [turn_job([view(PP + 2048, TT, PW)[:, t, h * HD:(h + 1) * HD] for t in range(TT)], P, kT_c[:, h, :])
                  for h in range(C_H)] + \
                 [turn_job([view(PP, TT, PW)[:, t, h * HD:(h + 1) * HD] for t in range(TT)], P, qT_c[:, h, :], -SC_C)
                  for h in range(C_H)]
        JOBS_AK = [turn_job([kv_a[:, t, h * HD:(h + 1) * HD] for t in range(TT)], P, kT_a[:, h, :])
                   for h in range(A_KV)]
        JOBS_AQ = [turn_job([q_a[:, t, h * HD:(h + 1) * HD] for t in range(TT)], P, qT_a[:, h % 4, :])
                   for h in range(A_H)]
        B_QC, B_KC = KC, KC + 4
        wuq_h = wuq.rearrange("p k (h e) -> p k h e", h=B_H)
        wukv_h = wukv.rearrange("p k (h e) -> p k h e", h=B_H)
        JOBS_B1 = [turn_job([cq_b[:, t, tok(r)] for t in range(TT)], P, cqT[:, r, :], cols[:, B_QC + r:B_QC + r + 1])
                   for r in range(4)] + \
                  [turn_job([ckv_b[:, t, tok(r)] for t in range(TT)], P, ckvT[:, r, :], cols[:, B_KC + r:B_KC + r + 1])
                   for r in range(2)] + \
                  [turn_job([ckv_b[:, t, B_KV:B_CKV_W] for t in range(TT)], B_ROPE, kpT[0:B_ROPE, :])]
        JOBS_B2 = [mm_job([(cqT[:, r, tok(t)], wuq_h[:, r, :, B_NOPE:]) for r in range(4)], B_H * B_ROPE,
                          qpe[:, t, :], SC_B) for t in range(TT)] + \
                  [mm_job([(wuq_h[:, r, h, 0:B_NOPE], cqT[:, r, :]) for r in range(4)], SEQ, qnT[:, h, :], SC_B)
                   for h in range(B_H)] + \
                  [mm_job([(wukv_h[:, r, h, 0:B_NOPE], ckvT[:, r, :]) for r in range(2)], SEQ, knT[:, h, :])
                   for h in range(B_H)] + \
                  [mm_job([(ckvT[:, r, tok(t)], wukv_h[:, r, :, B_NOPE:]) for r in range(2)], SEQ, v_b[:, t, :])
                   for t in range(TT)]
        JOBS_B3 = [turn_job([qpe[:, t, h * B_ROPE:(h + 1) * B_ROPE] for t in range(TT)], B_ROPE, qpT[0:B_ROPE, h, :])
                   for h in range(B_H)]
        assert 1 + len(JOBS_C + JOBS_AK + JOBS_AQ + JOBS_B1 + JOBS_B2 + JOBS_B3) == J1

        q_s, kv_s = view(ZQ, TT, S_H * S_D), view(ZV, TT, 2 * S_KV * S_D)
        qT_s, kT_s = view(ZT, 4, SEQ), view(ZK, S_KV, SEQ)

        def keys_of(n):
            return [n] if n == 0 else [n - 1, n]

        def scores_s(h, n):
            ks = keys_of(n)
            return [(qT_s[0:S_D, h % 4, tok(n)], kT_s[0:S_D, h // 4, ks[0] * P:(ks[-1] + 1) * P])]

        BR_S = dict(name="S", first=0, heads=S_H, scores=scores_s, y=0, j0=1, blk=1,
                    v=lambda h, kt: kv_s[:, kt, (S_KV + h // 4) * S_D:(S_KV + h // 4 + 1) * S_D])

        def tiles_of(br, i):
            return keys_of(i % 4) if br["name"] == "S" else list(range(TT))

        def dv_of(br):
            return S_D if br["name"] == "S" else HD

        JOBS_SK = [turn_job([kv_s[:, t, g * S_D:(g + 1) * S_D] for t in range(TT)], S_D, kT_s[0:S_D, g, :])
                   for g in range(S_KV)]
        JOBS_SQ = [turn_job([q_s[:, t, h * S_D:(h + 1) * S_D] for t in range(TT)], S_D, qT_s[0:S_D, h % 4, :], -S_SC)
                   for h in range(S_H)]
        u_g, v_g = view(ZQ, TT, PW), view(ZQ + 2048, TT, PW)
        sg_wt, sg_wT = view(PP, SG_G, P), view(PP + 1024, SG_G, P)
        ln_g, ln_b = view(PP + 2048, PW), view(PP + 2560, PW)
        gelu_tmp = view(ZT, TT * PW)
        qk_g, vv_g = view(ZV, TT, 2, G_H * G_DK), view(ZK, TT, G_H * G_DV)
        gate_w, gate_b, gla_g = view(PP + 3136, 256), view(PP + 3392, 256), view(PP + 3648, G_DV)
        gsum, gmasks = view(ZT, LEVELS + 2, P), view(ZT + 1024, LEVELS + 2, P)
        cgT = view(0, SEQ, of=late)
        lg, la = view(512, TT * 256, of=late), view(1536, TT, 256, of=late)
        soft = view(2560, TT * 256, of=late)
        eg = view(3584, 2, 2, 256, of=late)
        qke = late[:, 4608:6656].rearrange(
            "p (r t w n) -> p r t w n", r=2, t=2, w=2)
        qkT = view(6656, 2, 4, P, of=late)
        sacc = view(7680, TT, 2, 2 * P, of=late)
        stmp = view(9728, 2, 2, 2 * P, of=late)
        kt_g, qc_g = view(10752, TT, 256, of=late), view(11776, TT, 256, of=late)
        qcT = view(12800, TT, 2, P, of=late)
        state = view(13824, 8, 2, P, of=late)
        og = view(ZQ, TT, G_H, G_DV)
        osq = view(ZQ + 2048, G_H, G_DV)
        turn_tmp = view(ZT, 2, SEQ)

        JOB_CG = mm_job([(w, x) for k in range(KC) for w, x in
                         ((cgw_hi[:, k, :], act_lo[:, k, :]), (cgw_hi[:, k, :], act_hi[:, k, :]),
                          (cgw_lo[:, k, :], act_hi[:, k, :]))], SEQ, cgT[0:G_RANK, :])
        JOBS_QC = [turn_job([qc_g[:, 2 * pr + i, tok(hp)] for i in range(2) for hp in range(2)], P,
                            qcT[:, 2 * pr:2 * pr + 2, :, :].rearrange("p t h n -> p (t h n)")) for pr in range(2)]

        @block.sync
        def _(sp):
            def double(blk, l, p, j, w, col, width=PW):
                sp.wait_ge(lo_done.sem, lo_done.at(blk, l, p * ND + j + 1 - RS))
                apart(sp)
                src = w[bass.ds(l, 1), 2 * j * P:(2 * j + 2) * P, bass.ds(col, width)]
                sp.dma_start(stage[:, j % RS, :, 0:width], src.rearrange("o (a p) n -> p (o a) n", p=P))\
                  .then_inc(w_landed[j % RS].sem, 16)

            def mod_double(l, p, j):
                for k in (2 * j, 2 * j + 1):
                    sp.wait_ge(mod_used.sem, mod_used.at(0, l, p * KC + k + 1 - 2))
                    apart(sp)
                    src = io["w_mod_2"][bass.ds(l, 1), k * P:(k + 1) * P, bass.ds(p * PW, PW)]
                    sp.dma_start(wmod[:, k % 2, :], src.rearrange("o p n -> (o p) n"))\
                      .then_inc(mod_landed[k % 2].sem, 16)

            def in_panel(l, p, col, width=PW):
                for j in range(ND):
                    double(0, l, p, j, io["w_in"], col, width)
                    mod_double(l, p, j)

            def out_panel(blk, l, p, w, first=0, last=ND):
                for j in range(first, last):
                    double(blk, l, p, j, w, (p - NINS[blk]) * PW)

            def spread(dst, src, landed):
                sp.dma_start(dst, src.broadcast_to([P, src.shape[-1]])).then_inc(landed.sem, 16)

            sp.dma_start(rows[0:KC, :], io["c_2"].rearrange("o (k p) -> (o k) p", p=P)).then_inc(boot_dma, 16)
            for t in range(TT):
                sp.dma_start(Y[:, t, :], x_in[:, t, :]).then_inc(boot_x[t], 16)
            sp.wait_ge(boot_pe, 1)

            with sp.Fori(0, 2) as l:
                sp.dma_start(rows[0:KC, :], io["norm_pre"][bass.ds(l, 1), :].rearrange("o (k p) -> (o k) p", p=P))\
                  .then_inc(small_in.sem, 16)
                sp.dma_start(rows[KC:KC + 4, :], io["b_q_norm"][bass.ds(l, 1), :].rearrange("o (k p) -> (o k) p", p=P))\
                  .then_inc(small_in.sem, 16)
                sp.dma_start(rows[KC + 4:KC + 6, :], io["b_kv_norm"][bass.ds(l, 1), :].rearrange("o (k p) -> (o k) p", p=P))\
                  .then_inc(small_in.sem, 16)
                with sp.Fori(0, 2) as p:
                    in_panel(l, p, C_Q0 + p * PW)
                sp.wait_ge(xp_done.sem, xp_done.at(0, l, KC))
                apart(sp)
                sp.wait_ge(g_built.sem, g_built.at(0, l, 16 * 2 * C_H))
                apart(sp)
                sp.dma_start(gmask[:, :], io["near_mask"]).then_inc(g_in.sem, 16)
                sp.dma_start(view(ZQ, C_H * GM * GRID_W),
                             g_dram[bass.ds(l, 1)].rearrange("o p h m k -> (o p) (h m k)")).then_inc(g_in.sem, 16)
                with sp.Fori(2, 4) as p:
                    in_panel(l, p, C_Q0 + p * PW)
                in_panel(l, 4, 0)
                sp.wait_ge(fin_done.sem, fin_done.at(0, l, 16))
                apart(sp)
                sp.dma_start(view(PP + 3072, 2 * TT * HD), io["rope_a"].rearrange("p a t d -> p (a t d)"))\
                  .then_inc(a_in.sem, 16)
                for n, name in enumerate(("a_q_norm", "a_k_norm")):
                    src = io[name][bass.ds(l, 1), :]
                    sp.dma_start(view(PP + 2560 + n * HD, HD), src.broadcast_to([P, HD])).then_inc(a_in.sem, 16)
                with sp.Fori(5, 9) as p:
                    in_panel(l, p, (p - 4) * PW)
                in_panel(l, 9, B_CQ0)
                sp.wait_ge(fin_done.sem, fin_done.at(0, l, 48))
                apart(sp)
                sp.dma_start(view(PP, 4, 768), io["b_w_uq"][bass.ds(l, 1)].rearrange("o (k p) n -> p (o k) n", p=P))\
                  .then_inc(b_in.sem, 16)
                sp.dma_start(view(ZK, 2, 1024), io["b_w_ukv"][bass.ds(l, 1)].rearrange("o (k p) n -> p (o k) n", p=P))\
                  .then_inc(b_in.sem, 16)
                sp.dma_start(view(PP + 3072, 2 * TT * B_ROPE), io["rope_b"].rearrange("p a t d -> p (a t d)"))\
                  .then_inc(b_in.sem, 16)
                in_panel(l, 10, B_CKV0, B_CKV_W)
                in_panel(l, 11, B_G0)
                out_panel(0, l, NIN, io["w_out"], 0, LEAD)
                sp.wait_ge(fin_done.sem, fin_done.at(0, l, UNITS))
                apart(sp)
                spread(view(ZT, DM), io["norm_post"][bass.ds(l, 1), :], gain_in)
                out_panel(0, l, NIN, io["w_out"], LEAD)
                sp.wait_ge(x_saved.sem, x_saved.at(0, l, 16 * TT))
                apart(sp)
                sp.dma_start(xs, x_dram).then_inc(end_in.sem, 16)
                with sp.Fori(NIN + 1, NP) as p:
                    out_panel(0, l, p, io["w_out"])

            sp.wait_ge(mod_row.sem, mod_row.at(0, 2, 0))
            apart(sp)
            sp.wait_ge(mod_added.sem, mod_added.at(0, 2, 0))
            apart(sp)
            sp.dma_start(band[:, :], io["band"]).then_inc(boot2_dma, 16)
            sp.dma_start(pos_i[:, :].rearrange("p (t o) -> p t o", o=1),
                         io["positions_2"].rearrange("o (t p) -> p t o", p=P),
                         allow_slow_non_contiguous=True).then_inc(boot2_dma, 16)
            sp.dma_start(freq[:, :], io["freq"].rearrange("(o f) -> o f", o=1).broadcast_to([P, ROT // 2]))\
              .then_inc(boot2_dma, 16)

            def rows_in(first, src):
                n = src.shape[-1] // P
                sp.dma_start(rows[first:first + n, :], src.rearrange("o (k p) -> (o k) p", p=P))\
                  .then_inc(small_in.sem, 16)

            with sp.Fori(0, 2) as l:
                one = bass.ds(l, 1)
                sp.wait_ge(job_ev.sem, job_ev.at(1, l, 0))
                apart(sp)
                rows_in(0, io["g_pre_2"][one, :])
                rows_in(16, mod_dram[one, 0:DM])
                rows_in(32, mod_dram[one, DM:2 * DM])
                rows_in(48, io["b_mod_2"][one, 0:DM])
                rows_in(64, io["b_mod_2"][one, DM:2 * DM])
                sp.dma_start(rows[80:80 + SG_G, :], io["sg_b_2"][one].rearrange("o g t -> (o g) t"))\
                  .then_inc(small_in.sem, 16)
                sp.wait_ge(fin_done.sem, fin_done.at(1, l, 0))
                apart(sp)
                spread(sinks[:, :], io["swa_sinks_2"][one, :], sink_in)
                sp.dma_start(cgw[:, :, :], io["w_in_2"][one, :, CG0:CG0 + G_RANK].rearrange("o (k p) n -> p (o k) n", p=P))\
                  .then_inc(cg_in.sem, 16)
                with sp.Fori(0, 3) as p:
                    for j in range(ND):
                        double(1, l, p, j, io["w_in_2"], p * PW)
                with sp.Fori(3, 7) as p:
                    for j in range(ND):
                        double(1, l, p, j, io["w_in_2"], (p - 3) * PW + Z0)
                for j in range(ND):
                    double(1, l, 7, j, io["w_in_2"], SU0)
                sp.wait_ge(fin_done.sem, fin_done.at(1, l, UNITS))
                apart(sp)
                sp.dma_start(sg_wt, io["sg_w_2"][one].rearrange("o g t s -> t (o g) s")).then_inc(sg_in.sem, 16)
                spread(ln_g, io["sg_ln_g_2"][one, :], sg_in)
                spread(ln_b, io["sg_ln_b_2"][one, :], sg_in)
                sp.dma_start(gate_w[0:G_RANK, :], io["gla_w_gate_up_2"][one].rearrange("o r n -> (o r) n"))\
                  .then_inc(sg_in.sem, 16)
                spread(gate_b, io["gla_b_gate_2"][one, :], sg_in)
                spread(gla_g, io["gla_norm_g_2"][one, :], sg_in)
                with sp.Fori(8, 11) as p:
                    for j in range(ND):
                        double(1, l, p, j, io["w_in_2"], (p - 7) * PW + SU0)
                sp.wait_ge(prep.sem, prep.at(1, l, SG_READY + 1))
                apart(sp)
                sp.dma_start(gsum, io["gla_sums"]).then_inc(gla_in.sem, 16)
                sp.dma_start(gmasks, io["gla_masks"]).then_inc(gla_in.sem, 16)
                out_panel(1, l, NIN2, io["w_out_2"], 0, LEAD)
                sp.wait_ge(prep.sem, prep.at(1, l, Y_READY + 1))
                apart(sp)
                spread(view(ZT, DM), mod_dram[one, 2 * DM:3 * DM], gain_in)
                spread(view(ZV, DM), io["b_mod_2"][one, 2 * DM:3 * DM], gain_in)
                spread(view(ZK, DM), io["g_post_2"][one, :], gain_in)
                out_panel(1, l, NIN2, io["w_out_2"], LEAD)
                sp.wait_ge(x_saved.sem, x_saved.at(1, l, 16 * TT))
                apart(sp)
                sp.dma_start(xs, x_dram).then_inc(end_in.sem, 16)
                with sp.Fori(NIN2 + 1, NP2) as p:
                    out_panel(1, l, p, io["w_out_2"])
            sp.wait_ge(x_saved.sem, x_saved.at(1, 2, 16 * TT))
            apart(sp)

        @block.tensor
        def _(pe):
            def panel(blk, l, p, width=PW, src=None, n0=0):
                if src is not None:
                    for k in range(4):
                        turns(blk, l, n0, k, src)
                for j in range(ND):
                    pe.wait_ge(lo_done.sem, lo_done.at(blk, l, p * ND + j + 1))
                    for a in range(2):
                        k = 2 * j + a
                        hi_w, lo_w = whi[:, j % RH, a, 0:width], wlo[:, j % RH, a, 0:width]
                        if src is not None:
                            pe.wait_ge(xp_free.sem, xp_free.at(blk, l, n0 + k + 1))
                            if k + 4 < KC:
                                turns(blk, l, n0, k + 4, src)
                        for t in range(TT):
                            if k == 0:
                                pe.wait_ge(lin_free[t].sem, lin_free[t].at(blk, l, p))
                            out = LIN[t][:, 0:width]
                            hi_x, lo_x = act_hi[:, k, tok(t)], act_lo[:, k, tok(t)]
                            pe.matmul(out, hi_x, lo_w, start=(k == 0), stop=False)
                            pe.matmul(out, hi_x, hi_w, start=False, stop=False)
                            mm = pe.matmul(out, lo_x, hi_w, start=False, stop=(k == KC - 1))
                            if k == KC - 1:
                                mm.then_inc(lin_done.sem, 1)
                    if j < ND - 1:
                        mm.then_inc(w_used.sem, 1)

            def turns(blk, l, n0, k, src):
                if src is xs and k % (KC // 2) == 0:
                    pe.wait_ge(prep.sem, prep.at(blk, l, XS_READY + (2 * k // KC + 1) * TT))
                pe.wait_ge(xp_free.sem, xp_free.at(blk, l, n0 + k + 1 - 4))
                for t in range(TT):
                    tr = pe.transpose(XP[k % 4][:, tok(t)], src[:, t, tok(k)], ident[:, :])
                tr.then_inc(xp_done.sem, 1)

            def job(blk, l, n, jb):
                kind, parts, width, dst, scale = jb
                pe.wait_ge(job_ev.sem, job_ev.at(blk, l, n + 1 - 2))
                apart(pe)
                if kind == "turn":
                    for t, src in enumerate(parts):
                        mm = pe.transpose(JOB[n % 2][0:width, t * src.shape[0]:(t + 1) * src.shape[0]], src,
                                          ident[0:src.shape[0], 0:src.shape[0]])
                else:
                    for r, (lhs, rhs) in enumerate(parts):
                        mm = pe.matmul(JOB[n % 2][0:lhs.shape[-1], 0:width], lhs, rhs, start=(r == 0), stop=(r == len(parts) - 1))
                mm.then_inc(job_done.sem, 1)

            def score(blk, l, br, i):
                u = br["first"] + i
                pe.wait_ge(exp_done.sem, exp_done.at(blk, l, u + 1 - 2))
                parts = br["scores"](i // 4, i % 4)
                for r, (lhs, rhs) in enumerate(parts):
                    mm = pe.matmul(SCORE[u % 2][:, 0:P * len(tiles_of(br, i))], lhs, rhs, start=(r == 0),
                                   stop=(r == len(parts) - 1))
                mm.then_inc(score_done.sem, 1)

            def turn(blk, l, br, i):
                u = br["first"] + i
                pe.wait_ge(exp_done.sem, exp_done.at(blk, l, u + 1))
                pe.wait_ge(pt_done.sem, pt_done.at(blk, l, u + 1 - 2))
                for kt in range(len(tiles_of(br, i))):
                    mm = pe.transpose(TURN[u % 2][:, tok(kt)], probs[:, u % 4, tok(kt)], ident[:, :])
                mm.then_inc(turn_done.sem, 1)

            def pv(blk, l, br, i):
                u = br["first"] + i
                pe.wait_ge(pt_done.sem, pt_done.at(blk, l, u + 1))
                pe.wait_ge(fin_done.sem, fin_done.at(blk, l, u + 1 - 2))
                tiles = tiles_of(br, i)
                for n, kt in enumerate(tiles):
                    mm = pe.matmul(OUTB[u % 2][:, 0:dv_of(br)], probsT[:, u % 4, tok(n)], br["v"](i // 4, kt),
                                   start=(n == 0), stop=(n == len(tiles) - 1))
                mm.then_inc(pv_done.sem, 1)

            def attention(blk, l, br, early=None):
                n = 4 * br["heads"]
                for i in range(n + 3):
                    if early and i % 4 == 0 and i < n:
                        early(i // 4)
                    if i < n:
                        score(blk, l, br, i)
                    if 2 <= i < n + 2:
                        turn(blk, l, br, i - 2)
                    if i >= 3:
                        pv(blk, l, br, i - 3)
                pe.wait_ge(fin_done.sem, fin_done.at(blk, l, br["first"] + n))

            def mod_row_sum(l, p):
                pe.wait_ge(mod_added.sem, mod_added.at(0, l, (p + 1) * KC))
                pe.wait_ge(mod_ev.sem, mod_ev.at(0, l, p))
                pe.matmul(MSUM[0:1, :], ones[:, 0:1], macc[:, :], start=True, stop=True).then_inc(mod_sum.sem, 1)

            def in_panel(l, p, width=PW, **kw):
                panel(0, l, p, width, **kw)
                mod_row_sum(l, p)

            def banks_free(l, panels, blk=0):
                for t in range(TT):
                    pe.wait_ge(lin_free[t].sem, lin_free[t].at(blk, l, panels))

            pe.sem_inc(w_used.sem, w_used.credit)
            pe.sem_inc(mod_sum.sem, mod_sum.credit)
            pe.sem_inc(lin_done.sem, lin_done.credit)
            pe.sem_inc(turn_done.sem, turn_done.credit)
            pe.sem_inc(pv_done.sem, pv_done.credit)
            pe.wait_ge(boot_pool, 4)
            pe.wait_ge(boot_dma, 16)
            pe.transpose(JOB[0][:, 0:KC], rows[0:KC, :], ident[0:KC, 0:KC]).then_inc(boot_pe, 1)
            pe.wait_ge(boot_dve, 1)
            with pe.Fori(0, 2) as l:
                pe.wait_ge(small_in.sem, small_in.at(0, l, 48))
                pe.wait_ge(lin_free[0].sem, lin_free[0].at(0, l, 0))
                job(0, l, 0, turn_job([rows[0:KC + 6, :]], P, None))
                pe.wait_ge(job_ev.sem, job_ev.at(0, l, 1))
                in_panel(l, 0, src=xs)
                apart(pe)
                with pe.Fori(1, 4) as p:
                    in_panel(l, p)
                banks_free(l, 4)
                pe.wait_ge(mod_ev.sem, mod_ev.at(0, l, 4))
                for n, jb in enumerate(JOBS_C):
                    job(0, l, BR_C["j0"] + n, jb)
                pe.wait_ge(job_ev.sem, job_ev.at(0, l, BR_C["j0"] + 8))
                attention(0, l, BR_C)
                apart(pe)
                with pe.Fori(4, 9) as p:
                    in_panel(l, p)
                banks_free(l, 9)
                pe.wait_ge(mod_ev.sem, mod_ev.at(0, l, 9))
                pe.wait_ge(prep.sem, prep.at(0, l, A_READY + 1))
                j0 = BR_A["j0"]
                for n, jb in enumerate(JOBS_AK + JOBS_AQ[0:1]):
                    job(0, l, j0 + n, jb)

                def next_queries(h):
                    if h + 1 < A_H:
                        job(0, l, j0 + 3 + h, JOBS_AQ[h + 1])
                    pe.wait_ge(job_ev.sem, job_ev.at(0, l, j0 + 3 + h))
                attention(0, l, BR_A, next_queries)
                in_panel(l, 9)
                in_panel(l, 10, B_CKV_W)
                in_panel(l, 11)
                banks_free(l, NIN)
                pe.wait_ge(mod_ev.sem, mod_ev.at(0, l, NIN))
                pe.wait_ge(prep.sem, prep.at(0, l, BTM_READY + 1))
                n = BR_B["j0"]
                for jb in JOBS_B1:
                    job(0, l, n, jb)
                    n += 1
                pe.wait_ge(b_in.sem, b_in.at(0, l, 48))
                pe.wait_ge(job_ev.sem, job_ev.at(0, l, n))
                for jb in JOBS_B2:
                    job(0, l, n, jb)
                    n += 1
                pe.wait_ge(prep.sem, prep.at(0, l, QPE_READY + 1))
                for jb in JOBS_B3:
                    job(0, l, n, jb)
                    n += 1
                pe.wait_ge(job_ev.sem, job_ev.at(0, l, n))
                attention(0, l, BR_B)
                panel(0, l, NIN, src=Y, n0=KC)
                apart(pe)
                with pe.Fori(NIN + 1, NP) as p:
                    panel(0, l, p)

            def ajob(l, n, parts):
                pe.wait_ge(ajob_ev.sem, ajob_ev.at(1, l, n + 1 - 2))
                for lhs, rhs, c, w in parts:
                    mm = pe.matmul(OUTB[n % 2][:, c:c + w], lhs, rhs, start=True, stop=True)
                mm.then_inc(ajob_done.sem, 1)

            def decay_sums(l, n, level, pr):
                ajob(l, n, [(gsum[:, level, :], la[:, 2 * pr + i, :], i * 256, 256) for i in range(2)])

            def level_turns(l, g, level, t):
                if g >= 2:
                    pe.wait_ge(gte_done.sem, gte_done.at(1, l, g + 1 - 2))
                s = g // 2
                if level < LEVELS:
                    pe.wait_ge(ge_done.sem, ge_done.at(1, l, 2 + (s // (LEVELS + 1)) * LEVELS + level + 1))
                for w in range(2):
                    for hp in range(2):
                        src = qk_g[:, t, w, tok(hp)] if level == LEVELS else qke[:, s % 2, t % 2, w, tok(hp)]
                        mm = pe.transpose(TURN[g % 2][:, tok(2 * w + hp)], src, ident[:, :])
                mm.then_inc(gt_done.sem, 1)

            def level_scores(l, g):
                pe.wait_ge(gte_done.sem, gte_done.at(1, l, g + 1))
                if g == 1:
                    pe.wait_ge(job_ev.sem, job_ev.at(1, l, 39))
                if g >= 2:
                    pe.wait_ge(gm_done.sem, gm_done.at(1, l, g + 1 - 2))
                for hp in range(2):
                    for e in range(2):
                        half = slice(e * G_DK, (e + 1) * G_DK)
                        mm = pe.matmul(LEVEL[g % 2][e][:, tok(hp)], qkT[half, g % 2, 2 + hp, :], qkT[half, g % 2, hp, :],
                                       start=True, stop=True)
                mm.then_inc(gs_done.sem, 1)

            def gla(l):
                n = 27
                pe.wait_ge(cg_lo.sem, cg_lo.at(1, l, 1))
                job(1, l, n, JOB_CG)
                pe.wait_ge(job_ev.sem, job_ev.at(1, l, n + 1))
                pe.wait_ge(sg_in.sem, sg_in.at(1, l, 96))
                for pr in range(2):
                    pe.wait_ge(job_ev.sem, job_ev.at(1, l, n + 1 + pr + 1 - 2))
                    for i in range(2):
                        mm = pe.matmul(JOB[(n + 1 + pr) % 2][:, i * 256:(i + 1) * 256], cgT[0:G_RANK, tok(2 * pr + i)],
                                       gate_w[0:G_RANK, :], start=True, stop=True)
                    mm.then_inc(job_done.sem, 1)
                pe.wait_ge(gla_in.sem, gla_in.at(1, l, 32))
                pe.wait_ge(prep.sem, prep.at(1, l, LA_READY + 1))
                for n_, (level, pr) in enumerate(((CUM, 0), (CUM, 1), (TAIL, 0), (TAIL, 1))):
                    decay_sums(l, n_, level, pr)
                ajob(l, 4, [(la[:, t, tok(hp)], gsum[:, CUM, CHUNK - 1:P:CHUNK], hp * 8 + 2 * t, 2)
                            for hp in range(2) for t in range(TT)])
                for pr in range(2):
                    pe.wait_ge(prep.sem, prep.at(1, l, QC_READY + pr + 1))
                    job(1, l, 30 + pr, JOBS_QC[pr])
                pe.wait_ge(ge_done.sem, ge_done.at(1, l, 2))
                for c in range(7):
                    t, half = c // 2, slice(c % 2 * CHUNK, (c % 2 + 1) * CHUNK)
                    pe.wait_ge(job_ev.sem, job_ev.at(1, l, 32 + c + 1 - 2))
                    apart(pe)
                    for hp in range(2):
                        for e in range(2):
                            h = 2 * hp + e
                            mm = pe.matmul(JOB[c % 2][e * G_DK:(e + 1) * G_DK, tok(hp)],
                                           kt_g[half, t, h * G_DK:(h + 1) * G_DK], vv_g[half, t, tok(h)],
                                           start=True, stop=True)
                    mm.then_inc(job_done.sem, 1)
                order = [(pr, level, i) for pr in range(2) for level in range(LEVELS + 1) for i in range(2)]
                decay_sums(l, 5, 0, 0)
                decay_sums(l, 6, 1, 0)
                for g in range(len(order) + 1):
                    if g < len(order):
                        pr, level, i = order[g]
                        level_turns(l, g, level, 2 * pr + i)
                        if i == 1:
                            k = pr * LEVELS + level + 2
                            if level < LEVELS and k < 2 * LEVELS:
                                decay_sums(l, 5 + k, k % LEVELS, k // LEVELS)
                    if g >= 1:
                        level_scores(l, g - 1)
                pe.wait_ge(ga_done.sem, ga_done.at(1, l, 24))
                pe.wait_ge(job_ev.sem, job_ev.at(1, l, 39))
                for t in range(TT):
                    if t >= 2:
                        pe.wait_ge(go_free.sem, go_free.at(1, l, t + 1 - 2))
                    apart(pe)
                    for h in range(G_H):
                        hp, e = h // 2, h % 2
                        for half in range(2):
                            c = 2 * t + half
                            pe.matmul(PAST[t % 2][e][half * CHUNK:(half + 1) * CHUNK, tok(hp)],
                                      qcT[e * G_DK:(e + 1) * G_DK, t, hp, half * CHUNK:(half + 1) * CHUNK],
                                      state[e * G_DK:(e + 1) * G_DK, c, hp, :], start=True, stop=True)
                        mm = pe.matmul(OUTB[t % 2][:, tok(h)], sacc[:, t, e, tok(hp)], vv_g[:, t, tok(h)],
                                       start=True, stop=True)
                    mm.then_inc(go_done.sem, 1)

            with pe.Fori(0, 2) as l:
                pe.wait_ge(small_in.sem, small_in.at(1, l, 96))
                pe.wait_ge(lin_free[0].sem, lin_free[0].at(1, l, 0))
                job(1, l, 0, turn_job([rows[0:88, :]], P, None))
                pe.wait_ge(job_ev.sem, job_ev.at(1, l, 1))
                panel(1, l, 0, src=xs)
                apart(pe)
                with pe.Fori(1, 7) as p:
                    panel(1, l, p)
                banks_free(l, 7, 1)
                pe.wait_ge(prep.sem, prep.at(1, l, S_READY + 1))
                j0 = BR_S["j0"]
                for n, jb in enumerate(JOBS_SK + JOBS_SQ[0:1]):
                    job(1, l, j0 + n, jb)

                def next_queries2(h):
                    if h + 1 < S_H:
                        job(1, l, j0 + 5 + h, JOBS_SQ[h + 1])
                    pe.wait_ge(job_ev.sem, job_ev.at(1, l, j0 + 5 + h))
                attention(1, l, BR_S, next_queries2)
                apart(pe)
                with pe.Fori(7, 11) as p:
                    panel(1, l, p)
                banks_free(l, NIN2, 1)
                pe.wait_ge(gla_in.sem, gla_in.at(1, l, 32))
                pe.wait_ge(prep.sem, prep.at(1, l, SG_READY + 1))
                for n in range(2):
                    job(1, l, 21 + n, turn_job([sg_wt[:, 4 * n + i, :] for i in range(4)], P, None))
                for n in range(4):
                    pe.wait_ge(job_ev.sem, job_ev.at(1, l, max(23, 23 + n + 1 - 2)))
                    for i in range(2):
                        g = 2 * n + i
                        mm = pe.matmul(JOB[(23 + n) % 2][:, i * 256:(i + 1) * 256], sg_wT[:, g, :],
                                       v_g[:, :, g * SG_C:(g + 1) * SG_C], start=True, stop=True)
                    mm.then_inc(job_done.sem, 1)
                gla(l)
                pe.wait_ge(prep.sem, prep.at(1, l, Y_READY + 1))
                panel(1, l, NIN2, src=Y, n0=KC)
                apart(pe)
                with pe.Fori(NIN2 + 1, NP2) as p:
                    panel(1, l, p)

        @block.scalar
        def _(act):
            def split_hi(blk, l, p, j, width=PW):
                act.wait_ge(w_landed[j % RS].sem, w_landed[j % RS].at(blk, l, 16 * (p * (ND // RS) + j // RS + 1)))
                used, n = ring_free(p, j)
                act.wait_ge(used.sem, used.at(blk, l, n))
                act.activation(whi[:, j % RH, :, 0:width], stage[:, j % RS, :, 0:width], ACT.Copy)\
                   .then_inc(hi_done.sem, 1)

            def panel(blk, l, p, take, width=PW, after=True, next_width=PW, between=None, turned=None):
                if turned:
                    for k in range(2 * LEAD):
                        turned(k)
                for j in range(LEAD, ND):
                    split_hi(blk, l, p, j, width)
                    if turned:
                        turned(2 * j)
                        turned(2 * j + 1)
                    if between:
                        between(j)
                if after:
                    for j in range(LEAD):
                        split_hi(blk, l, p + 1, j, next_width)
                if take:
                    take(l, p)

            def take_copy(dst, width=PW, blk=0):
                def go(l, p):
                    for t in (0, 2):
                        act.wait_ge(lin_done.sem, lin_done.at(blk, l, p * TT + t + 1))
                        act.activation(dst(t, p), LIN[t][:, 0:width], ACT.Copy).then_inc(lin_free[t].sem, 1)
                return go

            def take_tanh(blk=0):
                def go(l, p):
                    for t in range(TT):
                        act.wait_ge(lin_done.sem, lin_done.at(blk, l, p * TT + t + 1))
                        if t >= 2:
                            act.wait_ge(lin_free[t - 2].sem, lin_free[t - 2].at(blk, l, p + 1))
                        act.activation(tanh_tmp[:, t % 2, :], LIN[t][:, :], ACT.Tanh, scale=0.5)\
                           .then_inc(tanh_done.sem, 1)
                return go

            def mod_row_out(l, p):
                act.wait_ge(mod_sum.sem, mod_sum.at(0, l, p + 1))
                act.wait_ge(mod_row.sem, mod_row.at(0, l, 16 * p))
                act.activation(mrow[:, :], MSUM[0:1, :], ACT.Copy).then_inc(mod_ev.sem, 1)
                act.wait_ge(mod_ev.sem, mod_ev.at(0, l, p + 1))
                act.dma_start(mod_dram[bass.ds(l, 1), bass.ds(p * PW, PW)], mrow[:, :]).then_inc(mod_row.sem, 16)

            def in_panel(l, p, take, **kw):
                panel(0, l, p, take, **kw)
                mod_row_out(l, p)

            def square_sums(blk, l):
                for t in range(TT):
                    act.wait_ge(prep.sem, prep.at(blk, l, t + 1 - TT))
                    if blk == 0:
                        act.wait_ge(boot_x[t], 16)
                    act.dma_start(x_dram[:, t, :], Y[:, t, :]).then_inc(x_saved.sem, 16)
                    act.activation(xs[:, t, :], Y[:, t, :], ACT.Square, accum_out=ss[:, t:t + 1])\
                       .then_inc(sq_done.sem, 1)

            def turned_hi(blk, l, n0, scale):
                def go(k):
                    act.wait_ge(xp_done.sem, xp_done.at(blk, l, n0 + k + 1))
                    s = scale if isinstance(scale, float) else scale[:, k:k + 1]
                    act.activation(act_hi[:, k, :], XP[k % 4][:, :], ACT.Copy, scale=s).then_inc(xp_hi.sem, 1)
                return go

            def turned_mod(l):
                def go(k):
                    act.wait_ge(xp_done.sem, xp_done.at(1, l, k + 1))
                    act.wait_ge(xp_free.sem, xp_free.at(1, l, k + 1 - 2))
                    act.activation(turn_tmp[:, k % 2, :], XP[k % 4][:, :], ACT.Identity, scale=cols[:, k:k + 1],
                                   bias=cols[:, KC + k:KC + k + 1]).then_inc(xp_hi.sem, 1)
                return go

            def exp(blk, l, br, i):
                u = br["first"] + i
                act.wait_ge(max_done.sem, max_done.at(blk, l, u + 1))
                act.wait_ge(turn_done.sem, turn_done.at(blk, l, u + 1 - 4))
                kw = dict(bias=nmx[:, u % 4, 1:2])
                if br["name"] == "A":
                    kw["scale"] = rsq[:, i % 4, i // 4:i // 4 + 1]
                elif br["name"] != "B":
                    kw["scale"] = -1.0
                w = P * len(tiles_of(br, i))
                act.activation(probs[:, u % 4, 0:w], SCORE[u % 2][:, 0:w], ACT.Exp, accum_out=sm[:, u % 4:u % 4 + 1], **kw)\
                   .then_inc(exp_done.sem, 1)
                if br["name"] == "S":
                    act.activation(es[:, u % 4:u % 4 + 1], sinks[:, i // 4:i // 4 + 1], ACT.Exp, bias=nmx[:, u % 4, 1:2],
                                   scale=-1.0)

            def take_turn(blk, l, br, i):
                u = br["first"] + i
                act.wait_ge(turn_done.sem, turn_done.at(blk, l, u + 1))
                act.wait_ge(pv_done.sem, pv_done.at(blk, l, u + 1 - 4))
                w = P * len(tiles_of(br, i))
                act.activation(probsT[:, u % 4, 0:w], TURN[u % 2][:, 0:w], ACT.Copy).then_inc(pt_done.sem, 1)

            def attention(blk, l, br):
                n = 4 * br["heads"]
                for i in range(n + 2):
                    if i >= 2:
                        take_turn(blk, l, br, i - 2)
                    if i < n:
                        exp(blk, l, br, i)

            def out_panel(blk, l, p, after, turned=None):
                panel(blk, l, p, None, after=after, turned=turned)
                for t in range(TT):
                    act.wait_ge(sq_done.sem, sq_done.at(blk, l, TT + (p - NINS[blk]) * TT + t - 1))
                    act.wait_ge(lin_done.sem, lin_done.at(blk, l, p * TT + t + 1))
                    act.activation((mprod, macc)[t % 2][:, :], LIN[t][:, :], ACT.Square,
                                   accum_out=ss[:, bass.ds(TT + t * NOUT + p - NINS[blk], 1)]).then_inc(sq_done.sem, 1)

            act.sem_inc(exp_done.sem, exp_done.credit)
            act.sem_inc(mod_ev.sem, mod_ev.credit)
            act.sem_inc(ajob_ev.sem, ajob_ev.credit)
            act.sem_inc(mod_row.sem, mod_row.credit)
            act.sem_inc(pt_done.sem, pt_done.credit)
            act.wait_ge(boot_pe, 1)
            act.activation(ctmp[:, :], JOB[0][:, 0:KC], ACT.Tanh, scale=0.5).then_inc(boot_act, 1)
            with act.Fori(0, 2) as l:
                square_sums(0, l)
                for j in range(LEAD):
                    split_hi(0, l, 0, j)
                act.wait_ge(job_ev.sem, job_ev.at(0, l, 1))
                in_panel(l, 0, take_copy(lambda t, p: view(0, TT, PW)[:, t, :]), turned=turned_hi(0, l, 0, cols))
                in_panel(l, 1, take_copy(lambda t, p: view(2048, TT, PW)[:, t, :]))
                in_panel(l, 2, take_copy(lambda t, p: v_c[:, t, :]))
                in_panel(l, 3, take_tanh())
                attention(0, l, BR_C)
                with act.Fori(4, 6) as p:
                    in_panel(l, p, take_copy(lambda t, p: zone[:, bass.ds(ZQ + t * 1024 + (p - 4) * PW, PW)]))
                in_panel(l, 6, take_copy(lambda t, p: kv_a[:, t, :]))
                with act.Fori(7, 9) as p:
                    in_panel(l, p, take_tanh())
                attention(0, l, BR_A)
                in_panel(l, 9, take_copy(lambda t, p: cq_b[:, t, :]), next_width=B_CKV_W)
                in_panel(l, 10, take_copy(lambda t, p: ckv_b[:, t, :], B_CKV_W), width=B_CKV_W)
                in_panel(l, 11, take_tanh())
                attention(0, l, BR_B)
                out_panel(0, l, NIN, True, turned=turned_hi(0, l, KC, 0.5))
                with act.Fori(NIN + 1, NP - 1) as p:
                    out_panel(0, l, p, True)
                out_panel(0, l, NP - 1, False)
            act.wait_ge(mod_row.sem, mod_row.at(0, 2, 0))

            def sines(l):
                def go(j):
                    if j == 5:
                        act.wait_ge(angles_done.sem, angles_done.at(1, l, 1))
                        act.activation(rot[:, 1, :, :], rtmp[:, 2, :, :], ACT.Sin).then_inc(rot_done.sem, 1)
                        act.activation(rot[:, 0, :, :], rtmp[:, 3, :, :], ACT.Sin).then_inc(rot_done.sem, 1)
                return go

            def gelu_between(l):
                def go(j):
                    if j not in (2, 3, 4, 5):
                        return
                    x = u_g if j < 4 else v_g
                    if j == 2:
                        for t in range(TT):
                            act.wait_ge(lin_free[t].sem, lin_free[t].at(1, l, 9))
                    act.wait_ge(gelu_dve.sem, gelu_dve.at(1, l, j - 2))
                    if j % 2 == 0:
                        act.activation(gelu_tmp, x.rearrange("p t n -> p (t n)"), ACT.Square).then_inc(gelu_act.sem, 1)
                    else:
                        act.activation(gelu_tmp, gelu_tmp, ACT.Tanh, scale=GELU_B).then_inc(gelu_act.sem, 1)
                return go

            def take_decays(l, n, dst):
                act.wait_ge(ajob_done.sem, ajob_done.at(1, l, n + 1))
                act.activation(dst, OUTB[n % 2][:, 0:512], ACT.Exp).then_inc(ajob_ev.sem, 1)

            def gla(l):
                act.wait_ge(soft_dve.sem, soft_dve.at(1, l, 1))
                act.activation(soft, soft, ACT.Exp).then_inc(soft_act.sem, 1)
                act.wait_ge(soft_act.sem, soft_act.at(1, l, 1))
                act.activation(soft, soft, ACT.Ln, bias=1.0).then_inc(soft_act.sem, 1)
                for n in range(4):
                    if n >= 2:
                        act.wait_ge(prep.sem, prep.at(1, l, QC_READY + n + 1 - 2))
                    take_decays(l, n, eg[:, n % 2, :, :].rearrange("p t n -> p (t n)"))
                act.wait_ge(ajob_done.sem, ajob_done.at(1, l, 5))
                act.activation(decay[:, :, :].rearrange("p h c -> p (h c)"), OUTB[0][:, 0:16], ACT.Exp).then_inc(ajob_ev.sem, 1)

                def level_decays(k):
                    act.wait_ge(ge_done.sem, ge_done.at(1, l, 2 + k + 1 - 2))
                    take_decays(l, 5 + k, eg[:, k % 2, :, :].rearrange("p t n -> p (t n)"))
                level_decays(0)
                level_decays(1)
                for g in range(4 * (LEVELS + 1)):
                    act.wait_ge(gt_done.sem, gt_done.at(1, l, g + 1))
                    if g >= 2:
                        act.wait_ge(gs_done.sem, gs_done.at(1, l, g + 1 - 2))
                    act.activation(qkT[:, g % 2, :, :].rearrange("p w n -> p (w n)"), TURN[g % 2][:, :], ACT.Copy)\
                       .then_inc(gte_done.sem, 1)
                    pr, level, i = g // (2 * LEVELS + 2), g // 2 % (LEVELS + 1), g % 2
                    k = pr * LEVELS + level + 2
                    if i == 1 and level < LEVELS and k < 2 * LEVELS:
                        level_decays(k)

            with act.Fori(0, 2) as l:
                square_sums(1, l)
                for j in range(LEAD):
                    split_hi(1, l, 0, j)
                act.wait_ge(prep.sem, prep.at(1, l, XS_READY + 1))
                panel(1, l, 0, take_copy(lambda t, p: q_s[:, t, 0:PW], blk=1), turned=turned_mod(l))
                panel(1, l, 1, take_copy(lambda t, p: q_s[:, t, PW:2 * PW], blk=1), between=sines(l))
                panel(1, l, 2, take_copy(lambda t, p: kv_s[:, t, :], blk=1))
                with act.Fori(3, 7) as p:
                    panel(1, l, p, take_tanh(1))
                act.wait_ge(sink_in.sem, sink_in.at(1, l, 16))
                attention(1, l, BR_S)
                with act.Fori(7, 9) as p:
                    panel(1, l, p, take_copy(lambda t, p: zone[:, bass.ds(ZQ + (p - 7) * 2048 + t * PW, PW)], blk=1))
                panel(1, l, 9, take_copy(lambda t, p: view(ZV, TT, PW)[:, t, :], blk=1), between=gelu_between(l))

                def cg_high(j):
                    if j == 3:
                        act.wait_ge(cg_in.sem, cg_in.at(1, l, 16))
                        act.activation(cgw_hi[:, :, :], cgw[:, :, :], ACT.Copy).then_inc(cg_hi.sem, 1)
                panel(1, l, 10, take_copy(lambda t, p: vv_g[:, t, :], blk=1), between=cg_high)
                gla(l)
                out_panel(1, l, NIN2, True, turned=turned_hi(1, l, KC, 0.5))
                with act.Fori(NIN2 + 1, NP2 - 1) as p:
                    out_panel(1, l, p, True)
                out_panel(1, l, NP2 - 1, False)
            for t in range(TT):
                act.wait_ge(prep.sem, prep.at(1, 2, t + 1 - TT))
                act.dma_start(x_dram[:, t, :], Y[:, t, :]).then_inc(x_saved.sem, 16)

        @block.vector
        def _(dve):

            def split_lo(blk, l, p, j, width=PW):
                c = p * ND + j
                dve.wait_ge(hi_done.sem, hi_done.at(blk, l, c + 1))
                used, n = ring_free(p, j)
                dve.wait_ge(used.sem, used.at(blk, l, n))
                dve.tensor_tensor(wlo[:, j % RH, :, 0:width], stage[:, j % RS, :, 0:width],
                                  whi[:, j % RH, :, 0:width].bitcast(F32), ALU.subtract).then_inc(lo_done.sem, 1)

            def panel(blk, l, p, take, width=PW, after=True, next_width=PW, between=None, turned=None):
                if turned:
                    for k in range(2 * LEAD):
                        turned(k)
                for j in range(LEAD, ND):
                    split_lo(blk, l, p, j, width)
                    if turned:
                        turned(2 * j)
                        turned(2 * j + 1)
                    if between:
                        between(j)
                if after:
                    for j in range(LEAD):
                        split_lo(blk, l, p + 1, j, next_width)
                if take:
                    take(l, p)

            def take_copy(dst, width=PW, blk=0):
                def go(l, p):
                    for t in (1, 3):
                        dve.wait_ge(lin_done.sem, lin_done.at(blk, l, p * TT + t + 1))
                        dve.tensor_copy(dst(t, p), LIN[t][:, 0:width]).then_inc(lin_free[t].sem, 1)
                return go

            def take_gate(ycol, n, blk=0):
                def go(l, p):
                    for t in range(TT):
                        dve.wait_ge(tanh_done.sem, tanh_done.at(blk, l, n(p) * TT + t + 1))
                        dve.scalar_tensor_tensor(out=Y[:, t, bass.ds(ycol(p), PW)], in0=tanh_tmp[:, t % 2, :], scalar=1.0,
                                                 in1=LIN[t][:, :], op0=ALU.add, op1=ALU.mult)\
                           .then_inc(lin_free[t].sem, 1)
                return go

            def rsqrt(blk, l, n, width):
                v, y, a = (nv[:, i, 0:n] for i in range(3))
                dve.wait_ge(dve_link.sem, dve_link.now(blk, l))
                dve.tensor_scalar(v, ss[:, 0:n], 1.0 / width, EPS, ALU.mult, ALU.add).then_inc(dve_link.next(), 1)
                dve.wait_ge(dve_link.sem, dve_link.now(blk, l))
                dve.tensor_scalar(a.bitcast(I32), v.bitcast(I32), 1, None, ALU.logical_shift_right)\
                   .then_inc(dve_link.next(), 1)
                dve.wait_ge(dve_link.sem, dve_link.now(blk, l))
                dve.tensor_scalar(y.bitcast(I32), a.bitcast(I32), -1, 0x5F3759DF, ALU.mult, ALU.add)\
                   .then_inc(dve_link.next(), 1)
                for i in range(3):
                    dve.wait_ge(dve_link.sem, dve_link.now(blk, l))
                    dve.tensor_tensor(a, y, y, ALU.mult).then_inc(dve_link.next(), 1)
                    dve.wait_ge(dve_link.sem, dve_link.now(blk, l))
                    dve.scalar_tensor_tensor(out=a, in0=a, scalar=-0.5, in1=v, op0=ALU.mult, op1=ALU.mult)\
                       .then_inc(dve_link.next(), 1)
                    dve.wait_ge(dve_link.sem, dve_link.now(blk, l))
                    out = rs[:, 0:n] if i == 2 else y
                    dve.scalar_tensor_tensor(out=out, in0=a, scalar=1.5, in1=y, op0=ALU.add, op1=ALU.mult)\
                       .then_inc(dve_link.next(), 1)
                dve.wait_ge(dve_link.sem, dve_link.now(blk, l))

            def normalise(blk, l):
                for t in range(TT):
                    dve.wait_ge(sq_done.sem, sq_done.at(blk, l, t + 1))
                rsqrt(blk, l, TT, DM)
                for cols_ in (slice(0, DM // 2), slice(DM // 2, DM)):
                    for t in range(TT):
                        dve.tensor_scalar(xs[:, t, cols_], Y[:, t, cols_], rs[:, t:t + 1], None, ALU.mult)\
                           .then_inc(prep.sem, 1)

            def turned_lo(blk, l, n0, scale):
                def go(k):
                    dve.wait_ge(xp_hi.sem, xp_hi.at(blk, l, n0 + k + 1))
                    s = scale if isinstance(scale, float) else scale[:, k:k + 1]
                    dve.scalar_tensor_tensor(out=act_lo[:, k, :], in0=XP[k % 4][:, :], scalar=s,
                                             in1=act_hi[:, k, :].bitcast(F32), op0=ALU.mult, op1=ALU.subtract)\
                       .then_inc(xp_free.sem, 1)
                return go

            def turned_mod(l):
                def go(k):
                    dve.wait_ge(xp_hi.sem, xp_hi.at(1, l, k + 1))
                    dve.tensor_copy(act_hi[:, k, :], turn_tmp[:, k % 2, :]).then_inc(dve_link.next(), 1)
                    dve.wait_ge(dve_link.sem, dve_link.now(1, l))
                    dve.tensor_tensor(act_lo[:, k, :], turn_tmp[:, k % 2, :], act_hi[:, k, :].bitcast(F32), ALU.subtract)\
                       .then_inc(xp_free.sem, 1)
                return go

            def take_job(blk, l, n, jb):
                kind, parts, width, dst, scale = jb
                dve.wait_ge(job_done.sem, job_done.at(blk, l, n + 1))
                if kind == "turn":
                    src = JOB[n % 2][0:width, 0:sum(s.shape[0] for s in parts)]
                else:
                    src = JOB[n % 2][:, 0:width]
                if isinstance(scale, float) and scale == 1.0:
                    dve.tensor_copy(dst, src).then_inc(job_ev.sem, 1)
                else:
                    dve.tensor_scalar(dst, src, scale, None, ALU.mult).then_inc(job_ev.sem, 1)

            def row_max(blk, l, br, i):
                u = br["first"] + i
                h, t = i // 4, i % 4
                dve.wait_ge(score_done.sem, score_done.at(blk, l, u + 1))
                s, m, nm = SCORE[u % 2][:, :], nmx[:, u % 4, 0:1], nmx[:, u % 4, 1:2]
                if br["name"] == "C":
                    bias = g_c[:, h, 6 - 2 * t:14 - 2 * t, :].rearrange("p m k -> p (m k)")
                    apart(dve)
                    dve.tensor_tensor_reduce(s, s, bias, 1.0, 3.0e38, ALU.add, ALU.min, nm).then_inc(max_done.sem, 1)
                elif br["name"] == "A":
                    dve.tensor_reduce(m, s, AX.X, ALU.max, negate=True).then_inc(dve_link.next(), 1)
                    dve.wait_ge(dve_link.sem, dve_link.now(blk, l))
                    dve.tensor_tensor(nm, m, rsq[:, t, h:h + 1], ALU.mult).then_inc(max_done.sem, 1)
                elif br["name"] == "S":
                    w = P * len(tiles_of(br, i))
                    apart(dve)
                    dve.tensor_tensor_reduce(s[:, 0:w], s[:, 0:w], band[:, 2 * P - w:2 * P], 1.0, sinks[:, h:h + 1],
                                             ALU.add, ALU.min, nm).then_inc(max_done.sem, 1)
                else:
                    dve.tensor_reduce(nm, s, AX.X, ALU.max, negate=True).then_inc(max_done.sem, 1)

            def finish(blk, l, br, i):
                u = br["first"] + i
                h, t = i // 4, i % 4
                dve.wait_ge(pv_done.sem, pv_done.at(blk, l, u + 1))
                total, dv = sm[:, u % 4:u % 4 + 1], dv_of(br)
                if br["name"] == "S":
                    total = den[:, u % 4:u % 4 + 1]
                    dve.tensor_tensor(total, sm[:, u % 4:u % 4 + 1], es[:, u % 4:u % 4 + 1], ALU.add)\
                       .then_inc(dve_link.next(), 1)
                    dve.wait_ge(dve_link.sem, dve_link.now(blk, l))
                dve.reciprocal(ri[:, u % 4, 0:1], total).then_inc(dve_link.next(), 1)
                dve.wait_ge(dve_link.sem, dve_link.now(blk, l))
                y = Y[:, t, br["y"] + h * dv:br["y"] + (h + 1) * dv]
                dve.scalar_tensor_tensor(out=y, in0=OUTB[u % 2][:, 0:dv], scalar=ri[:, u % 4, 0:1], in1=y,
                                         op0=ALU.mult, op1=ALU.mult).then_inc(fin_done.sem, 1)

            def attention(blk, l, br, early=None):
                n = 4 * br["heads"]
                for i in range(n + 3):
                    if early and i % 4 == 0 and i < n:
                        early(i // 4)
                    if i < n:
                        row_max(blk, l, br, i)
                    if i >= 3:
                        finish(blk, l, br, i - 3)

            def out_panel(blk, l, p, after, between=None, turned=None):
                panel(blk, l, p, None, after=after, between=between, turned=turned)
                for t in range(TT):
                    dve.wait_ge(sq_done.sem, sq_done.at(blk, l, TT + (p - NINS[blk]) * TT + t + 1))
                    dve.tensor_tensor(Y[:, t, bass.ds((p - NINS[blk]) * PW, PW)], LIN[t][:, :],
                                      zone[:, bass.ds(ZT + (p - NINS[blk]) * PW, PW)], ALU.mult).then_inc(lin_free[t].sem, 1)

            def residual(blk, l):
                dve.tensor_reduce(ss[:, 0:TT], ss[:, TT:TT + TT * NOUT].rearrange("p (t q) -> p t q", t=TT), AX.X, ALU.add)\
                   .then_inc(dve_link.next(), 1)
                rsqrt(blk, l, TT, DM)
                dve.wait_ge(end_in.sem, end_in.at(blk, l, 16))
                for t in range(TT):
                    dve.scalar_tensor_tensor(out=Y[:, t, :], in0=Y[:, t, :], scalar=rs[:, t:t + 1], in1=xs[:, t, :],
                                             op0=ALU.mult, op1=ALU.add).then_inc(prep.sem, 1)

            def rope(blk, l, x, t1, t2, cos, sin, half):
                dve.tensor_tensor(t1, x, cos, ALU.mult).then_inc(dve_link.next(), 1)
                for s in range(2):
                    dve.tensor_tensor(t2.rearrange("p h (a s f) -> p h a s f", a=2, s=2)[:, :, :, s, :],
                                      x.rearrange("p h (a s f) -> p h a s f", a=2, s=2)[:, :, :, 1 - s, :],
                                      sin.rearrange("p h (a s f) -> p h a s f", a=2, s=2)[:, :, :, s, :], ALU.mult)\
                       .then_inc(dve_link.next(), 1)
                dve.wait_ge(dve_link.sem, dve_link.now(blk, l))
                return dve.tensor_tensor(x, t1, t2, ALU.add)

            def over(ap, n):
                return ap.unsqueeze(1).broadcast_to([P, n, ap.shape[-1]])

            gains_a = view(PP + 2560, 2, HD)
            rope_a = view(PP + 3072, 2, TT, HD)

            def a_sums(l, t):
                nh = A_H + A_KV
                sq = view(PP, nh, HD)
                if t == 0:
                    for i in range(TT):
                        dve.wait_ge(lin_free[i].sem, lin_free[i].at(0, l, 7))
                q, k = q_a[:, t, :], kv_a[:, t, 0:A_KV * HD]
                dve.wait_ge(dve_link.sem, dve_link.now(0, l))
                dve.tensor_tensor(view(PP, A_H * HD), q, q, ALU.mult).then_inc(dve_link.next(), 1)
                dve.tensor_tensor(view(PP + A_H * HD, A_KV * HD), k, k, ALU.mult).then_inc(dve_link.next(), 1)
                dve.wait_ge(dve_link.sem, dve_link.now(0, l))
                dve.tensor_reduce(ss[:, t * nh:(t + 1) * nh], sq, AX.X, ALU.add).then_inc(dve_link.next(), 1)

            def a_rope(l, t):
                nh = A_H + A_KV
                q = q_a[:, t, :].rearrange("p (h d) -> p h d", d=HD)
                k = kv_a[:, t, 0:A_KV * HD].rearrange("p (h d) -> p h d", d=HD)
                rk = rs[:, t * nh + A_H:(t + 1) * nh].unsqueeze(2).broadcast_to([P, A_KV, HD])
                if t == 0:
                    dve.wait_ge(a_in.sem, a_in.at(0, l, 48))
                dve.tensor_tensor(k, k, rk, ALU.mult).then_inc(dve_link.next(), 1)
                dve.tensor_tensor(q, q, over(gains_a[:, 0, :], A_H), ALU.mult).then_inc(dve_link.next(), 1)
                dve.wait_ge(dve_link.sem, dve_link.now(0, l))
                dve.tensor_tensor(k, k, over(gains_a[:, 1, :], A_KV), ALU.mult).then_inc(dve_link.next(), 1)
                dve.wait_ge(dve_link.sem, dve_link.now(0, l))
                for x, n, o in ((q, A_H, 0), (k, A_KV, A_H * HD)):
                    done = rope(0, l, x, view(PP + o, n, HD), view(PP + 1280 + o, n, HD),
                                over(rope_a[:, 0, t, :], n), over(rope_a[:, 1, t, :], n), 32)
                    if t == TT - 1 and n == A_KV:
                        done.then_inc(prep.sem, 1)
                    else:
                        done.then_inc(dve_link.next(), 1)
                        dve.wait_ge(dve_link.sem, dve_link.now(0, l))

            def a_between1(l):
                def go(j):
                    if j < 6:
                        a_sums(l, j - 2)
                    elif j == 6:
                        rsqrt(0, l, TT * (A_H + A_KV), HD)
                        dve.tensor_scalar(rsq[:, :, :], rs[:, 0:40].rearrange("p (t h) -> p t h", t=TT)[:, :, 0:A_H],
                                          SC_A, None, ALU.mult).then_inc(dve_link.next(), 1)
                    else:
                        a_rope(l, 0)
                return go

            def a_between2(l):
                def go(j):
                    if j < 5:
                        a_rope(l, j - 1)
                return go

            def b_between(l):
                junk = view(ZT + 1024, PW)

                def go(j):
                    if j == 2:
                        for t in range(TT):
                            dve.wait_ge(lin_free[t].sem, lin_free[t].at(0, l, 11))
                        for t in range(TT):
                            for x, o in ((cq_b[:, t, :], 0), (ckv_b[:, t, 0:B_KV], TT)):
                                dve.tensor_tensor_reduce(junk[:, 0:x.shape[-1]], x, x, float(B_Q // x.shape[-1]), 0.0,
                                                         ALU.mult, ALU.add, ss[:, o + t:o + t + 1])\
                                   .then_inc(dve_link.next(), 1)
                                dve.wait_ge(dve_link.sem, dve_link.now(0, l))
                    elif j == 3:
                        rsqrt(0, l, 2 * TT, B_Q)
                    elif j == 4:
                        for t in range(TT):
                            dve.tensor_scalar(cq_b[:, t, :], cq_b[:, t, :], rs[:, t:t + 1], None, ALU.mult)\
                               .then_inc(dve_link.next(), 1)
                            dve.tensor_scalar(ckv_b[:, t, 0:B_KV], ckv_b[:, t, 0:B_KV], rs[:, TT + t:TT + t + 1], None,
                                              ALU.mult).then_inc(dve_link.next(), 1)
                    elif j == 5:
                        dve.wait_ge(b_in.sem, b_in.at(0, l, 48))
                        dve.wait_ge(dve_link.sem, dve_link.now(0, l))
                        rope(0, l, ckv_b[:, :, B_KV:B_CKV_W], view(PP + 3584, TT, B_ROPE), view(PP + 3840, TT, B_ROPE),
                             cos_b, sin_b, 16).then_inc(prep.sem, 1)
                return go

            dve.sem_inc(lo_done.sem, lo_done.credit)
            for c in lin_free:
                dve.sem_inc(c.sem, c.credit)
            for c in (xp_free, job_ev, fin_done, prep):
                dve.sem_inc(c.sem, c.credit)
            dve.wait_ge(boot_act, 1)
            dve.scalar_tensor_tensor(out=csil[:, :], in0=ctmp[:, :], scalar=1.0, in1=JOB[0][:, 0:KC],
                                     op0=ALU.add, op1=ALU.mult).then_inc(boot_dve, 1)
            dve.wait_ge(boot_dve, 1)
            dve.tensor_scalar(csil[:, :], csil[:, :], 0.5, None, ALU.mult).then_inc(boot_dve, 1)
            with dve.Fori(0, 2) as l:
                dve_link.made = 0
                dve.wait_ge(job_done.sem, job_done.at(0, l, 1))
                dve.tensor_copy(cols[:, 0:KC + 6], JOB[0][:, 0:KC + 6]).then_inc(job_ev.sem, 1)
                normalise(0, l)
                for j in range(LEAD):
                    split_lo(0, l, 0, j)
                dve.wait_ge(job_ev.sem, job_ev.at(0, l, 1))

                def mask_bias(j):
                    if j == 4:
                        dve.wait_ge(g_in.sem, g_in.at(0, l, 32))
                        g = view(ZQ, C_H * GM, GRID_W)
                        dve.scalar_tensor_tensor(out=g, in0=g, scalar=-1.0, in1=over(gmask[:, :], C_H * GM),
                                                 op0=ALU.mult, op1=ALU.subtract).then_inc(dve_link.next(), 1)

                panel(0, l, 0, take_copy(lambda t, p: view(0, TT, PW)[:, t, :]), turned=turned_lo(0, l, 0, cols))
                panel(0, l, 1, take_copy(lambda t, p: view(2048, TT, PW)[:, t, :]))
                panel(0, l, 2, take_copy(lambda t, p: v_c[:, t, :]), between=mask_bias)
                dve.wait_ge(x_saved.sem, x_saved.at(0, l, 16 * TT))
                panel(0, l, 3, take_gate(lambda p: Y_C, lambda p: 0))
                for n, jb in enumerate(JOBS_C):
                    take_job(0, l, BR_C["j0"] + n, jb)
                dve.wait_ge(dve_link.sem, dve_link.now(0, l))
                attention(0, l, BR_C)
                with dve.Fori(4, 6) as p:
                    panel(0, l, p, take_copy(lambda t, p: zone[:, bass.ds(ZQ + t * 1024 + (p - 4) * PW, PW)]))
                panel(0, l, 6, take_copy(lambda t, p: kv_a[:, t, :]))
                panel(0, l, 7, take_gate(lambda p: 0, lambda p: 1), between=a_between1(l))
                panel(0, l, 8, take_gate(lambda p: PW, lambda p: 2), between=a_between2(l))
                j0 = BR_A["j0"]
                for n, jb in enumerate(JOBS_AK + JOBS_AQ[0:1]):
                    take_job(0, l, j0 + n, jb)

                def next_queries(h):
                    if h + 1 < A_H:
                        take_job(0, l, j0 + 3 + h, JOBS_AQ[h + 1])
                attention(0, l, BR_A, next_queries)
                panel(0, l, 9, take_copy(lambda t, p: cq_b[:, t, :]), next_width=B_CKV_W)
                panel(0, l, 10, take_copy(lambda t, p: ckv_b[:, t, :], B_CKV_W), width=B_CKV_W)
                panel(0, l, 11, take_gate(lambda p: Y_B, lambda p: 3), between=b_between(l))
                n = BR_B["j0"]
                for jb in JOBS_B1 + JOBS_B2:
                    take_job(0, l, n, jb)
                    n += 1
                dve.wait_ge(job_ev.sem, job_ev.at(0, l, BR_B["j0"] + 11))
                for t in range(TT):
                    x = qpe[:, t, :].rearrange("p (h d) -> p h d", h=B_H)
                    done = rope(0, l, x, late_tmp[:, 0, t * 256:(t + 1) * 256].rearrange("p (h d) -> p h d", h=B_H),
                                late_tmp[:, 1, t * 256:(t + 1) * 256].rearrange("p (h d) -> p h d", h=B_H),
                                over(cos_b[:, t, :], B_H), over(sin_b[:, t, :], B_H), 16)
                    if t == TT - 1:
                        done.then_inc(prep.sem, 1)
                    else:
                        done.then_inc(dve_link.next(), 1)
                dve.wait_ge(dve_link.sem, dve_link.now(0, l))
                for jb in JOBS_B3:
                    take_job(0, l, n, jb)
                    n += 1
                attention(0, l, BR_B)

                def gain_landed(j):
                    if j == ND - 1:
                        dve.wait_ge(gain_in.sem, gain_in.at(0, l, 16))
                out_panel(0, l, NIN, True, gain_landed, turned=turned_lo(0, l, KC, 0.5))
                with dve.Fori(NIN + 1, NP - 1) as p:
                    out_panel(0, l, p, True)
                out_panel(0, l, NP - 1, False)
                residual(0, l)
                assert dve_link.made == DVE_LINKS1, dve_link.made

            def angles(l):
                prod, turns, sine, cosine, part1, part2 = (rtmp[:, i, :, :] for i in range(6))
                turn1, turn2 = 6.28125, 0.0019350051879882812
                turn3 = 2 * np.pi - turn1 - turn2

                def go(j):
                    if j != 3:
                        return
                    dve.wait_ge(boot2_dma, 48)
                    dve.tensor_copy(pos_f[:, :], pos_i[:, :]).then_inc(dve_link.next(), 1)
                    dve.wait_ge(dve_link.sem, dve_link.now(1, l))
                    dve.tensor_tensor(prod, pos_f[:, :].unsqueeze(2).broadcast_to([P, TT, ROT // 2]),
                                      freq[:, :].unsqueeze(1).broadcast_to([P, TT, ROT // 2]), ALU.mult)\
                       .then_inc(dve_link.next(), 1)
                    dve.wait_ge(dve_link.sem, dve_link.now(1, l))
                    dve.tensor_scalar(turns, prod, 1 / (2 * np.pi), 1.5 * 2 ** 23, ALU.mult, ALU.add)\
                       .then_inc(dve_link.next(), 1)
                    dve.wait_ge(dve_link.sem, dve_link.now(1, l))
                    dve.tensor_scalar(turns, turns, 1.5 * 2 ** 23, None, ALU.subtract).then_inc(dve_link.next(), 1)
                    dve.wait_ge(dve_link.sem, dve_link.now(1, l))
                    for out, turn, x in ((part1, turn1, prod), (part2, turn2, part1), (part1, turn3, part2)):
                        dve.scalar_tensor_tensor(out=out, in0=turns, scalar=-turn, in1=x, op0=ALU.mult, op1=ALU.add)\
                           .then_inc(dve_link.next(), 1)
                        dve.wait_ge(dve_link.sem, dve_link.now(1, l))
                    dve.tensor_scalar(sine, part1, 3.1415925, -3.1415925, ALU.min, ALU.max).then_inc(dve_link.next(), 1)
                    dve.wait_ge(dve_link.sem, dve_link.now(1, l))
                    dve.scalar_tensor_tensor(out=prod, in0=sine, scalar=-1.0, in1=sine, op0=ALU.mult, op1=ALU.max)\
                       .then_inc(dve_link.next(), 1)
                    dve.wait_ge(dve_link.sem, dve_link.now(1, l))
                    dve.tensor_scalar(cosine, prod, -1.0, np.pi / 2, ALU.mult, ALU.add).then_inc(angles_done.sem, 1)
                return go

            def swa_rope(l):
                for t in range(TT):
                    dve.wait_ge(lin_free[t].sem, lin_free[t].at(1, l, 3))
                dve.wait_ge(rot_done.sem, rot_done.at(1, l, 2))
                hh = ROT // 2
                cos = rot[:, 0, :, :].unsqueeze(2)
                sin = rot[:, 1, :, :].unsqueeze(2)
                for x, n, o in ((q_s, S_H, 0), (kv_s[:, :, 0:S_KV * S_D], S_KV, 2048)):
                    xh = x.rearrange("p t (h d) -> p t h d", d=S_D)
                    x1, x2 = xh[:, :, :, 0:hh], xh[:, :, :, hh:ROT]
                    c, s_ = (a.broadcast_to([P, TT, n, hh]) for a in (cos, sin))
                    t1, t2, t3, t4 = (view(PP + o + i * TT * n * hh, TT, n, hh) for i in range(4))
                    dve.tensor_tensor(t1, x1, c, ALU.mult).then_inc(dve_link.next(), 1)
                    dve.tensor_tensor(t2, x2, s_, ALU.mult).then_inc(dve_link.next(), 1)
                    dve.tensor_tensor(t3, x2, c, ALU.mult).then_inc(dve_link.next(), 1)
                    dve.tensor_tensor(t4, x1, s_, ALU.mult).then_inc(dve_link.next(), 1)
                    dve.wait_ge(dve_link.sem, dve_link.now(1, l))
                    dve.tensor_tensor(x1, t1, t2, ALU.subtract).then_inc(dve_link.next(), 1)
                    if n == S_H:
                        dve.tensor_tensor(x2, t3, t4, ALU.add).then_inc(dve_link.next(), 1)
                dve.wait_ge(dve_link.sem, dve_link.now(1, l))
                dve.tensor_tensor(x2, t3, t4, ALU.add).then_inc(prep.sem, 1)

            def gelu_between(l):
                def go(j):
                    if j not in (2, 3, 4, 5):
                        return
                    x = (u_g if j < 4 else v_g).rearrange("p t n -> p (t n)")
                    if j == 2:
                        for t in range(TT):
                            dve.wait_ge(lin_free[t].sem, lin_free[t].at(1, l, 9))
                    dve.wait_ge(gelu_act.sem, gelu_act.at(1, l, j - 1))
                    if j % 2 == 0:
                        dve.tensor_scalar(gelu_tmp, gelu_tmp, GELU_A, 1.0, ALU.mult, ALU.add)\
                           .then_inc(dve_link.next(), 1)
                        dve.wait_ge(dve_link.sem, dve_link.now(1, l))
                        dve.tensor_tensor(gelu_tmp, gelu_tmp, x, ALU.mult).then_inc(gelu_dve.sem, 1)
                    else:
                        dve.scalar_tensor_tensor(out=x, in0=gelu_tmp, scalar=1.0, in1=x, op0=ALU.add, op1=ALU.mult)\
                           .then_inc(gelu_dve.sem, 1)
                return go

            def norm_between(l):
                def go(j):
                    if j == 5:
                        dve.wait_ge(cg_hi.sem, cg_hi.at(1, l, 1))
                        dve.tensor_tensor(cgw_lo[:, :, :], cgw[:, :, :], cgw_hi[:, :, :].bitcast(F32), ALU.subtract)\
                           .then_inc(cg_lo.sem, 1)
                    if j == 2:
                        dve.wait_ge(gelu_dve.sem, gelu_dve.at(1, l, 4))
                        for t in range(TT):
                            dve.bn_stats(bnst[:, t, :], v_g[:, t, :]).then_inc(dve_link.next(), 1)
                        dve.wait_ge(dve_link.sem, dve_link.now(1, l))
                        apart(dve)
                        for t in range(TT):
                            dve.bn_aggr(mv[:, t, :], bnst[:, t, :]).then_inc(dve_link.next(), 1)
                        dve.wait_ge(dve_link.sem, dve_link.now(1, l))
                        dve.tensor_copy(ss[:, 0:TT], mv[:, :, 1]).then_inc(dve_link.next(), 1)
                        rsqrt(1, l, TT, 4.0)
                        dve.tensor_scalar(rs[:, 0:TT], rs[:, 0:TT], 0.5, None, ALU.mult).then_inc(dve_link.next(), 1)
                        dve.wait_ge(sg_in.sem, sg_in.at(1, l, 96))
                        dve.wait_ge(dve_link.sem, dve_link.now(1, l))
                    elif j in (3, 4):
                        for t in (2 * j - 6, 2 * j - 5):
                            dve.tensor_scalar(v_g[:, t, :], v_g[:, t, :], mv[:, t, 0:1], rs[:, t:t + 1],
                                              ALU.subtract, ALU.mult).then_inc(dve_link.next(), 1)
                            dve.wait_ge(dve_link.sem, dve_link.now(1, l))
                            dve.tensor_tensor(v_g[:, t, :], v_g[:, t, :], ln_g, ALU.mult).then_inc(dve_link.next(), 1)
                            dve.wait_ge(dve_link.sem, dve_link.now(1, l))
                            done = dve.tensor_tensor(v_g[:, t, :], v_g[:, t, :], ln_b, ALU.add)
                            if t == TT - 1:
                                done.then_inc(prep.sem, 1)
                            else:
                                done.then_inc(dve_link.next(), 1)
                return go

            def spatial(l):
                for n in range(2):
                    dve.wait_ge(job_done.sem, job_done.at(1, l, 21 + n + 1))
                    dve.scalar_tensor_tensor(out=sg_wT[:, 4 * n:4 * n + 4, :],
                                             in0=JOB[(21 + n) % 2][:, :].rearrange("p (g t) -> p g t", g=4), scalar=0.5,
                                             in1=gmasks[:, LEVELS + 1, :].unsqueeze(1).broadcast_to([P, 4, P]),
                                             op0=ALU.mult, op1=ALU.mult).then_inc(job_ev.sem, 1)
                for n in range(4):
                    dve.wait_ge(job_done.sem, job_done.at(1, l, 23 + n + 1))
                    for i in range(2):
                        g = 2 * n + i
                        tmp = view(PP + (n % 2) * PW + i * 256, TT, SG_C)
                        src = JOB[(23 + n) % 2][:, i * 256:(i + 1) * 256].rearrange("p (t c) -> p t c", t=TT)
                        ins = dve.scalar_tensor_tensor(out=tmp, in0=src, scalar=bias_c[:, g:g + 1],
                                                       in1=u_g[:, :, g * SG_C:(g + 1) * SG_C], op0=ALU.add, op1=ALU.mult)
                        if i == 1:
                            ins.then_inc(job_ev.sem, 1)
                        else:
                            ins.then_inc(dve_link.next(), 1)
                    dve.wait_ge(job_ev.sem, job_ev.at(1, l, 23 + n + 1))
                    dve.wait_ge(dve_link.sem, dve_link.now(1, l))
                    for i in range(2):
                        g = 2 * n + i
                        y = Y[:, :, Y_B + g * SG_C:Y_B + (g + 1) * SG_C]
                        dve.tensor_tensor(y, y, view(PP + (n % 2) * PW + i * 256, TT, SG_C), ALU.mult)\
                           .then_inc(dve_link.next(), 1)

            def gla(l):
                dve.wait_ge(job_done.sem, job_done.at(1, l, 28))
                dve.tensor_copy(cgT[0:G_RANK, :], JOB[1][0:G_RANK, :]).then_inc(job_ev.sem, 1)
                for pr in range(2):
                    dve.wait_ge(job_done.sem, job_done.at(1, l, 28 + pr + 1))
                    dve.tensor_tensor(lg[:, pr * 512:(pr + 1) * 512].rearrange("p (t n) -> p t n", t=2),
                                      JOB[pr % 2][:, :].rearrange("p (t n) -> p t n", t=2),
                                      over(gate_b, 2), ALU.add).then_inc(job_ev.sem, 1)
                dve.wait_ge(job_ev.sem, job_ev.at(1, l, 30))
                dve.scalar_tensor_tensor(out=soft, in0=lg, scalar=-1.0, in1=lg, op0=ALU.mult, op1=ALU.min)\
                   .then_inc(soft_dve.sem, 1)
                dve.tensor_scalar(qk_g[:, :, 0, :], qk_g[:, :, 0, :], G_DK ** -0.5, None, ALU.mult)\
                   .then_inc(dve_link.next(), 1)
                dve.wait_ge(soft_act.sem, soft_act.at(1, l, 2))
                dve.scalar_tensor_tensor(out=la.rearrange("p t n -> p (t n)"), in0=lg, scalar=0.0, in1=soft,
                                         op0=ALU.min, op1=ALU.subtract).then_inc(prep.sem, 1)
                dve.wait_ge(dve_link.sem, dve_link.now(1, l))
                for n in range(2):
                    dve.wait_ge(ajob_ev.sem, ajob_ev.at(1, l, n + 1))
                    dve.tensor_tensor(qc_g[:, 2 * n:2 * n + 2, :], qk_g[:, 2 * n:2 * n + 2, 0, :], eg[:, n % 2, :, :],
                                      ALU.mult).then_inc(prep.sem, 1)
                for n in range(2):
                    dve.wait_ge(ajob_ev.sem, ajob_ev.at(1, l, 2 + n + 1))
                    dve.tensor_tensor(kt_g[:, 2 * n:2 * n + 2, :], qk_g[:, 2 * n:2 * n + 2, 1, :], eg[:, n % 2, :, :],
                                      ALU.mult).then_inc(ge_done.sem, 1)
                for pr in range(2):
                    take_job(1, l, 30 + pr, JOBS_QC[pr])
                dve.wait_ge(ajob_ev.sem, ajob_ev.at(1, l, 5))
                dve.memset(state[:, 0, :, :], 0.0).then_inc(dve_link.next(), 1)
                for c in range(7):
                    dve.wait_ge(job_done.sem, job_done.at(1, l, 32 + c + 1))
                    if c == 0:
                        dve.tensor_copy(state[:, 1, :, :], JOB[0][:, 0:256].rearrange("p (h v) -> p h v", h=2))\
                           .then_inc(job_ev.sem, 1)
                        continue
                    dve.wait_ge(job_ev.sem, job_ev.at(1, l, 32 + c))
                    dve.wait_ge(dve_link.sem, dve_link.now(1, l))
                    for hp in range(2):
                        ins = dve.scalar_tensor_tensor(out=state[:, c + 1, hp, :], in0=state[:, c, hp, :],
                                                       scalar=decay[:, hp, c:c + 1], in1=JOB[c % 2][:, tok(hp)],
                                                       op0=ALU.mult, op1=ALU.add)
                        if hp == 0:
                            ins.then_inc(dve_link.next(), 1)
                        else:
                            ins.then_inc(job_ev.sem, 1)

                def decayed(k):
                    pr, level = k // LEVELS, k % LEVELS
                    s = pr * (LEVELS + 1) + level
                    dve.wait_ge(ajob_ev.sem, ajob_ev.at(1, l, 5 + k + 1))
                    if s >= 2:
                        dve.wait_ge(gt_done.sem, gt_done.at(1, l, 2 * (s - 1)))
                    for i in range(2):
                        ins = dve.tensor_tensor(qke[:, s % 2, i, :, :], qk_g[:, 2 * pr + i, :, :],
                                                over(eg[:, k % 2, i, :], 2), ALU.mult)
                        if i == 0:
                            ins.then_inc(dve_link.next(), 1)
                        else:
                            ins.then_inc(ge_done.sem, 1)
                decayed(0)
                for g in range(4 * (LEVELS + 1)):
                    pr, level, i = g // (2 * LEVELS + 2), g // 2 % (LEVELS + 1), g % 2
                    t = 2 * pr + i
                    if i == 0 and level < LEVELS and pr * LEVELS + level + 1 < 2 * LEVELS:
                        decayed(pr * LEVELS + level + 1)
                    dve.wait_ge(gs_done.sem, gs_done.at(1, l, g + 1))
                    if level >= 1 and not (pr == 0 and level == 1):
                        dve.wait_ge(ga_done.sem, ga_done.at(1, l, pr * 12 + (level - 1) * 2 + i + 1 - 2))
                    for e in range(2):
                        dst = sacc[:, t, e, :] if level == 0 else stmp[:, g % 2, e, :]
                        ins = dve.tensor_tensor(dst.rearrange("p (h n) -> p h n", h=2),
                                                LEVEL[g % 2][e][:, 0:256].rearrange("p (h n) -> p h n", h=2),
                                                over(gmasks[:, level, :], 2), ALU.mult)
                        if e == 0:
                            ins.then_inc(dve_link.next(), 1)
                        else:
                            ins.then_inc(gm_done.sem, 1)
                for t in range(TT):
                    y = Y[:, t, Y_C:DM].rearrange("p (h v) -> p h v", h=G_H)
                    dve.tensor_tensor(y, y, over(gla_g, G_H), ALU.mult).then_inc(dve_link.next(), 1)
                for t in range(TT):
                    dve.wait_ge(go_done.sem, go_done.at(1, l, t + 1))
                    dve.tensor_copy(og[:, t, :, :], OUTB[t % 2][:, :].rearrange("p (h v) -> p h v", h=G_H))\
                       .then_inc(go_copied.sem, 1)
                    dve.wait_ge(go_copied.sem, go_copied.at(1, l, t + 1))
                    for e in range(2):
                        half = og[:, t, :, :].rearrange("p (h e) v -> p h e v", e=2)[:, :, e, :]
                        ins = dve.tensor_tensor(half, half, PAST[t % 2][e][:, 0:256].rearrange("p (h v) -> p h v", h=2), ALU.add)
                        if e == 0:
                            ins.then_inc(dve_link.next(), 1)
                        else:
                            ins.then_inc(go_free.sem, 1)
                    dve.wait_ge(go_free.sem, go_free.at(1, l, t + 1))
                    dve.wait_ge(dve_link.sem, dve_link.now(1, l))
                    dve.tensor_tensor(osq, og[:, t, :, :], og[:, t, :, :], ALU.mult).then_inc(dve_link.next(), 1)
                    dve.wait_ge(dve_link.sem, dve_link.now(1, l))
                    dve.tensor_reduce(ss[:, t * G_H:(t + 1) * G_H], osq, AX.X, ALU.add).then_inc(dve_link.next(), 1)
                rsqrt(1, l, TT * G_H, G_DV)
                for n in range(TT * G_H):
                    t, h = n // G_H, n % G_H
                    y = Y[:, t, Y_C + h * G_DV:Y_C + (h + 1) * G_DV]
                    ins = dve.scalar_tensor_tensor(out=y, in0=og[:, t, h, :], scalar=rs[:, n:n + 1], in1=y,
                                                   op0=ALU.mult, op1=ALU.mult)
                    if n < TT * G_H - 1:
                        ins.then_inc(dve_link.next(), 1)
                    else:
                        ins.then_inc(prep.sem, 1)

            with dve.Fori(0, 2) as l:
                dve_link.made = 0
                dve.wait_ge(job_done.sem, job_done.at(1, l, 1))
                dve.tensor_copy(cols[:, 0:88], JOB[0][:, 0:88]).then_inc(job_ev.sem, 1)
                dve.wait_ge(job_ev.sem, job_ev.at(1, l, 1))
                dve.tensor_tensor(cols[:, 32:48], cols[:, 32:48], cols[:, 64:80], ALU.add).then_inc(dve_link.next(), 1)
                dve.tensor_tensor(cols[:, 16:32], cols[:, 16:32], cols[:, 48:64], ALU.add).then_inc(dve_link.next(), 1)
                dve.tensor_scalar(bias_c[:, :], cols[:, 80:88], 0.5, None, ALU.mult).then_inc(dve_link.next(), 1)
                dve.wait_ge(dve_link.sem, dve_link.now(1, l))
                dve.scalar_tensor_tensor(out=cols[:, 0:16], in0=cols[:, 32:48], scalar=1.0, in1=cols[:, 0:16],
                                         op0=ALU.add, op1=ALU.mult).then_inc(dve_link.next(), 1)
                normalise(1, l)
                for j in range(LEAD):
                    split_lo(1, l, 0, j)
                panel(1, l, 0, take_copy(lambda t, p: q_s[:, t, 0:PW], blk=1), turned=turned_mod(l))
                panel(1, l, 1, take_copy(lambda t, p: q_s[:, t, PW:2 * PW], blk=1), between=angles(l))
                panel(1, l, 2, take_copy(lambda t, p: kv_s[:, t, :], blk=1))
                dve.wait_ge(x_saved.sem, x_saved.at(1, l, 16 * TT))
                panel(1, l, 3, take_gate(lambda p: 0, lambda p: 0, 1), between=lambda j: swa_rope(l) if j == 4 else None)
                with dve.Fori(4, 7) as p:
                    panel(1, l, p, take_gate(lambda p: (p - 3) * PW, lambda p: p - 3, 1))
                j0 = BR_S["j0"]
                dve.wait_ge(sink_in.sem, sink_in.at(1, l, 16))
                dve.tensor_scalar(sinks[:, :], sinks[:, :], -1.0, None, ALU.mult).then_inc(dve_link.next(), 1)
                dve.wait_ge(dve_link.sem, dve_link.now(1, l))
                for n, jb in enumerate(JOBS_SK + JOBS_SQ[0:1]):
                    take_job(1, l, j0 + n, jb)

                def next_queries2(h):
                    if h + 1 < S_H:
                        take_job(1, l, j0 + 5 + h, JOBS_SQ[h + 1])
                attention(1, l, BR_S, next_queries2)
                with dve.Fori(7, 9) as p:
                    panel(1, l, p, take_copy(lambda t, p: zone[:, bass.ds(ZQ + (p - 7) * 2048 + t * PW, PW)], blk=1))
                panel(1, l, 9, take_copy(lambda t, p: view(ZV, TT, PW)[:, t, :], blk=1), between=gelu_between(l))
                panel(1, l, 10, take_copy(lambda t, p: vv_g[:, t, :], blk=1), between=norm_between(l))
                for t in range(TT):
                    dve.wait_ge(lin_free[t].sem, lin_free[t].at(1, l, NIN2))
                dve.wait_ge(gla_in.sem, gla_in.at(1, l, 32))
                spatial(l)
                gla(l)

                def gains(j):
                    if j == ND - 1:
                        g = view(ZT, DM)
                        dve.wait_ge(gain_in.sem, gain_in.at(1, l, 48))
                        dve.tensor_tensor(g, g, view(ZV, DM), ALU.add).then_inc(dve_link.next(), 1)
                        dve.wait_ge(dve_link.sem, dve_link.now(1, l))
                        dve.tensor_tensor(g, g, view(ZK, DM), ALU.mult).then_inc(dve_link.next(), 1)
                        dve.wait_ge(dve_link.sem, dve_link.now(1, l))
                out_panel(1, l, NIN2, True, gains, turned=turned_lo(1, l, KC, 0.5))
                with dve.Fori(NIN2 + 1, NP2 - 1) as p:
                    out_panel(1, l, p, True)
                out_panel(1, l, NP2 - 1, False)
                residual(1, l)
                assert dve_link.made == DVE_LINKS2, dve_link.made

        @block.gpsimd
        def _(pool):
            pool.sem_inc(mod_used.sem, mod_used.credit)
            pool.memset(ident[:, :], 0.0).then_inc(boot_pool, 1)
            pool.memset(ones[:, :], 1.0).then_inc(boot_pool, 1)
            pool.memset(view(ZV, RPB_P + 1), 0.0).then_inc(boot_pool, 1)
            pool.wait_ge(boot_pool, 3)
            pool.affine_select(out=ident[:, :], in_=ident[:, :], compare_op=ALU.not_equal, fill=1.0,
                               base=0, pattern=[[-1, P]], channel_multiplier=1).then_inc(boot_pool, 1)
            pool.dma_start(rpb_pad[0:2 * C_H * RPB_R, 48:48 + RPB_C],
                           io["c_rpb"].rearrange("l h r c -> (l h r) c")).then_inc(boot_rpb, 16)
            pool.wait_ge(boot_dve, 2)

            def mod_panel(l, p):
                for k in range(KC):
                    m = p * KC + k
                    pool.wait_ge(mod_landed[k % 2].sem, mod_landed[k % 2].at(0, l, 16 * (p * (KC // 2) + k // 2 + 1)))
                    if k == 0:
                        pool.wait_ge(mod_sum.sem, mod_sum.at(0, l, p))
                    apart(pool)
                    pool.tensor_scalar(mprod[:, :], wmod[:, k % 2, :], csil[:, k:k + 1], 0.0, ALU.mult, ALU.add)\
                        .then_inc(mod_used.sem, 1)
                    pool.wait_ge(mod_used.sem, mod_used.at(0, l, m + 1))
                    apart(pool)
                    if k == 0:
                        pool.tensor_copy(macc[:, :], mprod[:, :]).then_inc(mod_added.sem, 1)
                    else:
                        pool.tensor_tensor(macc[:, :], macc[:, :], mprod[:, :], ALU.add).then_inc(mod_added.sem, 1)
                    pool.wait_ge(mod_added.sem, mod_added.at(0, l, m + 1))

            def bias_tiles(l):
                for h in range(C_H):
                    for rr in range(2):
                        src = bass.AP(tensor=rpb_dram.tensor,
                                      offset=((l * C_H + h) * RPB_R + 1 - rr) * RPB_P + GRID_W - 1,
                                      ap=[[RPB_P, GM], [-1, GRID_W], [1, GRID_W]])
                        pool.dma_start(g_dram[l, rr * GRID_W:(rr + 1) * GRID_W, h].rearrange("c m k -> m c k"), src)\
                            .then_inc(g_built.sem, 16)

            for l in range(2):
                pool.wait_ge(prep.sem, prep.at(0, l, 0))
                apart(pool)
                mod_panel(l, 0)
                if l == 0:
                    pool.wait_ge(boot_rpb, 16)
                    pool.dma_start(rpb_dram, rpb_pad[0:2 * C_H * RPB_R, :]).then_inc(boot_rpb, 16)
                    pool.wait_ge(boot_rpb, 32)
                bias_tiles(l)
                with pool.Fori(1, NIN) as p:
                    mod_panel(l, p)
            with pool.Fori(0, 2) as l:
                for g in range(4 * (LEVELS + 1)):
                    pr, level, i = g // (2 * LEVELS + 2), g // 2 % (LEVELS + 1), g % 2
                    if level == 0:
                        continue
                    n = pr * 12 + (level - 1) * 2 + i
                    pool.wait_ge(gm_done.sem, gm_done.at(1, l, g + 1))
                    if n >= 2:
                        pool.wait_ge(ga_done.sem, ga_done.at(1, l, n - 1))
                    acc = sacc[:, 2 * pr + i, :, :]
                    pool.tensor_tensor(acc, acc, stmp[:, g % 2, :, :], ALU.add).then_inc(ga_done.sem, 1)


INPUTS = ["x", "norm_pre", "norm_post", "w_in", "a_q_norm", "a_k_norm", "b_q_norm", "b_kv_norm", "b_w_uq", "b_w_ukv",
          "c_rpb", "w_out", "c_2", "positions_2", "w_mod_2", "b_mod_2", "g_pre_2", "g_post_2", "w_in_2", "w_out_2",
          "swa_sinks_2", "sg_w_2", "sg_b_2", "sg_ln_g_2", "sg_ln_b_2", "gla_w_gate_up_2", "gla_b_gate_2",
          "gla_norm_g_2"]


def kernel(**inputs):
    import concourse.bacc as bacc
    from concourse.bass_utils import run_bass_kernel_spmd

    nc = bacc.Bacc("TRN2", target_bir_lowering=False, num_devices=1)
    rope_a, rope_b, near = tables()
    arrays = {name: np.ascontiguousarray(inputs[name]) for name in INPUTS}
    band, freq, sums, masks = tables_2()
    arrays |= {"rope_a": rope_a, "rope_b": rope_b, "near_mask": near, "band": band, "freq": freq,
               "gla_sums": sums, "gla_masks": masks}
    io = {name: nc.dram_tensor(f"in_{name}", a.shape, mybir.dt.from_np(a.dtype), kind="ExternalInput").ap()
          for name, a in arrays.items()}
    io["out"] = nc.dram_tensor("out_0", (1, SEQ, DM), F32, kind="ExternalOutput").ap()
    build(nc, io)
    r = run_bass_kernel_spmd(nc, [{f"in_{name}": a for name, a in arrays.items()}], core_ids=[0])
    return r.results[0]["out_0"]
```
